# Optimizing a Trainium2 kernel written in Bass

```python
import math
import jax, jax.numpy as jnp
from jax import lax
import numpy as np

D_MODEL = 1024
BATCH = 1
SEQ = 512
DEPTH = 2

GRID_W = 64
D_MIX = D_MODEL
ATTN_WIDTH = D_MIX // 2
SSD_WIDTH = D_MIX - ATTN_WIDTH
HEAD_DIM = 64
N_Q_HEADS = ATTN_WIDTH // HEAD_DIM
N_KV_HEADS = 2
KV_WIDTH = N_KV_HEADS * HEAD_DIM
Q_BLOCK = 128
ROPE_THETA = 10000.0
ROPE_AXIS_DIM = HEAD_DIM // 2
SSD_HEAD_DIM = 64
SSD_HEADS = SSD_WIDTH // SSD_HEAD_DIM
SSD_GROUPS = 2
D_STATE = 128
D_CONV = 5
CONV_PAD = D_CONV // 2
CHUNK = 128
CONV_CH = SSD_WIDTH + 2 * SSD_GROUPS * D_STATE
DT_MIN = 0.001
DT_MAX = 0.1
D_IN_PROJ = ATTN_WIDTH + 2 * KV_WIDTH + SSD_WIDTH + CONV_CH + 2 * SSD_HEADS
D_FF = -(-8 * D_MODEL // (3 * 256)) * 256
EPS = 1e-6


def rms_norm(x, w):
    xf = x.astype(jnp.float32)
    y = xf * lax.rsqrt(jnp.mean(xf * xf, axis=-1, keepdims=True) + EPS)
    return (y * w.astype(jnp.float32)).astype(x.dtype)

def _rot_half(x, cos, sin):
    x1, x2 = jnp.split(x, 2, axis=-1)
    return jnp.concatenate([x1 * cos - x2 * sin, x2 * cos + x1 * sin], axis=-1)

def axial_rope(x, cos_r, sin_r, cos_c, sin_c):
    xr, xc = jnp.split(x, 2, axis=-1)
    return jnp.concatenate([_rot_half(xr, cos_r, sin_r), _rot_half(xc, cos_c, sin_c)], axis=-1)

def axial_rope_tables(seq_len):
    rows = seq_len // GRID_W
    row_idx, col_idx = jnp.meshgrid(jnp.arange(rows), jnp.arange(GRID_W), indexing="ij")
    row_idx = row_idx.reshape(-1).astype(jnp.float32)
    col_idx = col_idx.reshape(-1).astype(jnp.float32)
    half = ROPE_AXIS_DIM // 2
    inv_freq = ROPE_THETA ** (-(2.0 * jnp.arange(half, dtype=jnp.float32)) / ROPE_AXIS_DIM)
    ang_r = row_idx[:, None] * inv_freq[None, :]
    ang_c = col_idx[:, None] * inv_freq[None, :]
    return (jnp.cos(ang_r)[:, None], jnp.sin(ang_r)[:, None],
            jnp.cos(ang_c)[:, None], jnp.sin(ang_c)[:, None])

def blocked_gqa(q, k, v):
    b, l, hq, d = q.shape
    r = hq // N_KV_HEADS
    nb = l // Q_BLOCK
    qb = (q * (1.0 / math.sqrt(d))).reshape(b, nb, Q_BLOCK, N_KV_HEADS, r, d)
    qb = jnp.moveaxis(qb, 1, 0)

    def one_block(qi):
        s = jnp.einsum("bqgrd,bkgd->bgrqk", qi, k)
        p = jax.nn.softmax(s, axis=-1)
        return jnp.einsum("bgrqk,bkgd->bqgrd", p, v)

    out = lax.map(one_block, qb)
    return jnp.moveaxis(out, 0, 1).reshape(b, l, hq * d)

def depthwise_conv_centred(x, w, bias):
    y = lax.conv_general_dilated(
        x, w[:, None, :].astype(x.dtype), window_strides=(1,), padding=[(CONV_PAD, CONV_PAD)],
        dimension_numbers=("NWC", "WIO", "NWC"), feature_group_count=x.shape[-1])
    return y + bias.astype(x.dtype)

def ssd_chunked(x, dt, a, bm, cm):
    b, l, h, p = x.shape
    g, n = bm.shape[2], bm.shape[3]
    r = h // g
    nc = l // CHUNK
    xc = (x * dt[..., None]).reshape(b, nc, CHUNK, g, r, p)
    ac = (dt * a).reshape(b, nc, CHUNK, g, r)
    bc = bm.reshape(b, nc, CHUNK, g, n)
    cc = cm.reshape(b, nc, CHUNK, g, n)
    a_cs = jnp.cumsum(ac, axis=2)
    diff = a_cs[:, :, :, None] - a_cs[:, :, None, :]
    mask = jnp.tril(jnp.ones((CHUNK, CHUNK), dtype=bool))[:, :, None, None]
    decay = jnp.exp(jnp.where(mask, diff, -jnp.inf))
    scores = jnp.einsum("bclgn,bcsgn->bclsg", cc, bc)
    y_diag = jnp.einsum("bclsgr,bcsgrp->bclgrp", scores[..., None] * decay, xc)
    decay_to_end = jnp.exp(a_cs[:, :, -1:] - a_cs)
    states = jnp.einsum("bclgn,bclgrp->bcgrpn", bc, xc * decay_to_end[..., None])
    chunk_decay = jnp.exp(a_cs[:, :, -1])

    def step(hs, inp):
        dec, st = inp
        return hs * dec[..., None, None] + st, hs

    h0 = jnp.zeros((b, g, r, p, n), dtype=states.dtype)
    _, states_in = lax.scan(step, h0, (jnp.moveaxis(chunk_decay, 1, 0), jnp.moveaxis(states, 1, 0)))
    states_in = jnp.moveaxis(states_in, 0, 1)
    y_off = jnp.einsum("bclgn,bcgrpn->bclgrp", cc, states_in) * jnp.exp(a_cs)[..., None]
    return (y_diag + y_off).reshape(b, l, h, p)

def ssd_mixer(z, xbc_raw, dt_raw, conv_w, conv_b, dt_bias, a_log, d_skip, norm_w):
    b, l, _ = z.shape
    xbc = jax.nn.silu(depthwise_conv_centred(xbc_raw, conv_w, conv_b)).astype(jnp.float32)
    xs, bm, cm = jnp.split(xbc, [SSD_WIDTH, SSD_WIDTH + SSD_GROUPS * D_STATE], axis=-1)
    xs = xs.reshape(b, l, SSD_HEADS, SSD_HEAD_DIM)
    bm = bm.reshape(b, l, SSD_GROUPS, D_STATE)
    cm = cm.reshape(b, l, SSD_GROUPS, D_STATE)
    dt = jax.nn.softplus(dt_raw.astype(jnp.float32).reshape(b, l, 2, SSD_HEADS)
                         + dt_bias.astype(jnp.float32))
    a = -jnp.exp(a_log.astype(jnp.float32))
    y_fwd = ssd_chunked(xs, dt[:, :, 0], a[0], bm, cm)
    flip = lambda t: jnp.flip(t, axis=1)
    y_bwd = flip(ssd_chunked(flip(xs), flip(dt[:, :, 1]), a[1], flip(bm), flip(cm)))
    y = y_fwd + y_bwd + xs * d_skip.astype(jnp.float32)[:, None]
    y = y.reshape(b, l, SSD_WIDTH) * jax.nn.silu(z.astype(jnp.float32))
    yg = y.reshape(b, l, SSD_GROUPS, SSD_WIDTH // SSD_GROUPS)
    yg = yg * lax.rsqrt(jnp.mean(yg * yg, axis=-1, keepdims=True) + EPS)
    return (yg.reshape(b, l, SSD_WIDTH) * norm_w.astype(jnp.float32)).astype(z.dtype)

def first_inputs(seed: int = 0) -> dict:
    key = jax.random.key(seed)
    ks = jax.random.split(key, 20)
    f32 = jnp.float32
    nrm = lambda k, shape, s: jax.random.normal(k, shape, f32) * s
    dt0 = jnp.exp(jax.random.uniform(ks[7], (DEPTH, 2, SSD_HEADS), f32,
                                     math.log(DT_MIN), math.log(DT_MAX)))
    return {
        "x": jax.random.normal(ks[0], (BATCH, SEQ, D_MODEL), f32),
        "norm_mix_w": 1.0 + nrm(ks[1], (DEPTH, D_MODEL), 0.02),
        "w_in": nrm(ks[2], (DEPTH, D_MODEL, D_IN_PROJ), D_MODEL ** -0.5),
        "q_norm_w": 1.0 + nrm(ks[3], (DEPTH, HEAD_DIM), 0.02),
        "k_norm_w": 1.0 + nrm(ks[4], (DEPTH, HEAD_DIM), 0.02),
        "conv_w": nrm(ks[5], (DEPTH, D_CONV, CONV_CH), D_CONV ** -0.5),
        "conv_b": nrm(ks[6], (DEPTH, CONV_CH), 0.01),
        "dt_bias": dt0 + jnp.log(-jnp.expm1(-dt0)),
        "a_log": jnp.log(jax.random.uniform(ks[8], (DEPTH, 2, SSD_HEADS), f32, 1.0, 16.0)),
        "d_skip": 1.0 + nrm(ks[9], (DEPTH, SSD_HEADS), 0.1),
        "ssd_norm_w": 1.0 + nrm(ks[10], (DEPTH, SSD_WIDTH), 0.02),
        "w_out": nrm(ks[11], (DEPTH, D_MIX, D_MODEL), D_MIX ** -0.5),
        "norm_ffn_w": 1.0 + nrm(ks[12], (DEPTH, D_MODEL), 0.02),
        "w_gate": nrm(ks[13], (DEPTH, D_MODEL, D_FF), D_MODEL ** -0.5),
        "w_up": nrm(ks[14], (DEPTH, D_MODEL, D_FF), D_MODEL ** -0.5),
        "w_down": nrm(ks[15], (DEPTH, D_FF, D_MODEL), D_FF ** -0.5),
        "final_norm_w": 1.0 + nrm(ks[16], (D_MODEL,), 0.02),
    }

def first_block(x, norm_mix_w, w_in, q_norm_w, k_norm_w, conv_w, conv_b, dt_bias, a_log, d_skip,
              ssd_norm_w, w_out, norm_ffn_w, w_gate, w_up, w_down, final_norm_w):
    b, l, _ = x.shape
    cos_r, sin_r, cos_c, sin_c = axial_rope_tables(l)
    split_at = np.cumsum([ATTN_WIDTH, KV_WIDTH, KV_WIDTH, SSD_WIDTH, CONV_CH]).tolist()
    for i in range(DEPTH):
        h = rms_norm(x, norm_mix_w[i])
        proj = jnp.einsum("bld,de->ble", h, w_in[i])
        q, k, v, z, xbc_raw, dt_raw = jnp.split(proj, split_at, axis=-1)
        q = rms_norm(q.reshape(b, l, N_Q_HEADS, HEAD_DIM), q_norm_w[i]).astype(jnp.float32)
        k = rms_norm(k.reshape(b, l, N_KV_HEADS, HEAD_DIM), k_norm_w[i]).astype(jnp.float32)
        v = v.reshape(b, l, N_KV_HEADS, HEAD_DIM).astype(jnp.float32)
        q = axial_rope(q, cos_r, sin_r, cos_c, sin_c)
        k = axial_rope(k, cos_r, sin_r, cos_c, sin_c)
        attn_out = blocked_gqa(q, k, v).astype(x.dtype)
        ssd_out = ssd_mixer(z, xbc_raw, dt_raw, conv_w[i], conv_b[i], dt_bias[i], a_log[i],
                            d_skip[i], ssd_norm_w[i])
        mixed = jnp.concatenate([attn_out, ssd_out], axis=-1)
        x = x + jnp.einsum("ble,ed->bld", mixed, w_out[i])
        h = rms_norm(x, norm_ffn_w[i])
        g = jnp.einsum("bld,df->blf", h, w_gate[i])
        u = jnp.einsum("bld,df->blf", h, w_up[i])
        x = x + jnp.einsum("blf,fd->bld", jax.nn.silu(g) * u, w_down[i])
    return rms_norm(x, final_norm_w)


DEPTH_2 = 1

HG_HEADS = 8
HG_HEAD_DIM = 128
HG_WIDTH = HG_HEADS * HG_HEAD_DIM
HG_CHUNK = 64
LRU_WIDTH = D_MODEL
LRU_HEADS = 8
LRU_HEAD_DIM = LRU_WIDTH // LRU_HEADS
LRU_CONV = 4
LRU_C = 8.0
CONV_WIDTH = D_MODEL
CONV_KERNEL = 31
N_BRANCH = 3
D_FF_2 = 2816
MIX_COLS = (4 * HG_WIDTH) + (2 * LRU_WIDTH) + (2 * CONV_WIDTH) + (N_BRANCH * D_MODEL)


def rmsnorm(x, g, eps=1e-6):
    xf = x.astype(jnp.float32)
    y = xf * lax.rsqrt(jnp.mean(xf * xf, axis=-1, keepdims=True) + eps)
    return (y * g.astype(jnp.float32)).astype(x.dtype)

def layernorm(x, g, b, eps=1e-5):
    xf = x.astype(jnp.float32)
    mu = jnp.mean(xf, axis=-1, keepdims=True)
    xc = xf - mu
    y = xc * lax.rsqrt(jnp.mean(xc * xc, axis=-1, keepdims=True) + eps)
    return (y * g.astype(jnp.float32) + b.astype(jnp.float32)).astype(x.dtype)

def swiglu_ffn(x, w_in, w_out):
    g, u = jnp.split(x @ w_in, 2, axis=-1)
    return (jax.nn.silu(g) * u) @ w_out

def causal_dwconv(x, w, b):
    k = w.shape[0]
    xp = jnp.pad(x, ((0, 0), (k - 1, 0), (0, 0)))
    y = lax.conv_general_dilated(
        xp, w[:, None, :].astype(x.dtype), window_strides=(1,), padding='VALID',
        dimension_numbers=('NWC', 'WIO', 'NWC'), feature_group_count=x.shape[-1])
    return y + b

def hgrn2_chunked(q, k, v, log_f):
    b_, s_, h_, dk = q.shape
    dv = v.shape[-1]
    n = s_ // HG_CHUNK

    def to_chunks(t):
        return t.reshape(b_, n, HG_CHUNK, h_, t.shape[-1]).transpose(1, 0, 3, 2, 4)

    qc, kc, vc, gc = to_chunks(q), to_chunks(k), to_chunks(v), to_chunks(log_f)
    causal = jnp.tril(jnp.ones((HG_CHUNK, HG_CHUNK), dtype=bool))[:, :, None]

    def step(state, inp):
        qb, kb, vb, gb = inp
        bcum = jnp.cumsum(gb, axis=2)
        diff = bcum[:, :, :, None, :] - bcum[:, :, None, :, :]
        decay = jnp.exp(jnp.where(causal, diff, -jnp.inf))
        scores = jnp.einsum('bhtk,bhsk,bhtsk->bhts', qb, kb, decay)
        o = (jnp.einsum('bhts,bhsv->bhtv', scores, vb)
             + jnp.einsum('bhtk,bhkv->bhtv', qb * jnp.exp(bcum), state))
        b_last = bcum[:, :, -1:, :]
        state = (jnp.exp(b_last[:, :, 0, :])[..., None] * state
                 + jnp.einsum('bhsk,bhsv->bhkv', kb * jnp.exp(b_last - bcum), vb))
        return state, o

    s0 = jnp.zeros((b_, h_, dk, dv), jnp.float32)
    _, o = lax.scan(step, s0, (qc, kc, vc, gc))
    return o.transpose(1, 0, 3, 2, 4).reshape(b_, s_, h_, dv)

def linear_scan(a, u):
    def combine(c1, c2):
        a1, b1 = c1
        a2, b2 = c2
        return a1 * a2, a2 * b1 + b2
    _, h = lax.associative_scan(combine, (a, u), axis=1)
    return h

def hybrid_mixer(u, lb, w_in, b_in, hg_norm, lru_conv_w, lru_conv_b, lru_gate_w, lru_gate_b,
                 lru_lambda, cv_dw_w, cv_dw_b, cv_ln_g, cv_ln_b, w_branch, w_out):
    bsz, s_, _ = u.shape
    f32 = jnp.float32
    proj = u @ w_in + b_in
    sizes = [HG_WIDTH] * 4 + [LRU_WIDTH] * 2 + [CONV_WIDTH] * 2 + [D_MODEL] * N_BRANCH
    cuts = [int(c) for c in np.cumsum(sizes)[:-1]]
    hq, hf, hi, hg, lx, lg, ca, cb, g_a, g_b, g_c = jnp.split(proj, cuts, axis=-1)

    hshape = (bsz, s_, HG_HEADS, HG_HEAD_DIM)
    q = jax.nn.silu(hq.astype(f32)).reshape(hshape)
    z = hf.astype(f32).reshape(hshape)
    lb_h = lb.astype(f32).reshape(HG_HEADS, HG_HEAD_DIM)
    f = lb_h + (1.0 - lb_h) * jax.nn.sigmoid(z)
    k = (1.0 - lb_h) * jax.nn.sigmoid(-z)
    v = hi.astype(f32).reshape(hshape)
    o_hg = hgrn2_chunked(q, k, v, jnp.log(f))
    y_hg = rmsnorm(o_hg, hg_norm).reshape(bsz, s_, HG_WIDTH).astype(u.dtype) * jax.nn.silu(hg)

    xb = causal_dwconv(lx, lru_conv_w, lru_conv_b)
    xh = xb.reshape(bsz, s_, LRU_HEADS, LRU_HEAD_DIM)
    gates = jnp.einsum('bshi,ghij->gbshj', xh, lru_gate_w).reshape(2, bsz, s_, LRU_WIDTH)
    gates = gates.astype(f32) + lru_gate_b.astype(f32)[:, None, None, :]
    r_t = jax.nn.sigmoid(gates[0])
    i_t = jax.nn.sigmoid(gates[1])
    log_a = -LRU_C * r_t * jax.nn.softplus(-lru_lambda.astype(f32))
    a_t = jnp.exp(log_a)
    mult = jnp.sqrt(-jnp.expm1(2.0 * log_a))
    h = linear_scan(a_t, mult * (i_t * xb.astype(f32)))
    y_lru = h.astype(u.dtype) * jax.nn.gelu(lg)

    cu = ca * jax.nn.sigmoid(cb)
    cu = causal_dwconv(cu, cv_dw_w, cv_dw_b)
    y_cv = jax.nn.silu(layernorm(cu, cv_ln_g, cv_ln_b))

    merged = (jax.nn.sigmoid(g_a) * (y_hg @ w_branch[0])
              + jax.nn.sigmoid(g_b) * (y_lru @ w_branch[1])
              + jax.nn.sigmoid(g_c) * (y_cv @ w_branch[2]))
    return merged @ w_out

def second_inputs(seed: int = 0) -> dict:
    key = jax.random.key(seed)
    ks = jax.random.split(key, 24)
    L, D = DEPTH_2, D_MODEL

    def nrm(k, shape, fan_in):
        return jax.random.normal(k, shape, jnp.float32) * (fan_in ** -0.5)

    def gain(k, shape):
        return 1.0 + 0.01 * jax.random.normal(k, shape, jnp.float32)

    a_c = jax.random.uniform(ks[14], (L, LRU_WIDTH), jnp.float32, minval=0.9, maxval=0.999)
    sig = a_c ** (1.0 / LRU_C)
    lru_lambda = jnp.log(sig) - jnp.log1p(-sig)

    return {
        "x": jax.random.normal(ks[0], (BATCH, SEQ, D), jnp.float32),
        "norm_ffn1": gain(ks[1], (L, D)),
        "ffn1_w_in": nrm(ks[2], (L, D, 2 * D_FF_2), D),
        "ffn1_w_out": nrm(ks[3], (L, D_FF_2, D), D_FF_2),
        "norm_mix": gain(ks[4], (L, D)),
        "w_in_mix": nrm(ks[5], (L, D, MIX_COLS), D),
        "b_in_mix": 0.01 * jax.random.normal(ks[6], (L, MIX_COLS), jnp.float32),
        "hgrn_lb_logits": 0.5 * jax.random.normal(ks[7], (L, HG_WIDTH), jnp.float32),
        "hg_norm": gain(ks[8], (L, HG_HEAD_DIM)),
        "lru_conv_w": nrm(ks[9], (L, LRU_CONV, LRU_WIDTH), LRU_CONV),
        "lru_conv_b": 0.01 * jax.random.normal(ks[10], (L, LRU_WIDTH), jnp.float32),
        "lru_gate_w": nrm(ks[11], (L, 2, LRU_HEADS, LRU_HEAD_DIM, LRU_HEAD_DIM), LRU_HEAD_DIM),
        "lru_gate_b": 0.01 * jax.random.normal(ks[12], (L, 2, LRU_WIDTH), jnp.float32),
        "lru_lambda": lru_lambda,
        "cv_dw_w": nrm(ks[15], (L, CONV_KERNEL, CONV_WIDTH), CONV_KERNEL),
        "cv_dw_b": 0.01 * jax.random.normal(ks[16], (L, CONV_WIDTH), jnp.float32),
        "cv_ln_g": gain(ks[17], (L, CONV_WIDTH)),
        "cv_ln_b": 0.01 * jax.random.normal(ks[18], (L, CONV_WIDTH), jnp.float32),
        "w_branch": nrm(ks[19], (L, N_BRANCH, D, D), D),
        "w_out_mix": nrm(ks[20], (L, D, D), D),
        "norm_ffn2": gain(ks[21], (L, D)),
        "ffn2_w_in": nrm(ks[22], (L, D, 2 * D_FF_2), D),
        "ffn2_w_out": nrm(ks[23], (L, D_FF_2, D), D_FF_2),
        "norm_final": gain(ks[13], (D,)),
    }

def second_block(x, norm_ffn1, ffn1_w_in, ffn1_w_out, norm_mix, w_in_mix, b_in_mix, hgrn_lb_logits,
              hg_norm, lru_conv_w, lru_conv_b, lru_gate_w, lru_gate_b, lru_lambda, cv_dw_w, cv_dw_b,
              cv_ln_g, cv_ln_b, w_branch, w_out_mix, norm_ffn2, ffn2_w_in, ffn2_w_out, norm_final):
    lb_all = jax.nn.softmax(hgrn_lb_logits.astype(jnp.float32), axis=0)
    lb_all = jnp.cumsum(lb_all, axis=0) - lb_all[:1]
    for l in range(DEPTH_2):
        x = x + 0.5 * swiglu_ffn(rmsnorm(x, norm_ffn1[l]), ffn1_w_in[l], ffn1_w_out[l])
        x = x + hybrid_mixer(rmsnorm(x, norm_mix[l]), lb_all[l], w_in_mix[l], b_in_mix[l],
                             hg_norm[l], lru_conv_w[l], lru_conv_b[l], lru_gate_w[l], lru_gate_b[l],
                             lru_lambda[l], cv_dw_w[l], cv_dw_b[l], cv_ln_g[l], cv_ln_b[l],
                             w_branch[l], w_out_mix[l])
        x = x + 0.5 * swiglu_ffn(rmsnorm(x, norm_ffn2[l]), ffn2_w_in[l], ffn2_w_out[l])
    return rmsnorm(x, norm_final)


_first_inputs = second_inputs


def second_inputs(seed=0):
    import zlib

    import numpy as np

    out = dict(_first_inputs(seed))
    spreads = {}
    factors = {'norm_ffn1': 8.0,
     'norm_mix': 8.0,
     'b_in_mix': 3.467,
     'hg_norm': 8.0,
     'lru_conv_b': 4.072,
     'lru_gate_b': 8.0,
     'cv_dw_b': 8.0,
     'cv_ln_g': 8.0,
     'cv_ln_b': 8.0,
     'norm_ffn2': 8.0,
     'norm_final': 5.495}
    for name, (base, spread) in spreads.items():
        noise = np.random.default_rng([zlib.crc32(name.encode()), seed]).standard_normal(out[name].shape)
        drawn = base * np.exp(spread * noise) if base else spread * noise
        out[name] = __import__('jax').numpy.asarray(drawn.astype(out[name].dtype))
    for name, factor in factors.items():
        out[name] = (out[name] * factor).astype(out[name].dtype)
    return out


_narrow_inputs = second_inputs


def second_inputs(seed=0):

    out = dict(_narrow_inputs(seed))
    wider = {'norm_mix': 3.54,
     'b_in_mix': 4.27,
     'hg_norm': 8.07,
     'lru_conv_b': 4.54,
     'lru_gate_b': 9.31,
     'cv_dw_b': 12.0,
     'cv_ln_g': 12.0,
     'cv_ln_b': 12.0,
     'norm_ffn2': 9.62,
     'norm_final': 6.17}
    for name, times in wider.items():
        mean = out[name].mean()
        out[name] = (mean + times * (out[name] - mean)).astype(out[name].dtype)
    return out


def setup_inputs(seed=0):
    out = dict(first_inputs(seed))
    for name, value in second_inputs(seed + 1).items():
        if name != "x":
            out[name + "_2"] = value
    return out


def reference(
    x, norm_mix_w, w_in, q_norm_w, k_norm_w, conv_w, conv_b, dt_bias, a_log, d_skip, ssd_norm_w,
    w_out, norm_ffn_w, w_gate, w_up, w_down, final_norm_w, norm_ffn1_2, ffn1_w_in_2,
    ffn1_w_out_2, norm_mix_2, w_in_mix_2, b_in_mix_2, hgrn_lb_logits_2, hg_norm_2, lru_conv_w_2,
    lru_conv_b_2, lru_gate_w_2, lru_gate_b_2, lru_lambda_2, cv_dw_w_2, cv_dw_b_2, cv_ln_g_2,
    cv_ln_b_2, w_branch_2, w_out_mix_2, norm_ffn2_2, ffn2_w_in_2, ffn2_w_out_2, norm_final_2,
):
    x = first_block(
        x, norm_mix_w, w_in, q_norm_w, k_norm_w, conv_w, conv_b, dt_bias, a_log, d_skip,
        ssd_norm_w, w_out, norm_ffn_w, w_gate, w_up, w_down, final_norm_w,
    )
    return second_block(
        x, norm_ffn1_2, ffn1_w_in_2, ffn1_w_out_2, norm_mix_2, w_in_mix_2, b_in_mix_2,
        hgrn_lb_logits_2, hg_norm_2, lru_conv_w_2, lru_conv_b_2, lru_gate_w_2, lru_gate_b_2,
        lru_lambda_2, cv_dw_w_2, cv_dw_b_2, cv_ln_g_2, cv_ln_b_2, w_branch_2, w_out_mix_2,
        norm_ffn2_2, ffn2_w_in_2, ffn2_w_out_2, norm_final_2,
    )


_drawn_inputs = setup_inputs


def setup_inputs(seed=0):
    import zlib

    import numpy as np

    out = dict(_drawn_inputs(seed))
    spreads = {}
    factors = {'q_norm_w': 8.0,
     'k_norm_w': 8.0,
     'cv_dw_b_2': 3.15,
     'cv_ln_g_2': 5.155,
     'cv_ln_b_2': 5.108}
    for name, (base, spread) in spreads.items():
        noise = np.random.default_rng([zlib.crc32(name.encode()), seed]).standard_normal(out[name].shape)
        drawn = base * np.exp(spread * noise) if base else spread * noise
        out[name] = __import__('jax').numpy.asarray(drawn.astype(out[name].dtype))
    for name, factor in factors.items():
        out[name] = (out[name] * factor).astype(out[name].dtype)
    return out
```

```python
import numpy as np
import concourse.bass as bass
from concourse import mybir

F32 = mybir.dt.float32
F32R = mybir.dt.float32r
U8 = mybir.dt.uint8
ALU = mybir.AluOpType
ACT = mybir.ActivationFunctionType
AX = mybir.AxisListType.X

P = 128
T = 512
D = 1024
DT = 8
FT = 22
NH = 8
CH = 4
RAW = 4
SPL = 4
LOOK = 3
SLOT = 1024
LEVELS = (64, 32, 16, 8, 4, 2, 1)
TAPS = 31
TINY = 2.0 ** -63


def plan():
    s = []

    def fm(name, i, c0, rows=((0, DT),)):
        for r0, nr in rows:
            s.append((name, i, r0, nr, c0, P))

    def tm(name, i, c0):
        for r0 in range(0, DT, 2):
            s.append((name, i, r0, 2, c0, 512))

    down = ((0, 8), (8, 8), (16, 6))
    for l in range(2):
        for j in range(5):
            fm("w_in", l, j * P)
        s.append(("w_in", l, 0, DT, 640, P))
        s.append(("w_in", l, 0, DT, 2304, 16))
        tm("w_in", l, 768)
        for j in range(8):
            fm("w_in", l, 1280 + j * P)
        for j in range(DT):
            fm("w_out", l, j * P)
        for j in range(FT):
            fm("w_gate", l, j * P)
            fm("w_up", l, j * P)
        for j in range(DT):
            fm("w_down", l, j * P, down)

    def ffn(a, b):
        for j in range(FT):
            fm(a, 0, j * P)
            fm(a, 0, 2816 + j * P)
        for j in range(DT):
            fm(b, 0, j * P, down)

    ffn("ffn1_w_in_2", "ffn1_w_out_2")
    m = "w_in_mix_2"
    tm(m, 0, 2048)
    tm(m, 0, 2560)
    for j in range(8):
        fm(m, 0, 1024 + j * P)
        fm(m, 0, j * P)
        fm(m, 0, 3072 + j * P)
    for j in range(8):
        fm(m, 0, 6144 + j * P)
        fm(m, 0, 7168 + j * P)

    def branch(x):
        for j in range(8):
            fm(m, 0, 8192 + x * D + j * P)
            fm("w_branch_2", x, j * P)

    branch(0)
    for j in range(8):
        fm(m, 0, 4096 + j * P)
        fm(m, 0, 5120 + j * P)
    branch(1)
    for j in range(8):
        fm(m, 0, 8192 + 2 * D + j * P)
    for j in range(8):
        fm("w_branch_2", 2, j * P)
    for j in range(8):
        fm("w_out_mix_2", 0, j * P)
    ffn("ffn2_w_in_2", "ffn2_w_out_2")
    return s


def columns():
    at, n = {}, 0
    for l in range(2):
        for name, k in (("nmix", 8), ("qn", 1), ("kn", 1), ("cw", 40), ("cb", 8), ("sn", 4), ("nffn", 8),
                        ("dtb", 16), ("alog", 16), ("dsk", 8)):
            at[name, l] = n
            n += k
    for name, k in (("fnorm", 8), ("nf1", 8), ("nmix2", 8), ("bin", 88), ("lb", 8), ("hgn", 1), ("lcw", 32),
                    ("lcb", 8), ("lgb", 16), ("lam", 8), ("cvw", 8 * TAPS), ("cvb", 8), ("cvg", 8), ("cvn", 8),
                    ("nf2", 8), ("nfin", 8), ("eps", 1), ("eps5", 1), ("one", 1)):
        at[name] = n
        n += k
    return at, n


class Record:

    def copy(self, *a, **k):
        return lambda e: e.copy(*a, **k)

    def activation(self, *a, **k):
        return lambda e: e.activation(*a, **k)

    def tensor_tensor(self, *a, **k):
        return lambda e: e.tensor_tensor(*a, **k)

    def tensor_scalar(self, *a, **k):
        return lambda e: e.tensor_scalar(*a, **k)

    def scalar_tensor_tensor(self, *a, **k):
        return lambda e: e.scalar_tensor_tensor(*a, **k)

    def tensor_tensor_scan(self, *a, **k):
        return lambda e: e.tensor_tensor_scan(*a, **k)

    def tensor_reduce(self, *a, **k):
        return lambda e: e.tensor_reduce(*a, **k)

    def tensor_copy(self, *a, **k):
        return lambda e: e.tensor_copy(*a, **k)

    def reciprocal(self, *a, **k):
        return lambda e: e.reciprocal(*a, **k)

    def copy_predicated(self, *a, **k):
        return lambda e: e.copy_predicated(*a, **k)

    def memset(self, *a, **k):
        return lambda e: e.memset(*a, **k)

    def matmul(self, *a, **k):
        return lambda e: e.matmul(*a, **k)

    def transpose(self, *a, **k):
        return lambda e: e.transpose(*a, **k)


class Engine:

    def __init__(self, sem):
        self.sem, self.n, self.queue, self.seen = sem, 0, [], {}

    def wait(self, *tokens):
        for sem, value in tokens:
            if self.seen.get(id(sem), 0) < value:
                self.seen[id(sem)] = value
                self.queue.append(lambda e, s=sem, v=value: e.wait_ge(s, v))

    def op(self, make):
        self.n += 1
        instruction = make(Record())
        self.queue.append(lambda e: instruction(e).then_inc(self.sem, 1))
        return (self.sem, self.n)

    def quiet(self, make):
        self.queue.append(make(Record()))

    def now(self):
        return (self.sem, self.n)


def build(nc, stream, xin, vecs, consts, masks, rope, hbias, gates, out):
    slots = plan()
    at, nvec = columns()
    base = nc.sbuf_base + (-nc.sbuf_base) % 64
    K = 1024

    def sb(name, kib, shape, dt=F32):
        return nc.alloc_sbuf_tensor_at(name, [P] + shape, dt, offset=base + int(kib * K))

    X = sb("X", 0, [DT, T])
    WR = sb("WR", 16, [RAW, SLOT])
    WHI = sb("WHI", 32, [SPL, SLOT], F32R)
    WLO = sb("WLO", 48, [SPL, SLOT], F32R)
    CON = sb("CON", 64, [7, P])
    VEC = sb("VEC", 67.5, [nvec])
    MSK = sb("MSK", 71, [8, P], U8)
    MSF = sb("MSF", 74, [8, P])
    NEGB = sb("NEGB", 72, [8])
    OML = sb("OML", 72.0625, [8])
    LBV = sb("LBV", 72.125, [8])
    C8 = sb("C8", 72.1875, [8])
    SMT = sb("SMT", 72.25, [4, 8])
    QNS = sb("QNS", 72.5, [2])
    SQ = sb("SQ", 74, [2, T])
    HF = sb("HF", 78, [2, T])
    RS = sb("RS", 82, [T])
    HHI = sb("HHI", 84, [DT, T], F32R)
    HLO = sb("HLO", 100, [DT, T], F32R)
    YHI = sb("YHI", 116, [DT, T], F32R)
    YLO = sb("YLO", 132, [DT, T], F32R)
    FHI = sb("FHI", 116, [FT, T], F32R)
    FLO = sb("FLO", 160, [FT, T], F32R)
    RT = sb("RT", 148, [5, P])
    COS = sb("COS", 150.5, [T])
    SIN = sb("SIN", 152.5, [T])
    Z = sb("Z", 156, [CH, T])
    XBC = sb("XBC", 164, [DT, T])
    Q = sb("Q", 180, [4, T])
    KD = sb("KD", 188, [2, T])
    V = sb("V", 192, [CH, P])
    PR = sb("PR", 194, [2, T])
    PT = sb("PT", 198, [2, CH, 256])
    NM = sb("NM", 206, [4])
    RSM = sb("RSM", 206.0625, [4])
    RIN = sb("RIN", 206.125, [4])
    DTR = sb("DTR", 206.25, [CH, 16])
    SGB = sb("SGB", 74, [4, T])
    XST = sb("XST", 84, [CH, T])
    BT = sb("BT", 92, [CH, 256])
    STF = sb("STF", 96, [3, T])
    STB = sb("STB", 102, [3, T])
    RA = sb("RA", 108, [8, P])
    DEC = sb("DEC", 112, [8, P])
    WF = sb("WF", 148, [8, P])
    WB = sb("WB", 152, [8, P])
    XCF = sb("XCF", 74, [T])
    XCB = sb("XCB", 76, [T])
    XCD = sb("XCD", 78, [T])
    MF = sb("MF", 80, [2, P])
    MB = sb("MB", 81, [2, P])
    YA = sb("YA", 82, [T])
    YB = sb("YB", 198, [T])
    SD = sb("SD", 180, [10, CH, 16])
    EX = sb("EX", 182.5, [5, CH, 16])
    DTE = sb("DTE", 184, [CH, 16])
    SS = sb("SS", 184.5, [2, 8])
    GHT = sb("GHT", 148, [8, T])
    HB = sb("HB", 132, [D])
    VH = sb("VH", 180, [CH, D])
    CU = sb("CU", 164, [DT, T])
    MG = sb("MG", 180, [DT, T])
    LF = sb("LF", 164, [T])
    CB = sb("CB", 166, [T])
    HK = sb("HK", 168, [T])
    HQ = sb("HQ", 170, [T])
    HD = sb("HD", 172, [T])
    HGS = sb("HGS", 174, [T])
    QT = sb("QT", 176, [2, T])
    KT = sb("KT", 196, [2, T])
    SAC = sb("SAC", 200, [CH, P])
    SOF = sb("SOF", 202, [768])
    RSET = sb("RSET", 205, [T])
    LX = sb("LX", 196, [T])
    XB = sb("XB", 198, [T])
    GR = sb("GR", 200, [T])
    GI = sb("GI", 202, [T])
    GA = sb("GA", 74, [T])
    GT = sb("GT", 76, [T])
    GG = sb("GG", 78, [T])
    GM = sb("GM", 80, [T])
    GW = sb("GW", 204, [2, 256])
    CVA = sb("CVA", 148, [2, T])
    SGA = sb("SGA", 152, [2, T])
    MU = sb("MU", 156, [T])
    PS = [nc.alloc_psum_tensor(f"PS{i}", [P, 512], F32) for i in range(8)]

    IDN, ONES, BONES, TRIF, TRIB, UP, LOW = (CON[:, i, :] for i in range(7))

    def vec(name, i=0, n=1):
        return VEC[:, at[name] + i:at[name] + i + n]

    sems = {}

    def sem(name):
        sems[name] = nc.alloc_semaphore(name)
        return sems[name]

    pe, dve, act, pool = (Engine(sem(n)) for n in ("s_pe", "s_dve", "s_act", "s_pool"))
    sp = Engine(None)
    engines = (pe, dve, act, pool)
    s_con, s_rope, s_hb, s_out = sem("s_con"), sem("s_rope"), sem("s_hb"), sem("s_out")
    s_gw = [sem(f"s_gw{i}") for i in range(2)]
    s_w = [sem(f"s_w{i}") for i in range(RAW)]

    def load(dst, src, s, value):
        sp.queue.append(lambda e: e.dma_start(dst, src).then_inc(s, 16))
        return (s, value)

    def everything():
        return [g.now() for g in engines]

    load(X[:, :, :], xin, s_con, 0)
    load(VEC[:, :], vecs, s_con, 0)
    load(CON[:, :, :], consts, s_con, 0)
    con = load(MSF[:, :, :], masks, s_con, 64)
    for g in engines:
        g.wait(con)
    mask_bytes = dve.op(lambda e: e.tensor_copy(MSK[:, :, :], MSF[:, :, :]))
    act.wait(mask_bytes)

    offset, o = [], 0
    for _, _, _, nr, _, ncol in slots:
        offset.append(o)
        o += P * nr * ncol
    state = {"load": 0, "split": 0, "next": 0}
    raw_free, split_free, split_done = {}, {}, {}

    def load_slot():
        i = state["load"]
        if i >= len(slots):
            return
        state["load"] += 1
        n = slots[i][3] * slots[i][5]
        if i >= RAW:
            sp.wait(*raw_free[i - RAW])
        src = stream[offset[i]:offset[i] + P * n].rearrange("(p n) -> p n", p=P)
        load(WR[:, i % RAW, 0:n], src, s_w[i % RAW], 0)

    def split_slot():
        i = state["split"]
        if i >= len(slots):
            return
        state["split"] += 1
        n = slots[i][3] * slots[i][5]
        raw, hi, lo = WR[:, i % RAW, 0:n], WHI[:, i % SPL, 0:n], WLO[:, i % SPL, 0:n]
        landed = (s_w[i % RAW], 16 * (i // RAW + 1))
        act.wait(landed)
        dve.wait(landed)
        if i >= SPL:
            act.wait(split_free[i - SPL])
            dve.wait(split_free[i - SPL])
        a = act.op(lambda e: e.copy(hi, raw))
        dve.wait(a)
        b = dve.op(lambda e: e.tensor_tensor(lo, raw, hi.bitcast(F32), ALU.subtract))
        raw_free[i] = (a, b)
        split_done[i] = (a, b)
        load_slot()

    for _ in range(RAW):
        load_slot()
    for _ in range(LOOK):
        split_slot()

    def take(name, i, r0, c0):
        k = state["next"]
        state["next"] += 1
        s = slots[k]
        assert s[:3] + (s[4],) == (name, i, r0, c0), (s, name, i, r0, c0)
        split_slot()
        pe.wait(*split_done[k])
        nr, ncol = s[3], s[5]
        n = nr * ncol
        hi = WHI[:, k % SPL, 0:n].rearrange("p (r c) -> p r c", r=nr)
        lo = WLO[:, k % SPL, 0:n].rearrange("p (r c) -> p r c", r=nr)
        return k, hi, lo

    bank_free = {i: [] for i in range(8)}
    turn = {"main": 0, "side": 0}

    def bank(kind="main"):
        b = turn[kind] % 4 + (0 if kind == "main" else 4)
        turn[kind] += 1
        pe.wait(*bank_free[b])
        return b

    def freed(b, *tokens):
        bank_free[b] = list(tokens)

    def mm(out_, lhsT, rhs, start, stop, last=False, **k):
        make = lambda e: e.matmul(out_, lhsT, rhs, start=start, stop=stop, **k)
        return pe.op(make) if last else pe.quiet(make)

    def transpose(out_, in_):
        return pe.op(lambda e: e.transpose(out_, in_, IDN))

    def product(name, i, c0, rhi, rlo, ready, rows=((0, DT),)):
        b = bank()
        for r0, nr in rows:
            k, hi, lo = take(name, i, r0, c0)
            for r in range(nr):
                pe.wait(*ready[r0 + r])
                first, final = r0 + r == 0, r0 + r == rows[-1][0] + rows[-1][1] - 1
                mm(PS[b][:, :], hi[:, r, :], rhi[:, r0 + r, :], first, False)
                mm(PS[b][:, :], hi[:, r, :], rlo[:, r0 + r, :], False, False)
                t = mm(PS[b][:, :], lo[:, r, :], rhi[:, r0 + r, :], False, final, last=r == nr - 1)
            split_free[k] = t
        return b, t

    def product_tokens(name, i, c0, ready):
        bs = [bank() for _ in range(CH)]
        ts = [None] * CH
        for r0 in range(0, DT, 2):
            k, hi, lo = take(name, i, r0, c0)
            for c in range(CH):
                for r in range(2):
                    pe.wait(*ready[r0 + r])
                    a, l = HHI[:, r0 + r, c * P:(c + 1) * P], HLO[:, r0 + r, c * P:(c + 1) * P]
                    first, final = r0 + r == 0, r0 + r == DT - 1
                    mm(PS[bs[c]][:, :], a, hi[:, r, :], first, False)
                    mm(PS[bs[c]][:, :], a, lo[:, r, :], False, False)
                    ts[c] = mm(PS[bs[c]][:, :], l, hi[:, r, :], False, final, last=r == 1)
            split_free[k] = ts[CH - 1]
        return list(zip(bs, ts))

    x_ready = [[] for _ in range(DT)]
    rs_free = [[]]

    def inverse_root(dst, src, n, eps, *ready):
        act.wait(*ready)
        t = act.op(lambda e: e.activation(dst, src, ACT.Ln, bias=eps, scale=1.0 / n))
        act.wait(t)
        return act.op(lambda e: e.activation(dst, dst, ACT.Exp, scale=-0.5))

    def mean_square():
        b = bank("side")
        for j in range(DT):
            act.wait(*x_ready[j])
            if j >= 2:
                act.wait(used[j - 2])
            else:
                used = [] if j == 0 else used
            t = act.op(lambda e, j=j: e.activation(SQ[:, j % 2, :], X[:, j, :], ACT.Square))
            pe.wait(t)
            used.append(mm(PS[b][:, :], ONES, SQ[:, j % 2, :], j == 0, j == DT - 1, last=True))
        act.wait(*rs_free[0])
        t = inverse_root(RS[:, :], PS[b][:, :], D, vec("eps"), used[-1])
        freed(b, t)
        return t

    def split(hi, lo, src, ready, free=()):
        act.wait(*ready, *free)
        a = act.op(lambda e: e.copy(hi, src))
        dve.wait(a, *ready, *free)
        return a, dve.op(lambda e: e.tensor_tensor(lo, src, hi.bitcast(F32), ALU.subtract))

    def norm_split(w):
        for g in (act, dve):
            g.wait(*everything())
        rs = mean_square()
        ready, free = [], [(), ()]
        for j in range(DT):
            dve.wait(rs, *x_ready[j], *free[j % 2])
            t = dve.op(lambda e, j=j: e.scalar_tensor_tensor(HF[:, j % 2, :], X[:, j, :], VEC[:, w + j:w + j + 1],
                                                            RS[:, :], ALU.mult, ALU.mult))
            ready.append(split(HHI[:, j, :], HLO[:, j, :], HF[:, j % 2, :], (t,)))
            free[j % 2] = ready[-1]
        rs_free[0] = [t]
        return ready

    def norm_x(w):
        rs = mean_square()
        for j in range(DT):
            dve.wait(rs, *x_ready[j])
            x_ready[j] = [dve.op(lambda e, j=j: e.scalar_tensor_tensor(
                X[:, j, :], X[:, j, :], VEC[:, w + j:w + j + 1], RS[:, :], ALU.mult, ALU.mult))]
        rs_free[0] = [x_ready[-1][0]]

    def add_to_x(j, b, t, scale=1.0):
        dve.wait(t, *x_ready[j])
        x_ready[j] = [dve.op(lambda e: e.scalar_tensor_tensor(X[:, j, :], PS[b][:, :], scale, X[:, j, :],
                                                              ALU.mult, ALU.add))]
        freed(b, x_ready[j][0])

    def ffn(w, gate, up, down, i, up0, scale):
        ready = norm_split(w)
        parts, sg_free, af_free = [], [(), ()], [(), ()]
        for j in range(FT):
            bg, tg = product(gate, i, j * P, HHI, HLO, ready)
            act.wait(tg, *sg_free[j % 2])
            s = act.op(lambda e: e.activation(SQ[:, j % 2, :], PS[bg][:, :], ACT.Silu))
            freed(bg, s)
            bu, tu = product(up, i, up0 + j * P, HHI, HLO, ready)
            dve.wait(s, tu, *af_free[j % 2])
            m = dve.op(lambda e: e.tensor_tensor(HF[:, j % 2, :], SQ[:, j % 2, :], PS[bu][:, :], ALU.mult))
            sg_free[j % 2] = (m,)
            freed(bu, m)
            parts.append(split(FHI[:, j, :], FLO[:, j, :], HF[:, j % 2, :], (m,)))
            af_free[j % 2] = parts[-1]
        for j in range(DT):
            b, t = product(down, i, j * P, FHI, FLO, parts, ((0, 8), (8, 8), (16, 6)))
            add_to_x(j, b, t, scale)

    def rope_tile(b, t, w, j, tables):
        raw = SGB[:, 0, :]
        act.wait(t, *tables, dve.now(), pe.now())
        a = act.op(lambda e: e.copy(raw, PS[b][:, :]))
        s = act.op(lambda e: e.activation(SGB[:, 1, :], PS[b][:, :], ACT.Square))
        freed(b, s)
        n = bank("side")
        pe.wait(s)
        t = mm(PS[n][:, :], BONES, SGB[:, 1, :], True, True, last=True)
        r = inverse_root(RS[:, :], PS[n][:, :], 64, vec("eps"), t)
        freed(n, r)
        dve.wait(a, r)
        qn = dve.op(lambda e: e.scalar_tensor_tensor(raw, raw, w, RS[:, :], ALU.mult, ALU.mult))
        for dst, plain, turned in ([(Q[:, j, :], None, 0)] if j < 4 else [(KD[:, 0, :], 1, 3), (KD[:, 1, :], 2, 4)]):
            pe.wait(qn)
            src, b1 = raw, None
            if plain is not None:
                b1 = bank("side")
                t1 = mm(PS[b1][:, :], RT[:, plain, :], raw, True, True, last=True)
                src = PS[b1][:, :]
                dve.wait(t1)
            b2 = bank("side")
            t2 = mm(PS[b2][:, :], RT[:, turned, :], raw, True, True, last=True)
            dve.wait(dve.now())
            u = dve.op(lambda e, src=src: e.tensor_tensor(SGB[:, 2, :], src, COS[:, :], ALU.mult))
            if b1 is not None:
                freed(b1, u)
            dve.wait(t2)
            v = dve.op(lambda e, b2=b2: e.tensor_tensor(SGB[:, 3, :], PS[b2][:, :], SIN[:, :], ALU.mult))
            freed(b2, v)
            dve.wait(u, v)
            q = dve.op(lambda e, dst=dst: e.tensor_tensor(dst, SGB[:, 2, :], SGB[:, 3, :], ALU.add))
        return q

    def attention(qk, v_ready, parts):
        probs, pr_free, pt_free, pt_done, pv = {}, [(), ()], [(), ()], {}, {}
        steps = [(h, c) for h in range(NH) for c in range(CH)]

        def scores(i):
            h, c = steps[i]
            lo = 64 * (h % 2)
            b = bank("side")
            pe.wait(*qk)
            t = mm(PS[b][:, :], Q[lo:lo + 64, h // 2, c * P:(c + 1) * P], KD[lo:lo + 64, h // 4, :], True, True, last=True)
            k = i % 4
            dve.wait(t, act.now() if i < 4 else probs[i - 4][1])
            m = dve.op(lambda e: e.tensor_reduce(NM[:, k:k + 1], PS[b][:, :], AX, ALU.max, negate=True))
            act.wait(m, *pr_free[i % 2])
            x = act.op(lambda e: e.activation(PR[:, i % 2, :], PS[b][:, :], ACT.Exp, bias=NM[:, k:k + 1],
                                              accum_out=RSM[:, k:k + 1]))
            freed(b, x)
            dve.wait(x)
            r = dve.op(lambda e: e.reciprocal(RIN[:, k:k + 1], RSM[:, k:k + 1]))
            dve.wait(r)
            n = dve.op(lambda e: e.tensor_scalar(PR[:, i % 2, :], PR[:, i % 2, :], RIN[:, k:k + 1], None, ALU.mult))
            probs[i] = (n, x)

        def turn_probs(i):
            h, c = steps[i]
            half = i // 2
            b = bank("side")
            pe.wait(probs[i][0])
            for k in range(CH):
                t = transpose(PS[b][:, k * P:(k + 1) * P], PR[:, i % 2, k * P:(k + 1) * P])
            pr_free[i % 2] = (t,)
            g = act if i % 2 else dve
            g.wait(t, *pt_free[half % 2])
            dst = PT[:, half % 2, :, (c % 2) * P:(c % 2 + 1) * P]
            src = PS[b][:, :].rearrange("p (k q) -> p k q", k=CH)
            e_ = g.op((lambda e: e.copy(dst, src)) if g is act else (lambda e: e.tensor_copy(dst, src)))
            freed(b, e_)
            pt_done[i] = e_

        def values(half):
            h, q0 = half // 2, 256 * (half % 2)
            lo = 64 * (h % 2)
            b = bank("side")
            pe.wait(pt_done[2 * half], pt_done[2 * half + 1], *v_ready)
            for k in range(CH):
                t = mm(PS[b][lo:lo + 64, 0:256], V[:, k, 64 * (h // 4):64 * (h // 4) + 64], PT[:, half % 2, k, :],
                       k == 0, k == CH - 1, last=k == CH - 1)
            pt_free[half % 2] = (t,)
            a, l = split(YHI[lo:lo + 64, h // 2, q0:q0 + 256], YLO[lo:lo + 64, h // 2, q0:q0 + 256],
                         PS[b][lo:lo + 64, 0:256], (t,))
            freed(b, a, l)
            parts[h // 2] += [a, l]

        n = len(steps)
        for i in range(n + 3):
            if i < n:
                scores(i)
            if 1 <= i <= n:
                turn_probs(i - 1)
            if i >= 3 and i % 2 == 1:
                values((i - 3) // 2)
            yield

    def heads_by(x, n=8, w=64):
        return x.unsqueeze(2).to_broadcast([P, n, w])

    def block1(l):
        cols = lambda name, i=0, n=1: VEC[:, at[name, l] + i:at[name, l] + i + n]
        for g in (dve, act, pool, pe, sp):
            g.wait(*everything())
        load(RT[:, :, :], rope[:, 0:640].rearrange("p (a b) -> p a b", a=5), s_rope, 0)
        load(COS[:, :], rope[:, 640:1152], s_rope, 0)
        tables = [load(SIN[:, :], rope[:, 1152:1664], s_rope, 48 * (l + 1))]
        for g in (pe, dve):
            g.wait(*tables)
        ready = norm_split(at["nmix", l])
        dve.op(lambda e: e.tensor_scalar(QNS[:, 0:1], cols("qn"), 0.125, None, ALU.mult))
        dve.wait(dve.now())
        for j in range(5):
            b, t = product("w_in", l, j * P, HHI, HLO, ready)
            qk = rope_tile(b, t, QNS[:, 0:1] if j < 4 else cols("kn"), j, tables)
        k, hi, lo = take("w_in", l, 0, 640)
        b = bank()
        for c in range(CH):
            for r in range(DT):
                a, s = HHI[:, r, c * P:(c + 1) * P], HLO[:, r, c * P:(c + 1) * P]
                o_ = PS[b][:, c * P:(c + 1) * P]
                mm(o_, a, hi[:, r, :], r == 0, False)
                mm(o_, a, lo[:, r, :], False, False)
                t = mm(o_, s, hi[:, r, :], False, r == DT - 1, last=r == DT - 1)
        split_free[k] = t
        act.wait(t)
        v_ready = [act.op(lambda e: e.copy(V[:, :, :].rearrange("p a b -> p (a b)"), PS[b][:, :]))]
        freed(b, v_ready[0])
        k, hi, lo = take("w_in", l, 0, 2304)
        b2 = bank()
        for c in range(CH):
            for r in range(DT):
                a, s = HHI[:, r, c * P:(c + 1) * P], HLO[:, r, c * P:(c + 1) * P]
                o_ = PS[b2][:, c * 16:c * 16 + 16]
                mm(o_, a, hi[:, r, :], r == 0, False)
                mm(o_, a, lo[:, r, :], False, False)
                t = mm(o_, s, hi[:, r, :], False, r == DT - 1, last=r == DT - 1)
        split_free[k] = t
        dve.wait(t)
        dt_raw = dve.op(lambda e: e.tensor_tensor(
            DTR[:, :, :], PS[b2][:, 0:64].rearrange("p (c h) -> p c h", c=CH),
            cols("dtb", 0, 16).unsqueeze(1).to_broadcast([P, CH, 16]), ALU.add))
        freed(b2, dt_raw)
        parts = [[] for _ in range(DT)]
        attn = attention([qk], v_ready, parts)
        z_done, x_done = [], []

        def projections():
            for c, (b, t) in enumerate(product_tokens("w_in", l, 768, ready)):
                act.wait(t)
                z_done.append(act.op(lambda e, c=c, b=b: e.copy(Z[:, c, :], PS[b][:, :])))
                freed(b, z_done[-1])
            yield
            yield
            yield
            yield
            for j in range(8):
                b, t = product("w_in", l, 1280 + j * P, HHI, HLO, ready)
                act.wait(t)
                w = lambda k: cols("cw", 8 * k + j)
                y = act.op(lambda e: e.activation(XBC[:, j, :], PS[b][:, :], ACT.Identity, bias=cols("cb", j), scale=w(2)))
                for k, s in ((0, -2), (1, -1), (3, 1), (4, 2)):
                    o0, o1 = max(0, -s), T - max(0, s)
                    dve.wait(y)
                    y = dve.op(lambda e, k=k, s=s, o0=o0, o1=o1: e.scalar_tensor_tensor(
                        XBC[:, j, o0:o1], PS[b][:, o0 + s:o1 + s], w(k), XBC[:, j, o0:o1], ALU.mult, ALU.add))
                freed(b, y)
                x_done.append(y)
                yield

        proj = projections()
        going = True
        step = 0
        for _ in attn:
            step += 1
            if going and step % 3 == 1:
                going = next(proj, "end") != "end"
        for _ in proj:
            pass
        for g in (dve, act, pool):
            g.wait(*everything())
        done = []
        for src in (Z[:, :, :], XBC[:, 0:4, :], XBC[:, 4:8, :]):
            act.wait(*z_done, *x_done, *done)
            s = act.op(lambda e, src=src: e.activation(SGB[:, :, :], src, ACT.Sigmoid))
            dve.wait(s)
            done = [dve.op(lambda e, src=src: e.tensor_tensor(src, src, SGB[:, :, :], ALU.mult))]
        silu = done
        sd = lambda i: SD[:, i, :, :]

        def chain(g, make, *also):
            g.wait(*also)
            t = g.op(make)
            for o_ in (dve, act):
                o_.wait(t)
            return t

        x0, tt, uu = DTR[:, :, :], ALU, None
        chain(dve, lambda e: e.tensor_scalar(sd(0), x0, -1.0, None, ALU.mult), dt_raw)
        chain(dve, lambda e: e.tensor_tensor(sd(0), sd(0), x0, ALU.max))
        chain(act, lambda e: e.activation(sd(1), sd(0), ACT.Exp, scale=-1.0))
        chain(dve, lambda e: e.tensor_scalar(sd(2), sd(1), 1.0, None, ALU.add))
        chain(act, lambda e: e.activation(sd(3), sd(2), ACT.Ln))
        chain(dve, lambda e: e.tensor_scalar(sd(2), sd(2), -1.0, None, ALU.add))
        chain(dve, lambda e: e.tensor_tensor(sd(2), sd(1), sd(2), ALU.subtract))
        chain(dve, lambda e: e.tensor_tensor(sd(3), sd(3), sd(2), ALU.add))
        chain(dve, lambda e: e.tensor_scalar(sd(0), x0, 0.0, None, ALU.max))
        chain(dve, lambda e: e.tensor_tensor(sd(4), sd(0), sd(3), ALU.add))
        step_ = sd(4)
        chain(act, lambda e: e.activation(SD[:, 5, 0, :], cols("alog", 0, 16), ACT.Exp))
        chain(dve, lambda e: e.tensor_scalar(SD[:, 5, 0, :], SD[:, 5, 0, :], -1.0, None, ALU.mult))
        da = chain(dve, lambda e: e.tensor_tensor(
            sd(6), step_, SD[:, 5, 0, :].unsqueeze(1).to_broadcast([P, CH, 16]), ALU.mult))
        b = bank("side")
        pe.wait(da)
        dA = sd(6).rearrange("p a b -> p (a b)")
        for i, m in enumerate((UP, LOW, TRIF, TRIB, ONES)):
            t = mm(PS[b][:, i * 64:(i + 1) * 64], m, dA, True, True, last=True)
        ex = chain(act, lambda e: e.activation(EX[:, :, :, :].rearrange("p a b c -> p (a b c)"), PS[b][:, 0:320], ACT.Exp), t)
        freed(b, ex)
        for d in range(2):
            dte = chain(dve, lambda e, d=d: e.tensor_tensor(
                DTE[:, :, 8 * d:8 * d + 8], step_[:, :, 8 * d:8 * d + 8], EX[:, d, :, 8 * d:8 * d + 8], ALU.mult))
        for c in range(CH):
            b = bank("side")
            pe.wait(*silu)
            for i in range(4):
                t = transpose(PS[b][:, i * P:(i + 1) * P], XBC[:, i, c * P:(c + 1) * P])
            act.wait(t)
            a = act.op(lambda e, b=b, c=c: e.copy(XST[:, c, :], PS[b][:, :]))
            freed(b, a)
            b = bank("side")
            for i in range(2):
                t = transpose(PS[b][:, i * P:(i + 1) * P], XBC[:, 4 + i, c * P:(c + 1) * P])
            act.wait(t)
            tok = act.op(lambda e, b=b, c=c: e.copy(BT[:, c, :], PS[b][:, 0:256]))
            freed(b, tok)
        by_head = lambda x: x.rearrange("p (h d) -> p h d", h=8)
        xcd_free, st = [()], {}
        for d, order, S in ((0, (0, 1, 2), STF), (1, (3, 2, 1), STB)):
            prev = None
            for n, c in enumerate(order):
                dve.wait(tok, dte, *xcd_free[0])
                x = dve.op(lambda e, c=c, d=d: e.tensor_tensor(
                    by_head(XCD[:, :]), by_head(XST[:, c, :]), heads_by(DTE[:, c, 8 * d:8 * d + 8]), ALU.mult))
                b = bank("side")
                pe.wait(x, tok)
                for g in range(2):
                    t = mm(PS[b][:, 256 * g:256 * g + 256], BT[:, c, g * P:(g + 1) * P], XCD[:, 256 * g:256 * g + 256],
                           True, True, last=True)
                xcd_free[0] = (t,)
                dve.wait(t)
                if prev is None:
                    s = dve.op(lambda e, b=b, S=S: e.tensor_copy(S[:, 0, :], PS[b][:, :]))
                else:
                    dve.wait(prev)
                    s = dve.op(lambda e, n=n, c=c, d=d, S=S: e.tensor_tensor(
                        by_head(S[:, n, :]), by_head(S[:, n - 1, :]), heads_by(EX[:, 4, c, 8 * d:8 * d + 8]), ALU.mult))
                    dve.wait(s)
                    s = dve.op(lambda e, n=n, b=b, S=S: e.tensor_tensor(S[:, n, :], S[:, n, :], PS[b][:, :], ALU.add))
                freed(b, s)
                prev = s
                st[d, c + 1 if d == 0 else c - 1] = (S, n, s)
        yt = [bank() for _ in range(4)]
        for c in range(CH):
            b = bank("side")
            for g in range(2):
                t = mm(PS[b][:, g * P:(g + 1) * P], XBC[:, 4 + g, c * P:(c + 1) * P], XBC[:, 6 + g, c * P:(c + 1) * P],
                       True, True, last=True)
            dve.wait(t, pe.now())
            sc = PS[b][:, 0:256].rearrange("p (g t) -> p g t", g=2)
            both = []
            for M, tri in ((MF, TRIF), (MB, TRIB)):
                both.append(dve.op(lambda e, M=M, tri=tri, sc=sc: e.tensor_tensor(
                    M[:, :, :], sc, tri.unsqueeze(1).to_broadcast([P, 2, P]), ALU.mult)))
            freed(b, *both)
            ws = []
            for d, tri, side_, M, W, XC in ((0, TRIF, UP, MF, WF, XCF), (1, TRIB, LOW, MB, WB, XCB)):
                dve.wait(pe.now(), act.now())
                r = dve.op(lambda e, c=c, d=d, tri=tri: e.tensor_tensor(
                    RA[:, :, :], heads_by(sd(6)[:, c, 8 * d:8 * d + 8], 8, P),
                    tri.unsqueeze(1).to_broadcast([P, 8, P]), ALU.mult))
                pe.wait(r)
                for g in range(2):
                    b = bank("side")
                    t = mm(PS[b][:, :], side_, RA[:, 4 * g:4 * g + 4, :].rearrange("p h t -> p (h t)"), True, True, last=True)
                    act.wait(t, dve.now())
                    a = act.op(lambda e, b=b, g=g: e.activation(
                        DEC[:, 4 * g:4 * g + 4, :].rearrange("p h t -> p (h t)"), PS[b][:, :], ACT.Exp))
                    freed(b, a)
                dve.wait(a, *both)
                for g in range(2):
                    ws.append(dve.op(lambda e, g=g, M=M, W=W: e.tensor_tensor(
                        W[:, 4 * g:4 * g + 4, :], DEC[:, 4 * g:4 * g + 4, :],
                        M[:, g, :].unsqueeze(1).to_broadcast([P, 4, P]), ALU.mult)))
                ws.append(dve.op(lambda e, c=c, d=d, XC=XC: e.tensor_tensor(
                    by_head(XC[:, :]), by_head(XST[:, c, :]), heads_by(step_[:, c, 8 * d:8 * d + 8]), ALU.mult)))
            yb = bank("side")
            pe.wait(*ws)
            for h in range(8):
                o_ = PS[yb][:, 64 * h:64 * h + 64]
                mm(o_, WF[:, h, :], XCF[:, 64 * h:64 * h + 64], True, False)
                t = mm(o_, WB[:, h, :], XCB[:, 64 * h:64 * h + 64], False, True, last=True)
            dve.wait(tok, *everything())
            y = dve.op(lambda e, c=c: e.tensor_tensor(by_head(YA[:, :]), by_head(XST[:, c, :]),
                                                      heads_by(cols("dsk", 0, 8)), ALU.mult))
            dve.wait(y, t)
            y = dve.op(lambda e, yb=yb: e.tensor_tensor(YA[:, :], YA[:, :], PS[yb][:, :], ALU.add))
            freed(yb, y)
            for d in range(2):
                if (d, c) not in st:
                    continue
                S, n, s = st[d, c]
                b = bank("side")
                pe.wait(s)
                for g in range(2):
                    t = mm(PS[b][:, 256 * g:256 * g + 256], XBC[:, 6 + g, c * P:(c + 1) * P], S[:, n, 256 * g:256 * g + 256],
                           True, True, last=True)
                dve.wait(t, y)
                u = dve.op(lambda e, b=b, c=c, d=d: e.tensor_tensor(
                    by_head(YB[:, :]), by_head(PS[b][:, :]), heads_by(EX[:, 2 + d, c, 8 * d:8 * d + 8]), ALU.mult))
                freed(b, u)
                dve.wait(u)
                y = dve.op(lambda e: e.tensor_tensor(YA[:, :], YA[:, :], YB[:, :], ALU.add))
            dve.wait(y)
            y = dve.op(lambda e, c=c: e.tensor_tensor(YA[:, :], YA[:, :], Z[:, c, :], ALU.mult))
            act.wait(y)
            for g in range(2):
                q = act.op(lambda e, c=c, g=g: e.activation(YB[:, 0:256], YA[:, 256 * g:256 * g + 256], ACT.Square,
                                                           accum_out=SS[:, 0, 2 * c + g:2 * c + g + 1]))
                act.wait(q)
            r = inverse_root(SS[:, 1, 2 * c:2 * c + 2], SS[:, 0, 2 * c:2 * c + 2], 256, vec("eps"))
            dve.wait(r)
            for g in range(2):
                y = dve.op(lambda e, c=c, g=g: e.tensor_scalar(
                    YA[:, 256 * g:256 * g + 256], YA[:, 256 * g:256 * g + 256], SS[:, 1, 2 * c + g:2 * c + g + 1], None, ALU.mult))
            pe.wait(y)
            for i in range(4):
                t = transpose(PS[yt[i]][:, c * P:(c + 1) * P], YA[:, i * P:(i + 1) * P])
        for i in range(4):
            act.wait(t)
            a = act.op(lambda e, i=i: e.activation(YHI[:, 4 + i, :], PS[yt[i]][:, :], ACT.Copy, scale=cols("sn", i)))
            dve.wait(a)
            d_ = dve.op(lambda e, i=i: e.scalar_tensor_tensor(YLO[:, 4 + i, :], PS[yt[i]][:, :], cols("sn", i),
                                                              YHI[:, 4 + i, :].bitcast(F32), ALU.mult, ALU.subtract))
            freed(yt[i], d_)
            parts[4 + i] += [a, d_]
        for j in range(DT):
            b, t = product("w_out", l, j * P, YHI, YLO, parts)
            add_to_x(j, b, t)
        for g in (dve, act, pool, pe):
            g.wait(*everything())
        ffn(at["nffn", l], "w_gate", "w_up", "w_down", l, 0, 1.0)

    def biased(i):
        return vec("bin", i)

    def gated(dst, b, t, bias, tmp, free=()):
        act.wait(t, *free)
        s = act.op(lambda e: e.activation(tmp, PS[b][:, :], ACT.Sigmoid, bias=bias))
        dve.wait(s, *free)
        y = dve.op(lambda e: e.scalar_tensor_tensor(dst, PS[b][:, :], bias, tmp, ALU.add, ALU.mult))
        freed(b, y)
        return y

    def small_vectors():
        s = lambda i: SMT[:, i, :]

        def go(g, make):
            t = g.op(make)
            for o_ in (dve, act):
                o_.wait(t)

        lg, lam = vec("lb", 0, 8), vec("lam", 0, 8)
        go(dve, lambda e: e.tensor_tensor(s(0), lg, lg, ALU.subtract))
        go(act, lambda e: e.activation(s(1), s(0), ACT.Exp))
        go(dve, lambda e: e.reciprocal(s(2), s(1)))
        go(dve, lambda e: e.tensor_tensor(s(3), s(1), s(2), ALU.mult))
        go(dve, lambda e: e.tensor_tensor(LBV[:, :], s(3), s(3), ALU.subtract))
        go(dve, lambda e: e.tensor_scalar(OML[:, :], LBV[:, :], -1.0, 1.0, ALU.mult, ALU.add))
        go(dve, lambda e: e.tensor_scalar(NEGB[:, :], vec("bin", 8, 8), -1.0, None, ALU.mult))
        go(dve, lambda e: e.tensor_scalar(s(0), lam, -1.0, None, ALU.mult))
        go(dve, lambda e: e.tensor_tensor(s(1), s(0), lam, ALU.max))
        go(act, lambda e: e.activation(s(1), s(1), ACT.Exp, scale=-1.0))
        go(dve, lambda e: e.tensor_scalar(s(2), s(1), 1.0, None, ALU.add))
        go(act, lambda e: e.activation(s(3), s(2), ACT.Ln))
        go(dve, lambda e: e.tensor_scalar(s(2), s(2), -1.0, None, ALU.add))
        go(dve, lambda e: e.tensor_tensor(s(2), s(1), s(2), ALU.subtract))
        go(dve, lambda e: e.tensor_tensor(s(3), s(3), s(2), ALU.add))
        go(dve, lambda e: e.tensor_scalar(s(0), s(0), 0.0, None, ALU.max))
        go(dve, lambda e: e.tensor_tensor(s(3), s(3), s(0), ALU.add))
        go(dve, lambda e: e.tensor_scalar(C8[:, :], s(3), -8.0, None, ALU.mult))

    def recurrence(j, ready, v_ready, lt):
        m = "w_in_mix_2"
        b, t = product(m, 0, 1024 + j * P, HHI, HLO, ready)
        act.wait(t, *everything())
        f = act.op(lambda e: e.activation(LF[:, :], PS[b][:, :], ACT.Sigmoid, bias=biased(8 + j)))
        k = act.op(lambda e: e.activation(HK[:, :], PS[b][:, :], ACT.Sigmoid, bias=NEGB[:, j:j + 1], scale=-1.0))
        freed(b, k)
        b, t = product(m, 0, j * P, HHI, HLO, ready)
        q = gated(HQ[:, :], b, t, biased(j), HD[:, :])
        b, t = product(m, 0, 3072 + j * P, HHI, HLO, ready)
        g = gated(HGS[:, :], b, t, biased(24 + j), QT[:, 1, :])
        dve.wait(f, k, q)
        f = dve.op(lambda e: e.tensor_scalar(LF[:, :], LF[:, :], OML[:, j:j + 1], LBV[:, j:j + 1], ALU.mult, ALU.add))
        k = dve.op(lambda e: e.tensor_scalar(HK[:, :], HK[:, :], OML[:, j:j + 1], None, ALU.mult))
        dve.wait(f)
        f2 = dve.op(lambda e: e.tensor_scalar(HD[:, :], LF[:, :], 1.0 / TINY, 1.0, ALU.mult, ALU.min))
        dve.wait(f2)
        f1 = dve.op(lambda e: e.tensor_scalar(LF[:, :], LF[:, :], TINY, None, ALU.max))
        act.wait(f1, f2)
        l2 = act.op(lambda e: e.activation(HD[:, :], HD[:, :], ACT.Ln))
        l1 = act.op(lambda e: e.activation(LF[:, :], LF[:, :], ACT.Ln))
        dve.wait(l1, l2)
        lf = dve.op(lambda e: e.tensor_tensor(LF[:, :], LF[:, :], HD[:, :], ALU.add))
        dve.wait(lf)
        cb = dve.op(lambda e: e.tensor_tensor_scan(CB[:, :], RSET[:, :], LF[:, :], 0.0, ALU.mult, ALU.add))
        pool.wait(*everything())
        sac = pool.op(lambda e: e.memset(SAC[:, :, :], 0.0))
        dve.wait(sac, cb, g)
        pool.wait(k)
        free = [(), ()]
        d_free = [cb]
        for n, h in enumerate(LEVELS + (0,)):
            if h:
                blk = lambda x: x.rearrange("p (n w) -> p n w", w=2 * h)
                nb = T // (2 * h)
                cbv, hd = blk(CB[:, :]), blk(HD[:, :])
                dve.wait(*d_free)
                dd = dve.op(lambda e, cbv=cbv, hd=hd, h=h, nb=nb: e.tensor_tensor(
                    hd, cbv, cbv[:, :, h - 1:h].to_broadcast([P, nb, 2 * h]), ALU.subtract))
                act.wait(dd)
                e1 = act.op(lambda e, hd=hd, h=h: e.activation(hd[:, :, h:2 * h], hd[:, :, h:2 * h], ACT.Exp))
                e2 = act.op(lambda e, hd=hd, h=h: e.activation(hd[:, :, 0:h], hd[:, :, 0:h], ACT.Exp, scale=-1.0))
                qt, kt = blk(QT[:, n % 2, :]), blk(KT[:, n % 2, :])
                qv, kv = blk(HQ[:, :]), blk(HK[:, :])
                dve.wait(e1, *free[n % 2])
                pool.wait(e2, *free[n % 2], *lt)
                a = dve.op(lambda e, qt=qt, qv=qv, hd=hd, h=h: e.tensor_tensor(
                    qt[:, :, h:2 * h], qv[:, :, h:2 * h], hd[:, :, h:2 * h], ALU.mult))
                c_ = pool.op(lambda e, kt=kt, kv=kv, hd=hd, h=h: e.tensor_tensor(
                    kt[:, :, 0:h], kv[:, :, 0:h], hd[:, :, 0:h], ALU.mult))
                d_free = [a, c_]
                pe.wait(a, c_)
                lhs, rhs = KT[:, n % 2, :], QT[:, n % 2, :]
            else:
                pe.wait(k, q)
                lhs, rhs = HK[:, :], HQ[:, :]
            b = bank("side")
            for c in range(CH):
                t = mm(PS[b][:, c * P:(c + 1) * P], lhs[:, c * P:(c + 1) * P], rhs[:, c * P:(c + 1) * P], True, True,
                       last=c == CH - 1)
            free[n % 2] = (t,)
            dve.wait(t, sac)
            sac = dve.op(lambda e, n=n, b=b: e.copy_predicated(
                SAC[:, :, :], MSK[:, n, :].unsqueeze(1).to_broadcast([P, CH, P]),
                PS[b][:, :].rearrange("p (c t) -> p c t", c=CH)))
            freed(b, sac)
        act.wait(*d_free)
        eb = act.op(lambda e: e.activation(HD[:, :], CB[:, :], ACT.Exp))
        act.wait(*lt, *free[0], *free[1])
        ends = [CB[:, c * P + P - 1:c * P + P] for c in range(CH)]
        whole = [HD[:, c * P + P - 1:c * P + P] for c in range(CH)]
        for c in range(3):
            ek = act.op(lambda e, c=c: e.activation(LF[:, c * P:(c + 1) * P], CB[:, c * P:(c + 1) * P], ACT.Exp,
                                                    bias=ends[c], scale=-1.0))
        QX, KX = QT[:, 0, :], KT[:, 0, :]
        dve.wait(eb, ek, *free[0], *free[1])
        a1 = dve.op(lambda e: e.tensor_tensor(QX[:, P:T], HQ[:, P:T], HD[:, P:T], ALU.mult))
        a2 = dve.op(lambda e: e.tensor_tensor(QX[:, 0:P], HQ[:, 3 * P:T], HD[:, 3 * P:T], ALU.mult))
        dve.wait(a1)
        a3 = dve.op(lambda e: e.tensor_scalar(QX[:, 3 * P:T], QX[:, 3 * P:T], whole[2], None, ALU.mult))
        a4 = dve.op(lambda e: e.tensor_tensor(KX[:, 0:3 * P], HK[:, 0:3 * P], LF[:, 0:3 * P], ALU.mult))
        dve.wait(a4)
        a5 = dve.op(lambda e: e.tensor_scalar(KX[:, 3 * P:T], KX[:, 0:P], whole[1], None, ALU.mult))
        pe.wait(a3, a5)
        ba = bank("side")
        mm(PS[ba][:, 0:P], KX[:, 0:P], QX[:, P:2 * P], True, True)
        ta = mm(PS[ba][:, P:3 * P], KX[:, 3 * P:T], QX[:, 2 * P:T], True, True, last=True)
        bb = bank("side")
        mm(PS[bb][:, 0:2 * P], KX[:, P:2 * P], QX[:, 2 * P:T], True, True)
        tb = mm(PS[bb][:, 2 * P:3 * P], KX[:, 2 * P:3 * P], QX[:, 0:P], True, True, last=True)
        act.wait(ta, tb)
        s1 = act.op(lambda e: e.copy(SOF[:, 0:384], PS[ba][:, 0:384]))
        s2 = act.op(lambda e: e.copy(SOF[:, 384:768], PS[bb][:, 0:384]))
        freed(ba, s1)
        freed(bb, s2)
        bo = bank("side")
        pe.wait(sac, s1, s2, *v_ready)
        v = [VH[:, c, j * P:(j + 1) * P] for c in range(CH)]
        o_ = PS[bo]
        kw = {"skip_group_check": True}
        mm(o_[:, P:T], v[0], SOF[:, 0:384], True, False, **kw)
        mm(o_[:, 0:P], v[0], SAC[:, 0, :], False, False, **kw)
        mm(o_[:, P:2 * P], v[1], SAC[:, 1, :], False, False, **kw)
        mm(o_[:, 2 * P:T], v[1], SOF[:, 384:640], False, False, **kw)
        mm(o_[:, 2 * P:3 * P], v[2], SAC[:, 2, :], False, False, **kw)
        mm(o_[:, 3 * P:T], v[2], SOF[:, 640:768], False, False, **kw)
        to = mm(o_[:, 3 * P:T], v[3], SAC[:, 3, :], False, True, last=True, **kw)
        act.wait(to)
        sq = act.op(lambda e: e.activation(SQ[:, 0, :], PS[bo][:, :], ACT.Square))
        bn = bank("side")
        pe.wait(sq)
        tn = mm(PS[bn][:, :], ONES, SQ[:, 0, :], True, True, last=True)
        act.wait(dve.now())
        r = inverse_root(RS[:, :], PS[bn][:, :], P, vec("eps"), tn)
        freed(bn, r)
        dve.wait(r, to)
        y = dve.op(lambda e: e.scalar_tensor_tensor(HF[:, 0, :], PS[bo][:, :], vec("hgn"), RS[:, :], ALU.mult, ALU.mult))
        freed(bo, y)
        dve.wait(y)
        y = dve.op(lambda e: e.tensor_tensor(HF[:, 0, :], HF[:, 0, :], HGS[:, :], ALU.mult))
        return split(YHI[:, j, :], YLO[:, j, :], HF[:, 0, :], (y,))

    def conv_in(j, ready):
        m = "w_in_mix_2"
        ba, ta = product(m, 0, 6144 + j * P, HHI, HLO, ready)
        bb, tb = product(m, 0, 7168 + j * P, HHI, HLO, ready)
        act.wait(tb, dve.now())
        s = act.op(lambda e: e.activation(SGA[:, j % 2, :], PS[bb][:, :], ACT.Sigmoid, bias=biased(56 + j)))
        freed(bb, s)
        dve.wait(s, ta)
        c = dve.op(lambda e: e.scalar_tensor_tensor(CU[:, j, :], PS[ba][:, :], biased(48 + j), SGA[:, j % 2, :], ALU.add, ALU.mult))
        freed(ba, c)
        return c

    def conv_taps(j, ready, done):
        acc = CVA[:, j % 2, :]
        w = lambda k: vec("cvw", 8 * k + j)
        act.wait(ready, dve.now())
        y = act.op(lambda e: e.activation(acc, CU[:, j, :], ACT.Identity, bias=vec("cvb", j), scale=w(TAPS - 1)))
        for s in range(1, TAPS):
            dve.wait(y)
            y = dve.op(lambda e, s=s: e.scalar_tensor_tensor(CVA[:, j % 2, s:T], CU[:, j, 0:T - s], w(TAPS - 1 - s),
                                                             CVA[:, j % 2, s:T], ALU.mult, ALU.add))
            if s % 6 == 0:
                yield
        act.wait(y)
        done[j] = act.op(lambda e: e.copy(CU[:, j, :], acc))
        yield

    def branch(x, ready, parts, taps, first):
        m = "w_in_mix_2"
        for j in range(8):
            b, t = product(m, 0, 8192 + x * D + j * P, HHI, HLO, ready)
            act.wait(t, *sga_free[j % 2])
            s = act.op(lambda e: e.activation(SGA[:, j % 2, :], PS[b][:, :], ACT.Sigmoid, bias=biased(64 + 8 * x + j)))
            freed(b, s)
            next(taps, None)
            b, t = product("w_branch_2", x, j * P, YHI, YLO, parts)
            merge(j, b, t, s, SGA[:, j % 2, :], first)
            sga_free[j % 2] = mg[j]
            next(taps, None)

    sga_free = [(), ()]
    mg = {}

    def merge(j, b, t, s, sg, first):
        dve.wait(s, t)
        if first:
            y = dve.op(lambda e: e.tensor_tensor(MG[:, j, :], sg, PS[b][:, :], ALU.mult))
        else:
            y = dve.op(lambda e: e.tensor_tensor(sg, sg, PS[b][:, :], ALU.mult))
            dve.wait(y, *mg[j])
            y = dve.op(lambda e: e.tensor_tensor(MG[:, j, :], MG[:, j, :], sg, ALU.add))
        freed(b, y)
        mg[j] = (y,)

    def lru(j, ready, gw, free):
        m = "w_in_mix_2"
        b, t = product(m, 0, 4096 + j * P, HHI, HLO, ready)
        act.wait(t, dve.now(), pe.now())
        x = act.op(lambda e: e.activation(LX[:, :], PS[b][:, :], ACT.Identity, bias=biased(32 + j)))
        freed(b, x)
        act.wait(x)
        y = act.op(lambda e: e.activation(XB[:, :], LX[:, :], ACT.Identity, bias=vec("lcb", j), scale=vec("lcw", 24 + j)))
        for s in range(1, 4):
            dve.wait(x, y)
            y = dve.op(lambda e, s=s: e.scalar_tensor_tensor(XB[:, s:T], LX[:, 0:T - s], vec("lcw", 8 * (3 - s) + j),
                                                             XB[:, s:T], ALU.mult, ALU.add))
        pe.wait(y, gw)
        g = []
        for i, dst in ((0, GR), (1, GI)):
            b = bank("side")
            t = mm(PS[b][:, :], GW[:, j % 2, i * P:(i + 1) * P], XB[:, :], True, True, last=True)
            act.wait(t)
            g.append(act.op(lambda e, b=b, i=i, dst=dst: e.activation(dst[:, :], PS[b][:, :], ACT.Sigmoid, bias=vec("lgb", 8 * i + j))))
            freed(b, g[-1])
        gw_used = t
        act.wait(*g)
        th = act.op(lambda e: e.activation(GT[:, :], GR[:, :], ACT.Tanh, scale=C8[:, j:j + 1]))
        a = act.op(lambda e: e.activation(GA[:, :], GR[:, :], ACT.Exp, scale=C8[:, j:j + 1]))
        dve.wait(th, *g)
        th = dve.op(lambda e: e.tensor_scalar(GT[:, :], GT[:, :], -2.0 * TINY, None, ALU.min))
        u = dve.op(lambda e: e.tensor_tensor(GI[:, :], GI[:, :], XB[:, :], ALU.mult))
        act.wait(th)
        l1 = act.op(lambda e: e.activation(GM[:, :], GT[:, :], ACT.Ln, scale=-2.0))
        l2 = act.op(lambda e: e.activation(GT[:, :], GT[:, :], ACT.Ln, bias=vec("one"), scale=-1.0))
        dve.wait(l1, l2)
        d = dve.op(lambda e: e.tensor_tensor(GM[:, :], GM[:, :], GT[:, :], ALU.subtract))
        act.wait(d)
        mu = act.op(lambda e: e.activation(GM[:, :], GM[:, :], ACT.Exp, scale=0.5))
        dve.wait(mu, u)
        u = dve.op(lambda e: e.tensor_tensor(GI[:, :], GI[:, :], GM[:, :], ALU.mult))
        dve.wait(u, a)
        h = dve.op(lambda e: e.tensor_tensor_scan(GR[:, :], GA[:, :], GI[:, :], 0.0, ALU.mult, ALU.add))
        b, t = product(m, 0, 5120 + j * P, HHI, HLO, ready)
        act.wait(t)
        ge = act.op(lambda e: e.activation(GG[:, :], PS[b][:, :], ACT.Gelu_apprx_tanh, bias=biased(40 + j)))
        freed(b, ge)
        dve.wait(h, ge)
        y = dve.op(lambda e: e.tensor_tensor(GG[:, :], GG[:, :], GR[:, :], ALU.mult))
        return split(YHI[:, j, :], YLO[:, j, :], GG[:, :], (y,), free), gw_used

    def over_channels(src, ready):
        b = bank("side")
        for j in range(DT):
            pe.wait(*ready[j])
            t = mm(PS[b][:, :], ONES, src(j), j == 0, j == DT - 1, last=True)
        return b, t

    def block2():
        ffn(at["nf1"], "ffn1_w_in_2", "ffn1_w_in_2", "ffn1_w_out_2", 0, 2816, 0.5)
        for g in (dve, act, pool, pe, sp):
            g.wait(*everything())
        m = "w_in_mix_2"
        hb = load(HB[:, :], hbias, s_hb, 16)
        small_vectors()
        pool.op(lambda e: e.memset(RSET[:, :], 1.0))
        pool.wait(pool.now())
        pool.op(lambda e: e.memset(RSET[:, :].rearrange("p (c t) -> p c t", c=CH)[:, :, 0:1], 0.0))
        pool.op(lambda e: e.memset(KT[:, :, :], 0.0))
        pool.op(lambda e: e.memset(QT[:, :, :], 0.0))
        lt = [pool.now()]
        for g in (dve, act):
            g.wait(*lt)
        ready = norm_split(at["nmix2"])
        v_ready = []
        for g_ in range(2):
            for c, (b, t) in enumerate(product_tokens(m, 0, 2048 + 512 * g_, ready)):
                dve.wait(t, hb)
                v_ready.append(dve.op(lambda e, c=c, b=b, g_=g_: e.tensor_tensor(
                    VH[:, c, 512 * g_:512 * g_ + 512], PS[b][:, :], HB[:, 512 * g_:512 * g_ + 512], ALU.add)))
                freed(b, v_ready[-1])
        act.wait(*v_ready)
        parts = [recurrence(j, ready, v_ready, lt) for j in range(8)]
        for g in (dve, act, pool):
            g.wait(*everything())
        cu = [conv_in(j, ready) for j in range(8)]
        done = {}

        def all_taps():
            for j in range(8):
                yield from conv_taps(j, cu[j], done)

        taps = all_taps()
        branch(0, ready, parts, taps, True)
        free = [pe.now()]
        parts = []
        gw_used = [(), ()]
        for j in range(8):
            sp.wait(*everything() if j == 0 else [], *gw_used[j % 2])
            gw = load(GW[:, j % 2, :], gates[j, :, :], s_gw[j % 2], 16 * (j // 2 + 1))
            p, u = lru(j, ready, gw, free)
            gw_used[j % 2] = (u,)
            parts.append(p)
            for _ in range(3):
                next(taps, None)
        branch(1, ready, parts, taps, False)
        free = [pe.now()]
        for _ in taps:
            pass
        for g in (dve, act):
            g.wait(*everything())
        sgs = []

        def gate(j):
            b, t = product(m, 0, 8192 + 2 * D + j * P, HHI, HLO, ready)
            act.wait(t, *everything()[1:2])
            sgs.append(act.op(lambda e: e.activation(GHT[:, j, :], PS[b][:, :], ACT.Sigmoid, bias=biased(80 + j))))
            freed(b, sgs[-1])

        b, t = over_channels(lambda j: CU[:, j, :], [(done[j],) for j in range(8)])
        act.wait(t)
        mu = act.op(lambda e: e.activation(LX[:, :], PS[b][:, :], ACT.Copy, scale=1.0 / D))
        freed(b, mu)
        cen, sq, used = [], [], []
        bv = bank("side")
        for j in range(8):
            dve.wait(mu, done[j])
            cen.append(dve.op(lambda e, j=j: e.tensor_tensor(CU[:, j, :], CU[:, j, :], LX[:, :], ALU.subtract)))
            act.wait(cen[j], *(used[j - 2:j - 1]))
            sq = act.op(lambda e, j=j: e.activation(SQ[:, j % 2, :], CU[:, j, :], ACT.Square))
            pe.wait(sq)
            used.append(mm(PS[bv][:, :], ONES, SQ[:, j % 2, :], j == 0, j == 7, last=True))
        r = inverse_root(RS[:, :], PS[bv][:, :], D, vec("eps5"), used[-1])
        freed(bv, r)
        for j in range(8):
            gate(j)
        parts = []
        act.wait(*free)
        for j in range(8):
            dve.wait(r, cen[j])
            y = dve.op(lambda e, j=j: e.tensor_tensor(CU[:, j, :], CU[:, j, :], RS[:, :], ALU.mult))
            act.wait(y)
            y = act.op(lambda e, j=j: e.activation(CU[:, j, :], CU[:, j, :], ACT.Silu, bias=vec("cvn", j), scale=vec("cvg", j)))
            parts.append(split(YHI[:, j, :], YLO[:, j, :], CU[:, j, :], (y,), free))
        for j in range(8):
            b, t = product("w_branch_2", 2, j * P, YHI, YLO, parts)
            merge(j, b, t, sgs[j], GHT[:, j, :], False)
        free = [pe.now()]
        parts = [split(YHI[:, j, :], YLO[:, j, :], MG[:, j, :], mg[j], free) for j in range(8)]
        for j in range(8):
            b, t = product("w_out_mix_2", 0, j * P, YHI, YLO, parts)
            add_to_x(j, b, t)
        for g in (dve, act, pool, pe):
            g.wait(*everything())
        ffn(at["nf2"], "ffn2_w_in_2", "ffn2_w_in_2", "ffn2_w_out_2", 0, 2816, 0.5)

    for l in range(2):
        block1(l)
    norm_x(at["fnorm"])
    block2()
    norm_x(at["nfin"])
    assert state["next"] == len(slots)
    for j in range(DT):
        sp.wait(*x_ready[j])
        load(out[:, j * T:(j + 1) * T], X[:, j, :], s_out, 0)
    sp.wait((s_out, 16 * DT))

    with nc.Block() as block:
        def run(g):
            def body(e):
                for make in g.queue:
                    make(e)
            return body

        block.sync(run(sp))
        block.tensor(run(pe))
        block.vector(run(dve))
        block.scalar(run(act))
        block.gpsimd(run(pool))


def shape_constants():
    i = np.arange(P)
    j, t = i[:, None], i[None, :]
    consts = np.stack([j == t, np.ones((P, P), bool), j // 64 == t // 64, j <= t, j >= t, j > t, j < t], 1)
    masks = [(j // (2 * h) == t // (2 * h)) & (j % (2 * h) < h) & (t % (2 * h) >= h) for h in LEVELS] + [j == t]
    masks = np.stack(masks, 1).astype(np.float32)
    half = 16
    inv = np.float32(10000.0) ** (-(np.float32(2.0) * np.arange(half, dtype=np.float32)) / np.float32(32))
    row = (np.arange(T) // 64).astype(np.float32)
    col = (np.arange(T) % 64).astype(np.float32)
    d = i % 64
    ang = np.where((d < 32)[:, None], row[None, :] * inv[d % 16][:, None], col[None, :] * inv[d % 16][:, None])
    ang = ang.astype(np.float32)
    turned = np.zeros((P, P), np.float32)
    for m in range(P):
        if m % 32 < 16:
            turned[m + 16, m] = -1.0
        else:
            turned[m - 16, m] = 1.0
    mats = [turned]
    for src in (np.eye(P, dtype=np.float32), turned):
        for g in range(2):
            mats.append(np.concatenate([src[:, 64 * g:64 * g + 64]] * 2, 1))
    rope = np.concatenate(mats + [np.cos(ang), np.sin(ang)], 1).astype(np.float32)
    return consts.astype(np.float32), masks, rope


def kernel(**inputs):
    import concourse.bacc as _bacc
    from concourse import mybir as _mybir
    from concourse.bass_utils import run_bass_kernel_spmd as _run

    a = {k: np.asarray(v) for k, v in inputs.items()}
    pieces = []
    for name, i, r0, nr, c0, ncol in plan():
        w = a[name]
        w = w[0, i] if name == "w_branch_2" else w[i]
        w = w[r0 * P:(r0 + nr) * P, c0:c0 + ncol]
        pieces.append(w.reshape(nr, P, ncol).transpose(1, 0, 2).reshape(-1))
    stream = np.concatenate(pieces)

    at, nvec = columns()
    vecs = np.zeros((P, nvec), np.float32)

    def put(key, v):
        v = v.reshape(-1, P).T
        vecs[:, at[key]:at[key] + v.shape[1]] = v

    def rows(key, v):
        v = v.reshape(1, -1)
        vecs[:, at[key]:at[key] + v.shape[1]] = np.broadcast_to(v, (P, v.shape[1]))

    for l in range(2):
        put(("nmix", l), a["norm_mix_w"][l])
        put(("qn", l), np.concatenate([a["q_norm_w"][l]] * 2))
        put(("kn", l), np.concatenate([a["k_norm_w"][l]] * 2))
        put(("cw", l), a["conv_w"][l])
        put(("cb", l), a["conv_b"][l])
        put(("sn", l), a["ssd_norm_w"][l])
        put(("nffn", l), a["norm_ffn_w"][l])
        rows(("dtb", l), a["dt_bias"][l])
        rows(("alog", l), a["a_log"][l])
        rows(("dsk", l), a["d_skip"][l])
    for key, name in (("fnorm", "final_norm_w"), ("nf1", "norm_ffn1_2"), ("nmix2", "norm_mix_2"), ("bin", "b_in_mix_2"),
                      ("lb", "hgrn_lb_logits_2"), ("hgn", "hg_norm_2"), ("lcw", "lru_conv_w_2"), ("lcb", "lru_conv_b_2"),
                      ("lgb", "lru_gate_b_2"), ("lam", "lru_lambda_2"), ("cvw", "cv_dw_w_2"), ("cvb", "cv_dw_b_2"),
                      ("cvg", "cv_ln_g_2"), ("cvn", "cv_ln_b_2"), ("nf2", "norm_ffn2_2"), ("nfin", "norm_final_2")):
        put(key, a[name])
    for key, value in (("eps", 1e-6), ("eps5", 1e-5), ("one", 1.0)):
        vecs[:, at[key]] = value
    xin = np.ascontiguousarray(a["x"][0].T.reshape(DT, P, T).transpose(1, 0, 2))
    hbias = np.ascontiguousarray(np.broadcast_to(a["b_in_mix_2"][0, 2048:3072][None, :], (P, D)))
    gates = np.ascontiguousarray(a["lru_gate_w_2"][0].transpose(1, 2, 0, 3).reshape(8, P, 256))
    consts, masks, rope = shape_constants()

    nc = _bacc.Bacc("TRN2", target_bir_lowering=False, num_devices=1)
    arrays, args = {}, []
    for name, v in (("stream", stream), ("xin", xin), ("vecs", vecs), ("consts", consts), ("masks", masks),
                    ("rope", rope), ("hbias", hbias), ("gates", gates)):
        arrays[f"in_{name}"] = v
        args.append(nc.dram_tensor(f"in_{name}", v.shape, _mybir.dt.from_np(v.dtype), kind="ExternalInput").ap())
    out = nc.dram_tensor("out_0", (P, DT * T), _mybir.dt.float32, kind="ExternalOutput").ap()
    build(nc, *args, out)
    r = _run(nc, [arrays], core_ids=[0])
    got = r.results[0]["out_0"].reshape(P, DT, T).transpose(1, 0, 2).reshape(D, T).T
    return np.ascontiguousarray(got).reshape(1, T, D)
```

```python
import numpy as np
import concourse.bass as bass
from concourse import mybir

F32 = mybir.dt.float32
F32R = mybir.dt.float32r
U8 = mybir.dt.uint8
ALU = mybir.AluOpType
ACT = mybir.ActivationFunctionType
AX = mybir.AxisListType.X

P = 128
T = 512
D = 1024
DT = 8
FT = 22
NH = 8
CH = 4
RAW = 4
SPL = 4
LOOK = 3
SLOT = 1024
LEVELS = (64, 32, 16, 8, 4, 2, 1)
TAPS = 31
TINY = 2.0 ** -63


def plan():
    s = []

    def fm(name, i, c0, rows=((0, DT),)):
        for r0, nr in rows:
            s.append((name, i, r0, nr, c0, P))

    def tm(name, i, c0):
        for r0 in range(0, DT, 2):
            s.append((name, i, r0, 2, c0, 512))

    down = ((0, 8), (8, 8), (16, 6))
    for l in range(2):
        for j in (4, 0, 1, 2, 3):
            fm("w_in", l, j * P)
        fm("w_in", l, 640)
        fm("w_in", l, 2192)
        tm("w_in", l, 768)
        for j in range(8):
            fm("w_in", l, 1280 + j * P)
        for j in range(DT):
            fm("w_out", l, j * P)
        for j in range(FT):
            fm("w_gate", l, j * P)
            fm("w_up", l, j * P)
        for j in range(DT):
            fm("w_down", l, j * P, down)

    def ffn(a, b):
        for j in range(FT):
            fm(a, 0, j * P)
            fm(a, 0, 2816 + j * P)
        for j in range(DT):
            fm(b, 0, j * P, down)

    ffn("ffn1_w_in_2", "ffn1_w_out_2")
    m = "w_in_mix_2"
    tm(m, 0, 2048)
    tm(m, 0, 2560)
    for j in range(8):
        for c in (6144, 7168, 1024, 0, 3072):
            fm(m, 0, c + j * P)
    for j in range(8):
        fm(m, 0, 4096 + j * P)
        fm(m, 0, 5120 + j * P)
        fm(m, 0, 8192 + j * P)
        fm("w_branch_2", 0, j * P)

    def branch(x):
        for j in range(8):
            fm(m, 0, 8192 + x * D + j * P)
            fm("w_branch_2", x, j * P)

    branch(1)
    for j in range(8):
        fm(m, 0, 8192 + 2 * D + j * P)
    for j in range(8):
        fm("w_branch_2", 2, j * P)
    for j in range(8):
        fm("w_out_mix_2", 0, j * P)
    ffn("ffn2_w_in_2", "ffn2_w_out_2")
    return s


def columns():
    at, n = {}, 0
    for l in range(2):
        for name, k in (("nmix", 8), ("qn", 1), ("kn", 1), ("cw", 40), ("cb", 8), ("sn", 4), ("nffn", 8),
                        ("dtb", 16), ("alog", 16), ("dsk", 8)):
            at[name, l] = n
            n += k
    for name, k in (("fnorm", 8), ("nf1", 8), ("nmix2", 8), ("bin", 88), ("lb", 8), ("hgn", 1), ("lcw", 32),
                    ("lcb", 8), ("lgb", 16), ("lam", 8), ("cvw", 8 * TAPS), ("cvb", 8), ("cvg", 8), ("cvn", 8),
                    ("nf2", 8), ("nfin", 8), ("eps", 1), ("eps5", 1), ("one", 1)):
        at[name] = n
        n += k
    return at, n


class Record:

    def copy(self, *a, **k):
        return lambda e: e.copy(*a, **k)

    def activation(self, *a, **k):
        return lambda e: e.activation(*a, **k)

    def tensor_tensor(self, *a, **k):
        return lambda e: e.tensor_tensor(*a, **k)

    def tensor_scalar(self, *a, **k):
        return lambda e: e.tensor_scalar(*a, **k)

    def scalar_tensor_tensor(self, *a, **k):
        return lambda e: e.scalar_tensor_tensor(*a, **k)

    def tensor_tensor_scan(self, *a, **k):
        return lambda e: e.tensor_tensor_scan(*a, **k)

    def tensor_reduce(self, *a, **k):
        return lambda e: e.tensor_reduce(*a, **k)

    def tensor_copy(self, *a, **k):
        return lambda e: e.tensor_copy(*a, **k)

    def reciprocal(self, *a, **k):
        return lambda e: e.reciprocal(*a, **k)

    def copy_predicated(self, *a, **k):
        return lambda e: e.copy_predicated(*a, **k)

    def memset(self, *a, **k):
        return lambda e: e.memset(*a, **k)

    def matmul(self, *a, **k):
        return lambda e: e.matmul(*a, **k)

    def transpose(self, *a, **k):
        return lambda e: e.transpose(*a, **k)


class Engine:

    def __init__(self, sem):
        self.sem, self.n, self.queue, self.seen = sem, 0, [], {}

    def wait(self, *tokens):
        for sem, value in tokens:
            if self.seen.get(id(sem), 0) < value:
                self.seen[id(sem)] = value
                self.queue.append(lambda e, s=sem, v=value: e.wait_ge(s, v))

    def op(self, make):
        self.n += 1
        instruction = make(Record())
        self.queue.append(lambda e: instruction(e).then_inc(self.sem, 1))
        return (self.sem, self.n)

    def quiet(self, make):
        self.queue.append(make(Record()))

    def now(self):
        return (self.sem, self.n)


def build(nc, xkeep, stream, xin, vecs, consts, masks, rope, hbias, gates, out):
    slots = plan()
    at, nvec = columns()
    base = nc.sbuf_base + (-nc.sbuf_base) % 64
    K = 1024

    def sb(name, kib, shape, dt=F32):
        return nc.alloc_sbuf_tensor_at(name, [P] + shape, dt, offset=base + int(kib * K))

    X = sb("X", 0, [DT, T])
    WR = sb("WR", 16, [RAW, SLOT])
    WHI = sb("WHI", 32, [SPL, SLOT], F32R)
    WLO = sb("WLO", 48, [SPL, SLOT], F32R)
    CON = sb("CON", 64, [7, P])
    VEC = sb("VEC", 67.5, [nvec])
    MSK = sb("MSK", 71, [8, P], U8)
    MSF = sb("MSF", 74, [8, P])
    NEGB = sb("NEGB", 72, [8])
    OML = sb("OML", 72.0625, [8])
    LBV = sb("LBV", 72.125, [8])
    C8 = sb("C8", 72.1875, [8])
    SMT = sb("SMT", 72.25, [4, 8])
    QNS = sb("QNS", 72.5, [2])
    SQ = sb("SQ", 74, [2, T])
    HF = sb("HF", 78, [2, T])
    RS = sb("RS", 82, [T])
    HHI = sb("HHI", 84, [DT, T], F32R)
    HLO = sb("HLO", 100, [DT, T], F32R)
    YHI = sb("YHI", 116, [DT, T], F32R)
    YLO = sb("YLO", 132, [DT, T], F32R)
    FHI = sb("FHI", 116, [FT, T], F32R)
    FLO = sb("FLO", 160, [FT, T], F32R)
    RQ = sb("RQ", 0, [7, T])
    RT = sb("RT", 148, [5, P])
    COS = sb("COS", 150.5, [T])
    SIN = sb("SIN", 152.5, [T])
    Z = sb("Z", 156, [CH, T])
    XBC = sb("XBC", 164, [DT, T])
    Q = sb("Q", 180, [4, T])
    KD = sb("KD", 188, [2, T])
    V = sb("V", 192, [CH, P])
    PR = sb("PR", 194, [2, T])
    PT = sb("PT", 198, [2, CH, 256])
    NM = sb("NM", 206, [4])
    RSM = sb("RSM", 206.0625, [4])
    RIN = sb("RIN", 206.125, [4])
    DTR = sb("DTR", 206.25, [CH, 16])
    SGB = sb("SGB", 74, [4, T])
    RRS = sb("RRS", 82, [T])
    XST = sb("XST", 84, [CH, T])
    BT = sb("BT", 92, [CH, 256])
    STF = sb("STF", 96, [3, T])
    STB = sb("STB", 102, [3, T])
    RAF = sb("RAF", 108, [8, P])
    DEF = sb("DEF", 112, [8, P])
    RAB = sb("RAB", 0, [8, P])
    DEB = sb("DEB", 4, [8, P])
    YB = sb("YB", 8, [T])
    SD = sb("SD", 10, [7, CH, 16])
    EX = sb("EX", 12, [5, CH, 16])
    DTE = sb("DTE", 13.5, [CH, 16])
    SS = sb("SS", 14, [2, 8])
    WF = sb("WF", 148, [8, P])
    WB = sb("WB", 152, [8, P])
    XCF = sb("XCF", 74, [T])
    XCB = sb("XCB", 76, [T])
    XCD = sb("XCD", 78, [T])
    MF = sb("MF", 80, [2, P])
    MB = sb("MB", 81, [2, P])
    YA = sb("YA", 82, [T])
    FB = sb("FB", 0, [2, T])
    KB = sb("KB", 4, [2, T])
    QB = sb("QB", 8, [2, T])
    GB = sb("GB", 12, [2, T])
    YL = sb("YL", 0, [DT, T])
    GHT = sb("GHT", 148, [8, T])
    CVA = sb("CVA", 148, [2, T])
    SGA = sb("SGA", 152, [2, T])
    CB = sb("CB", 156, [T])
    SAC = sb("SAC", 158, [CH, P])
    HD = sb("HD", 160, [2, T])
    HB = sb("HB", 132, [D])
    CU = sb("CU", 164, [DT, T])
    VH = sb("VH", 180, [CH, D])
    MG = sb("MG", 180, [DT, T])
    QT = sb("QT", 196, [2, T])
    KT = sb("KT", 200, [2, T])
    SOF = sb("SOF", 204, [768])
    LX = sb("LX", 156, [2, T])
    GG = sb("GG", 160, [2, T])
    XB = sb("XB", 74, [T])
    GR = sb("GR", 76, [T])
    GI = sb("GI", 78, [T])
    GA = sb("GA", 80, [T])
    GT = sb("GT", 82, [T])
    GM = sb("GM", 196, [T])
    GW = sb("GW", 198, [2, 256])
    LMU = sb("LMU", 196, [T])
    PS = [nc.alloc_psum_tensor(f"PS{i}", [P, 512], F32) for i in range(8)]

    IDN, ONES, BONES, TRIF, TRIB, UP, LOW = (CON[:, i, :] for i in range(7))

    def vec(name, i=0, n=1):
        return VEC[:, at[name] + i:at[name] + i + n]

    sems = {}

    def sem(name):
        sems[name] = nc.alloc_semaphore(name)
        return sems[name]

    pe, dve, act, pool = (Engine(sem(n)) for n in ("s_pe", "s_dve", "s_act", "s_pool"))
    sp = Engine(None)
    engines = (pe, dve, act, pool)
    s_con, s_rope, s_hb, s_out = sem("s_con"), sem("s_rope"), sem("s_hb"), sem("s_out")
    s_spill = sem("s_spill")
    s_back = [sem(f"s_back{i}") for i in range(DT)]
    s_gw = [sem(f"s_gw{i}") for i in range(2)]
    s_w = [sem(f"s_w{i}") for i in range(RAW)]

    def load(dst, src, s, value, g=None):
        (g or sp).queue.append(lambda e: e.dma_start(dst, src).then_inc(s, 16))
        return (s, value)

    def everything():
        return [g.now() for g in engines]

    load(X[:, :, :], xin, s_con, 0)
    load(VEC[:, :], vecs, s_con, 0)
    load(CON[:, :, :], consts, s_con, 0)
    con = load(MSF[:, :, :], masks, s_con, 64)
    for g in engines:
        g.wait(con)
    mask_bytes = dve.op(lambda e: e.tensor_copy(MSK[:, :, :], MSF[:, :, :]))
    act.wait(mask_bytes)

    offset, o = [], 0
    for _, _, _, nr, _, ncol in slots:
        offset.append(o)
        o += P * nr * ncol
    state = {"load": 0, "split": 0, "next": 0}
    raw_free, split_free, split_done = {}, {}, {}

    def load_slot():
        i = state["load"]
        if i >= len(slots):
            return
        state["load"] += 1
        n = slots[i][3] * slots[i][5]
        if i >= RAW:
            sp.wait(*raw_free[i - RAW])
        src = stream[offset[i]:offset[i] + P * n].rearrange("(p n) -> p n", p=P)
        load(WR[:, i % RAW, 0:n], src, s_w[i % RAW], 0)

    def split_slot():
        i = state["split"]
        if i >= len(slots):
            return
        state["split"] += 1
        n = slots[i][3] * slots[i][5]
        raw, hi, lo = WR[:, i % RAW, 0:n], WHI[:, i % SPL, 0:n], WLO[:, i % SPL, 0:n]
        landed = (s_w[i % RAW], 16 * (i // RAW + 1))
        act.wait(landed)
        dve.wait(landed)
        if i >= SPL:
            act.wait(split_free[i - SPL])
            dve.wait(split_free[i - SPL])
        a = act.op(lambda e: e.copy(hi, raw))
        dve.wait(a)
        b = dve.op(lambda e: e.tensor_tensor(lo, raw, hi.bitcast(F32), ALU.subtract))
        raw_free[i] = (a, b)
        split_done[i] = (a, b)
        load_slot()

    for _ in range(RAW):
        load_slot()
    for _ in range(LOOK):
        split_slot()

    def take(name, i, r0, c0):
        k = state["next"]
        state["next"] += 1
        s = slots[k]
        assert s[:3] + (s[4],) == (name, i, r0, c0), (s, name, i, r0, c0)
        split_slot()
        pe.wait(*split_done[k])
        nr, ncol = s[3], s[5]
        n = nr * ncol
        hi = WHI[:, k % SPL, 0:n].rearrange("p (r c) -> p r c", r=nr)
        lo = WLO[:, k % SPL, 0:n].rearrange("p (r c) -> p r c", r=nr)
        return k, hi, lo

    bank_free = {i: [] for i in range(8)}
    turn = {"main": 0, "side": 0}

    def bank(kind="main"):
        b = turn[kind] % 4 + (0 if kind == "main" else 4)
        turn[kind] += 1
        pe.wait(*bank_free[b])
        return b

    def freed(b, *tokens):
        bank_free[b] = list(tokens)

    def mm(out_, lhsT, rhs, start, stop, last=False, **k):
        make = lambda e: e.matmul(out_, lhsT, rhs, start=start, stop=stop, **k)
        return pe.op(make) if last else pe.quiet(make)

    def transpose(out_, in_):
        return pe.op(lambda e: e.transpose(out_, in_, IDN))

    side_work, filler = [], []

    def pump(n=1):
        for _ in range(n):
            if not side_work:
                return
            if next(side_work[0], "end") == "end":
                side_work.pop(0)

    def fill(n=1):
        for _ in range(n):
            if filler and next(filler[0], "end") == "end":
                filler.pop(0)

    def finish():
        while side_work:
            pump()

    def product(name, i, c0, rhi, rlo, ready, rows=((0, DT),)):
        b = bank()
        for r0, nr in rows:
            k, hi, lo = take(name, i, r0, c0)
            for r in range(nr):
                pe.wait(*ready[r0 + r])
                first, final = r0 + r == 0, r0 + r == rows[-1][0] + rows[-1][1] - 1
                mm(PS[b][:, :], hi[:, r, :], rhi[:, r0 + r, :], first, False)
                mm(PS[b][:, :], hi[:, r, :], rlo[:, r0 + r, :], False, False)
                t = mm(PS[b][:, :], lo[:, r, :], rhi[:, r0 + r, :], False, final, last=r == nr - 1)
                if r % 2 and r < nr - 1:
                    pump()
            split_free[k] = t
            pump()
        return b, t

    def product_tokens(name, i, c0, ready):
        bs = [bank() for _ in range(CH)]
        ts = [None] * CH
        for r0 in range(0, DT, 2):
            k, hi, lo = take(name, i, r0, c0)
            for c in range(CH):
                for r in range(2):
                    pe.wait(*ready[r0 + r])
                    a, l = HHI[:, r0 + r, c * P:(c + 1) * P], HLO[:, r0 + r, c * P:(c + 1) * P]
                    first, final = r0 + r == 0, r0 + r == DT - 1
                    mm(PS[bs[c]][:, :], a, hi[:, r, :], first, False)
                    mm(PS[bs[c]][:, :], a, lo[:, r, :], False, False)
                    ts[c] = mm(PS[bs[c]][:, :], l, hi[:, r, :], False, final, last=r == 1)
                pump()
            split_free[k] = ts[CH - 1]
        return list(zip(bs, ts))

    x_ready = [[] for _ in range(DT)]
    rs_free = [[]]

    def inverse_root(dst, src, n, eps, *ready):
        act.wait(*ready)
        t = act.op(lambda e: e.activation(dst, src, ACT.Ln, bias=eps, scale=1.0 / n))
        act.wait(t)
        return act.op(lambda e: e.activation(dst, dst, ACT.Exp, scale=-0.5))

    def mean_square():
        b = bank("side")
        for j in range(DT):
            act.wait(*x_ready[j])
            if j >= 2:
                act.wait(used[j - 2])
            else:
                used = [] if j == 0 else used
            t = act.op(lambda e, j=j: e.activation(SQ[:, j % 2, :], X[:, j, :], ACT.Square))
            pe.wait(t)
            used.append(mm(PS[b][:, :], ONES, SQ[:, j % 2, :], j == 0, j == DT - 1, last=True))
        act.wait(*rs_free[0])
        t = inverse_root(RS[:, :], PS[b][:, :], D, vec("eps"), used[-1])
        freed(b, t)
        return t

    def split(hi, lo, src, ready, free=()):
        act.wait(*ready, *free)
        a = act.op(lambda e: e.copy(hi, src))
        dve.wait(a, *ready, *free)
        return a, dve.op(lambda e: e.tensor_tensor(lo, src, hi.bitcast(F32), ALU.subtract))

    def norm_split(w):
        for g in (act, dve):
            g.wait(*everything())
        rs = mean_square()
        ready, free = [], [(), ()]
        for j in range(DT):
            dve.wait(rs, *x_ready[j], *free[j % 2])
            t = dve.op(lambda e, j=j: e.scalar_tensor_tensor(HF[:, j % 2, :], X[:, j, :], VEC[:, w + j:w + j + 1],
                                                            RS[:, :], ALU.mult, ALU.mult))
            ready.append(split(HHI[:, j, :], HLO[:, j, :], HF[:, j % 2, :], (t,)))
            free[j % 2] = ready[-1]
        rs_free[0] = [t]
        return ready

    def norm_x(w):
        rs = mean_square()
        for j in range(DT):
            dve.wait(rs, *x_ready[j])
            x_ready[j] = [dve.op(lambda e, j=j: e.scalar_tensor_tensor(
                X[:, j, :], X[:, j, :], VEC[:, w + j:w + j + 1], RS[:, :], ALU.mult, ALU.mult))]
        rs_free[0] = [x_ready[-1][0]]

    spills = [0]

    def spill():
        spills[0] += 1
        for r in x_ready:
            pool.wait(*r)
        return load(xkeep, X[:, :, :].rearrange("p a b -> p (a b)"), s_spill, 16 * spills[0], pool)

    def restore(*users):
        pool.wait(*users)
        for j in range(DT):
            x_ready[j] = [load(X[:, j, :], xkeep[:, j * T:(j + 1) * T], s_back[j], 16 * spills[0], pool)]

    def add_to_x(j, b, t, scale=1.0):
        dve.wait(t, *x_ready[j])
        x_ready[j] = [dve.op(lambda e: e.scalar_tensor_tensor(X[:, j, :], PS[b][:, :], scale, X[:, j, :],
                                                              ALU.mult, ALU.add))]
        freed(b, x_ready[j][0])

    def ffn(w, gate, up, down, i, up0, scale):
        ready = norm_split(w)
        parts, sg_free, af_free = [], [(), ()], [(), ()]
        for j in range(FT):
            bg, tg = product(gate, i, j * P, HHI, HLO, ready)
            act.wait(tg, *sg_free[j % 2])
            s = act.op(lambda e: e.activation(SQ[:, j % 2, :], PS[bg][:, :], ACT.Silu))
            freed(bg, s)
            bu, tu = product(up, i, up0 + j * P, HHI, HLO, ready)
            dve.wait(s, tu, *af_free[j % 2])
            m = dve.op(lambda e: e.tensor_tensor(HF[:, j % 2, :], SQ[:, j % 2, :], PS[bu][:, :], ALU.mult))
            sg_free[j % 2] = (m,)
            freed(bu, m)
            parts.append(split(FHI[:, j, :], FLO[:, j, :], HF[:, j % 2, :], (m,)))
            af_free[j % 2] = parts[-1]
        for j in range(DT):
            b, t = product(down, i, j * P, FHI, FLO, parts, ((0, 8), (8, 8), (16, 6)))
            add_to_x(j, b, t, scale)

    def rotated(j, raw, copied, w, done):
        dve_last = done[-1:]
        act.wait(copied, *dve_last)
        s = act.op(lambda e: e.activation(SGB[:, 0, :], raw, ACT.Square))
        yield
        n = bank("side")
        pe.wait(s)
        t = mm(PS[n][:, :], BONES, SGB[:, 0, :], True, True, last=True)
        yield
        r = inverse_root(RRS[:, :], PS[n][:, :], 64, vec("eps"), t)
        freed(n, r)
        dve.wait(r)
        qn = dve.op(lambda e: e.scalar_tensor_tensor(raw, raw, w, RRS[:, :], ALU.mult, ALU.mult))
        yield
        for dst, plain, turned in ([(Q[:, j, :], None, 0)] if j < 4 else [(KD[:, 0, :], 1, 3), (KD[:, 1, :], 2, 4)]):
            pe.wait(qn)
            src, b1 = raw, None
            if plain is not None:
                b1 = bank("side")
                t1 = mm(PS[b1][:, :], RT[:, plain, :], raw, True, True, last=True)
                src = PS[b1][:, :]
            b2 = bank("side")
            t2 = mm(PS[b2][:, :], RT[:, turned, :], raw, True, True, last=True)
            yield
            dve.wait(qn, t2, *done[-1:])
            u = dve.op(lambda e: e.tensor_tensor(SGB[:, 2, :], src, COS[:, :], ALU.mult))
            if b1 is not None:
                freed(b1, u)
            v = dve.op(lambda e: e.tensor_tensor(SGB[:, 3, :], PS[b2][:, :], SIN[:, :], ALU.mult))
            freed(b2, v)
            dve.wait(u, v)
            done.append(dve.op(lambda e: e.tensor_tensor(dst, SGB[:, 2, :], SGB[:, 3, :], ALU.add)))
            yield

    def attention(qk, v_ready, parts):
        probs, pr_free, pt_free, pt_done, pv = {}, [(), ()], [(), ()], {}, {}
        steps = [(h, c) for h in range(NH) for c in range(CH)]

        def scores(i):
            h, c = steps[i]
            lo = 64 * (h % 2)
            b = bank("side")
            pe.wait(*qk)
            t = mm(PS[b][:, :], Q[lo:lo + 64, h // 2, c * P:(c + 1) * P], KD[lo:lo + 64, h // 4, :], True, True, last=True)
            k = i % 4
            dve.wait(t, *(probs[i - 4] if i >= 4 else ()))
            m = dve.op(lambda e: e.tensor_reduce(NM[:, k:k + 1], PS[b][:, :], AX, ALU.max, negate=True))
            act.wait(m, *pr_free[i % 2])
            x = act.op(lambda e: e.activation(PR[:, i % 2, :], PS[b][:, :], ACT.Exp, bias=NM[:, k:k + 1],
                                              accum_out=RSM[:, k:k + 1]))
            freed(b, x)
            dve.wait(x)
            r = dve.op(lambda e: e.reciprocal(RIN[:, k:k + 1], RSM[:, k:k + 1]))
            dve.wait(r)
            n = dve.op(lambda e: e.tensor_scalar(PR[:, i % 2, :], PR[:, i % 2, :], RIN[:, k:k + 1], None, ALU.mult))
            probs[i] = (n, x)

        def turn_probs(i):
            h, c = steps[i]
            half = i // 2
            b = bank("side")
            pe.wait(probs[i][0])
            for k in range(CH):
                t = transpose(PS[b][:, k * P:(k + 1) * P], PR[:, i % 2, k * P:(k + 1) * P])
            pr_free[i % 2] = (t,)
            g = act if i % 2 else dve
            g.wait(t, *pt_free[half % 2])
            dst = PT[:, half % 2, :, (c % 2) * P:(c % 2 + 1) * P]
            src = PS[b][:, :].rearrange("p (k q) -> p k q", k=CH)
            e_ = g.op((lambda e: e.copy(dst, src)) if g is act else (lambda e: e.tensor_copy(dst, src)))
            freed(b, e_)
            pt_done[i] = e_

        def values(half):
            h, q0 = half // 2, 256 * (half % 2)
            lo = 64 * (h % 2)
            b = bank("side")
            pe.wait(pt_done[2 * half], pt_done[2 * half + 1], *v_ready)
            for k in range(CH):
                t = mm(PS[b][lo:lo + 64, 0:256], V[:, k, 64 * (h // 4):64 * (h // 4) + 64], PT[:, half % 2, k, :],
                       k == 0, k == CH - 1, last=k == CH - 1)
            pt_free[half % 2] = (t,)
            a, l = split(YHI[lo:lo + 64, h // 2, q0:q0 + 256], YLO[lo:lo + 64, h // 2, q0:q0 + 256],
                         PS[b][lo:lo + 64, 0:256], (t,))
            freed(b, a, l)
            parts[h // 2] += [a, l]

        n = len(steps)
        for i in range(n + 3):
            if i < n:
                scores(i)
            if 1 <= i <= n:
                turn_probs(i - 1)
            if i >= 3 and i % 2 == 1:
                values((i - 3) // 2)
            yield

    def heads_by(x, n=8, w=64):
        return x.unsqueeze(2).to_broadcast([P, n, w])

    def block1(l):
        cols = lambda name, i=0, n=1: VEC[:, at[name, l] + i:at[name, l] + i + n]
        for g in (dve, act, pool, pe, sp):
            g.wait(*everything())
        load(RT[:, :, :], rope[:, 0:640].rearrange("p (a b) -> p a b", a=5), s_rope, 0)
        load(COS[:, :], rope[:, 640:1152], s_rope, 0)
        tables = [load(SIN[:, :], rope[:, 1152:1664], s_rope, 48 * (l + 1))]
        for g in (pe, dve):
            g.wait(*tables)
        kept = spill()
        ready = norm_split(at["nmix", l])
        dve.op(lambda e: e.tensor_scalar(QNS[:, 0:1], cols("qn"), 0.125, None, ALU.mult))
        dve.wait(dve.now())
        for g in (act, dve):
            g.wait(kept, *ready[-1], dve.now())
        done = []
        for n, j in enumerate((4, 0, 1, 2, 3)):
            b, t = product("w_in", l, j * P, HHI, HLO, ready)
            act.wait(t)
            a = act.op(lambda e: e.copy(RQ[:, n, :], PS[b][:, :]))
            freed(b, a)
            side_work.append(rotated(j, RQ[:, n, :], a, QNS[:, 0:1] if j < 4 else cols("kn"), done))
        v_ready = []
        to_tokens = []

        def tokens(n, copied, after):
            b = bank("side")
            pe.wait(copied)
            for c in range(CH):
                t = transpose(PS[b][:, c * P:(c + 1) * P], RQ[:, n, c * P:(c + 1) * P])
            yield
            after(b, t)
            yield

        def v_out(b, t):
            act.wait(t)
            v_ready.append(act.op(lambda e: e.copy(V[:, :, :].rearrange("p a b -> p (a b)"), PS[b][:, :])))
            freed(b, v_ready[-1])

        def dt_out(b, t):
            dve.wait(t)
            v_ready.append(dve.op(lambda e: e.tensor_tensor(
                DTR[:, :, :], PS[b][:, :].rearrange("p (c h) -> p c h", c=CH)[:, :, 112:128],
                cols("dtb", 0, 16).unsqueeze(1).to_broadcast([P, CH, 16]), ALU.add)))
            freed(b, v_ready[-1])

        for n, c0, after in ((5, 640, v_out), (6, 2192, dt_out)):
            b, t = product("w_in", l, c0, HHI, HLO, ready)
            act.wait(t)
            a = act.op(lambda e: e.copy(RQ[:, n, :], PS[b][:, :]))
            freed(b, a)
            side_work.insert(1, tokens(n, a, after))
        parts = [[] for _ in range(DT)]

        def attend():
            yield from attention(done[-1:], v_ready, parts)

        side_work.append(attend())
        z_done, x_done = [], []
        for c, (b, t) in enumerate(product_tokens("w_in", l, 768, ready)):
            act.wait(t)
            z_done.append(act.op(lambda e: e.copy(Z[:, c, :], PS[b][:, :])))
            freed(b, z_done[-1])
        for j in range(8):
            b, t = product("w_in", l, 1280 + j * P, HHI, HLO, ready)
            act.wait(t)
            w = lambda k: cols("cw", 8 * k + j)
            y = act.op(lambda e: e.activation(XBC[:, j, :], PS[b][:, :], ACT.Identity, bias=cols("cb", j), scale=w(2)))
            for k, s in ((0, -2), (1, -1), (3, 1), (4, 2)):
                o0, o1 = max(0, -s), T - max(0, s)
                dve.wait(y)
                y = dve.op(lambda e: e.scalar_tensor_tensor(
                    XBC[:, j, o0:o1], PS[b][:, o0 + s:o1 + s], w(k), XBC[:, j, o0:o1], ALU.mult, ALU.add))
            freed(b, y)
            x_done.append(y)
        while len(side_work) > 1:
            pump()
        other = ssd(cols, z_done + x_done, parts)
        going = True
        while going or side_work:
            for _ in range(2):
                going = going and next(other, "end") != "end"
            pump()
        restore(*everything())
        for j in range(DT):
            b, t = product("w_out", l, j * P, YHI, YLO, parts)
            add_to_x(j, b, t)
        for g in (dve, act, pool, pe):
            g.wait(*everything())
        ffn(at["nffn", l], "w_gate", "w_up", "w_down", l, 0, 1.0)

    def ssd(cols, inputs, parts):
        start = everything()
        for g in (dve, act):
            g.wait(*start)
        done = []
        for src in (Z[:, :, :], XBC[:, 0:4, :], XBC[:, 4:8, :]):
            act.wait(*inputs, *done)
            s = act.op(lambda e: e.activation(SGB[:, :, :], src, ACT.Sigmoid))
            yield
            dve.wait(s)
            done = [dve.op(lambda e: e.tensor_tensor(src, src, SGB[:, :, :], ALU.mult))]
        silu = done
        yield
        sd = lambda i: SD[:, i, :, :]

        def chain(g, make, *also):
            g.wait(*also)
            t = g.op(make)
            for o_ in (dve, act):
                o_.wait(t)
            return t

        x0 = DTR[:, :, :]
        chain(dve, lambda e: e.tensor_scalar(sd(0), x0, -1.0, None, ALU.mult))
        chain(dve, lambda e: e.tensor_tensor(sd(0), sd(0), x0, ALU.max))
        chain(act, lambda e: e.activation(sd(1), sd(0), ACT.Exp, scale=-1.0))
        chain(dve, lambda e: e.tensor_scalar(sd(2), sd(1), 1.0, None, ALU.add))
        chain(act, lambda e: e.activation(sd(3), sd(2), ACT.Ln))
        yield
        chain(dve, lambda e: e.tensor_scalar(sd(2), sd(2), -1.0, None, ALU.add))
        chain(dve, lambda e: e.tensor_tensor(sd(2), sd(1), sd(2), ALU.subtract))
        chain(dve, lambda e: e.tensor_tensor(sd(3), sd(3), sd(2), ALU.add))
        chain(dve, lambda e: e.tensor_scalar(sd(0), x0, 0.0, None, ALU.max))
        chain(dve, lambda e: e.tensor_tensor(sd(4), sd(0), sd(3), ALU.add))
        step_ = sd(4)
        chain(act, lambda e: e.activation(SD[:, 5, 0, :], cols("alog", 0, 16), ACT.Exp))
        chain(dve, lambda e: e.tensor_scalar(SD[:, 5, 0, :], SD[:, 5, 0, :], -1.0, None, ALU.mult))
        da = chain(dve, lambda e: e.tensor_tensor(
            sd(6), step_, SD[:, 5, 0, :].unsqueeze(1).to_broadcast([P, CH, 16]), ALU.mult))
        yield
        b = bank()
        pe.wait(da)
        dA = sd(6).rearrange("p a b -> p (a b)")
        for i, m in enumerate((UP, LOW, TRIF, TRIB, ONES)):
            t = mm(PS[b][:, i * 64:(i + 1) * 64], m, dA, True, True, last=True)
        yield
        ex = chain(act, lambda e: e.activation(EX[:, :, :, :].rearrange("p a b c -> p (a b c)"), PS[b][:, 0:320], ACT.Exp), t)
        freed(b, ex)
        for d in range(2):
            dte = chain(dve, lambda e: e.tensor_tensor(
                DTE[:, :, 8 * d:8 * d + 8], step_[:, :, 8 * d:8 * d + 8], EX[:, d, :, 8 * d:8 * d + 8], ALU.mult))
        pe.wait(*silu)
        for c in range(CH):
            b = bank()
            for i in range(4):
                t = transpose(PS[b][:, i * P:(i + 1) * P], XBC[:, i, c * P:(c + 1) * P])
            b2 = bank()
            for i in range(2):
                t = transpose(PS[b2][:, i * P:(i + 1) * P], XBC[:, 4 + i, c * P:(c + 1) * P])
            yield
            act.wait(t)
            a = act.op(lambda e: e.copy(XST[:, c, :], PS[b][:, :]))
            freed(b, a)
            tok = act.op(lambda e: e.copy(BT[:, c, :], PS[b2][:, 0:256]))
            freed(b2, tok)
        by_head = lambda x: x.rearrange("p (h d) -> p h d", h=8)
        st, prev, xcd = {}, [None, None], [(), ()]
        XD = (XCD, XCF)
        for n in range(3):
            banks = []
            for d, c in ((0, n), (1, 3 - n)):
                dve.wait(tok, dte, *xcd[d])
                x = dve.op(lambda e: e.tensor_tensor(
                    by_head(XD[d][:, :]), by_head(XST[:, c, :]), heads_by(DTE[:, c, 8 * d:8 * d + 8]), ALU.mult))
                banks.append((d, c, x))
            yield
            got = []
            for d, c, x in banks:
                b = bank()
                pe.wait(x, tok)
                for g in range(2):
                    t = mm(PS[b][:, 256 * g:256 * g + 256], BT[:, c, g * P:(g + 1) * P], XD[d][:, 256 * g:256 * g + 256],
                           True, True, last=True)
                xcd[d] = (t,)
                got.append((d, c, b, t))
            yield
            for d, c, b, t in got:
                S = (STF, STB)[d]
                dve.wait(t)
                if n == 0:
                    s = dve.op(lambda e: e.tensor_copy(S[:, 0, :], PS[b][:, :]))
                else:
                    dve.wait(prev[d])
                    s = dve.op(lambda e: e.tensor_tensor(
                        by_head(S[:, n, :]), by_head(S[:, n - 1, :]), heads_by(EX[:, 4, c, 8 * d:8 * d + 8]), ALU.mult))
                    dve.wait(s)
                    s = dve.op(lambda e: e.tensor_tensor(S[:, n, :], S[:, n, :], PS[b][:, :], ALU.add))
                freed(b, s)
                prev[d] = s
                st[d, c + 1 if d == 0 else c - 1] = (S, n, s)
        ways = ((0, TRIF, UP, MF, RAF, DEF, WF, XCF), (1, TRIB, LOW, MB, RAB, DEB, WB, XCB))
        ra_read, w_read, ws, sq, y_out = [(), ()], list(xcd[1]), [], (), []
        for c in range(CH):
            bs = bank()
            for g in range(2):
                ts = mm(PS[bs][:, g * P:(g + 1) * P], XBC[:, 4 + g, c * P:(c + 1) * P], XBC[:, 6 + g, c * P:(c + 1) * P],
                        True, True, last=True)
            ras = []
            for d, tri, side_, M, RA, DEC, W, XC in ways:
                dve.wait(*ra_read[d])
                ras.append(dve.op(lambda e: e.tensor_tensor(
                    RA[:, :, :], heads_by(sd(6)[:, c, 8 * d:8 * d + 8], 8, P),
                    tri.unsqueeze(1).to_broadcast([P, 8, P]), ALU.mult)))
            yield
            sc = PS[bs][:, 0:256].rearrange("p (g t) -> p g t", g=2)
            both = []
            dve.wait(ts, *ws, *w_read)
            for d, tri, side_, M, RA, DEC, W, XC in ways:
                both.append(dve.op(lambda e: e.tensor_tensor(M[:, :, :], sc, tri.unsqueeze(1).to_broadcast([P, 2, P]), ALU.mult)))
            freed(bs, *both)
            xs_ = []
            for d, tri, side_, M, RA, DEC, W, XC in ways:
                xs_.append(dve.op(lambda e: e.tensor_tensor(
                    by_head(XC[:, :]), by_head(XST[:, c, :]), heads_by(step_[:, c, 8 * d:8 * d + 8]), ALU.mult)))
            decays = []
            for d, tri, side_, M, RA, DEC, W, XC in ways:
                pe.wait(ras[d])
                bd = []
                for g in range(2):
                    b = bank()
                    t = mm(PS[b][:, :], side_, RA[:, 4 * g:4 * g + 4, :].rearrange("p h t -> p (h t)"), True, True, last=True)
                    bd.append((b, t))
                ra_read[d] = (t,)
                yield
                for g, (b, t) in enumerate(bd):
                    act.wait(t, *ws)
                    a = act.op(lambda e: e.activation(
                        DEC[:, 4 * g:4 * g + 4, :].rearrange("p h t -> p (h t)"), PS[b][:, :], ACT.Exp))
                    freed(b, a)
                decays.append(a)
            yield
            ws = []
            for d, tri, side_, M, RA, DEC, W, XC in ways:
                dve.wait(decays[d], *both)
                for g in range(2):
                    ws.append(dve.op(lambda e: e.tensor_tensor(
                        W[:, 4 * g:4 * g + 4, :], DEC[:, 4 * g:4 * g + 4, :],
                        M[:, g, :].unsqueeze(1).to_broadcast([P, 4, P]), ALU.mult)))
            dve.wait(tok, *y_out)
            y = dve.op(lambda e: e.tensor_tensor(by_head(YA[:, :]), by_head(XST[:, c, :]), heads_by(cols("dsk", 0, 8)), ALU.mult))
            yield
            offs = []
            for d in range(2):
                if (d, c) not in st:
                    continue
                S, n, s = st[d, c]
                b = bank()
                pe.wait(s)
                for g in range(2):
                    t = mm(PS[b][:, 256 * g:256 * g + 256], XBC[:, 6 + g, c * P:(c + 1) * P], S[:, n, 256 * g:256 * g + 256],
                           True, True, last=True)
                offs.append((d, b, t))
            yb = bank()
            pe.wait(*ws, *xs_)
            for h in range(8):
                o_ = PS[yb][:, 64 * h:64 * h + 64]
                mm(o_, WF[:, h, :], XCF[:, 64 * h:64 * h + 64], True, False)
                td = mm(o_, WB[:, h, :], XCB[:, 64 * h:64 * h + 64], False, True, last=True)
            w_read = [td]
            yield
            for d, b, t in offs:
                dve.wait(t, y, *sq)
                u = dve.op(lambda e: e.tensor_tensor(
                    by_head(YB[:, :]), by_head(PS[b][:, :]), heads_by(EX[:, 2 + d, c, 8 * d:8 * d + 8]), ALU.mult))
                freed(b, u)
                dve.wait(u)
                y = dve.op(lambda e: e.tensor_tensor(YA[:, :], YA[:, :], YB[:, :], ALU.add))
            dve.wait(y, td)
            y = dve.op(lambda e: e.tensor_tensor(YA[:, :], YA[:, :], PS[yb][:, :], ALU.add))
            freed(yb, y)
            dve.wait(y)
            y = dve.op(lambda e: e.tensor_tensor(YA[:, :], YA[:, :], Z[:, c, :], ALU.mult))
            act.wait(y)
            yield
            for g in range(2):
                q = act.op(lambda e: e.activation(YB[:, 256 * g:256 * g + 256], YA[:, 256 * g:256 * g + 256], ACT.Square,
                                                  accum_out=SS[:, 0, 2 * c + g:2 * c + g + 1]))
            act.wait(q)
            sq = (q,)
            r = inverse_root(SS[:, 1, 2 * c:2 * c + 2], SS[:, 0, 2 * c:2 * c + 2], 256, vec("eps"))
            yield
            dve.wait(r, y)
            y_out = [dve.op(lambda e: e.tensor_scalar(
                Z[:, c, 256 * g:256 * g + 256], YA[:, 256 * g:256 * g + 256], SS[:, 1, 2 * c + g:2 * c + g + 1], None, ALU.mult))
                for g in range(2)]
        yield
        pe.wait(*y_out)
        for i in range(4):
            b = bank()
            for c in range(CH):
                t = transpose(PS[b][:, c * P:(c + 1) * P], Z[:, c, i * P:(i + 1) * P])
            act.wait(t)
            a = act.op(lambda e: e.activation(YHI[:, 4 + i, :], PS[b][:, :], ACT.Copy, scale=cols("sn", i)))
            dve.wait(a)
            d_ = dve.op(lambda e: e.scalar_tensor_tensor(YLO[:, 4 + i, :], PS[b][:, :], cols("sn", i),
                                                         YHI[:, 4 + i, :].bitcast(F32), ALU.mult, ALU.subtract))
            freed(b, d_)
            parts[4 + i] += [a, d_]
            yield

    def biased(i):
        return vec("bin", i)

    def gated(dst, b, t, bias, tmp, free=()):
        act.wait(t, *free)
        s = act.op(lambda e: e.activation(tmp, PS[b][:, :], ACT.Sigmoid, bias=bias))
        dve.wait(s, *free)
        y = dve.op(lambda e: e.scalar_tensor_tensor(dst, PS[b][:, :], bias, tmp, ALU.add, ALU.mult))
        freed(b, y)
        return y

    def small_vectors():
        s = lambda i: SMT[:, i, :]

        def go(g, make):
            t = g.op(make)
            for o_ in (dve, act):
                o_.wait(t)

        lg, lam = vec("lb", 0, 8), vec("lam", 0, 8)
        go(dve, lambda e: e.tensor_tensor(s(0), lg, lg, ALU.subtract))
        go(act, lambda e: e.activation(s(1), s(0), ACT.Exp))
        go(dve, lambda e: e.reciprocal(s(2), s(1)))
        go(dve, lambda e: e.tensor_tensor(s(3), s(1), s(2), ALU.mult))
        go(dve, lambda e: e.tensor_tensor(LBV[:, :], s(3), s(3), ALU.subtract))
        go(dve, lambda e: e.tensor_scalar(OML[:, :], LBV[:, :], -1.0, 1.0, ALU.mult, ALU.add))
        go(dve, lambda e: e.tensor_scalar(NEGB[:, :], vec("bin", 8, 8), -1.0, None, ALU.mult))
        go(dve, lambda e: e.tensor_scalar(s(0), lam, -1.0, None, ALU.mult))
        go(dve, lambda e: e.tensor_tensor(s(1), s(0), lam, ALU.max))
        go(act, lambda e: e.activation(s(1), s(1), ACT.Exp, scale=-1.0))
        go(dve, lambda e: e.tensor_scalar(s(2), s(1), 1.0, None, ALU.add))
        go(act, lambda e: e.activation(s(3), s(2), ACT.Ln))
        go(dve, lambda e: e.tensor_scalar(s(2), s(2), -1.0, None, ALU.add))
        go(dve, lambda e: e.tensor_tensor(s(2), s(1), s(2), ALU.subtract))
        go(dve, lambda e: e.tensor_tensor(s(3), s(3), s(2), ALU.add))
        go(dve, lambda e: e.tensor_scalar(s(0), s(0), 0.0, None, ALU.max))
        go(dve, lambda e: e.tensor_tensor(s(3), s(3), s(0), ALU.add))
        go(dve, lambda e: e.tensor_scalar(C8[:, :], s(3), -8.0, None, ALU.mult))

    def recurrence(j, inputs, v_ready, parts, seen):
        f, k, q, g = inputs
        LF, HK, HQ, HGS = (B[:, j % 2, :] for B in (FB, KB, QB, GB))
        last = seen[-1]
        dve.wait(f, k, *last)
        f = dve.op(lambda e: e.tensor_scalar(LF, LF, OML[:, j:j + 1], LBV[:, j:j + 1], ALU.mult, ALU.add))
        k = dve.op(lambda e: e.tensor_scalar(HK, HK, OML[:, j:j + 1], None, ALU.mult))
        dve.wait(f)
        f2 = dve.op(lambda e: e.tensor_scalar(HD[:, 0, :], LF, 1.0 / TINY, 1.0, ALU.mult, ALU.min))
        dve.wait(f2)
        f1 = dve.op(lambda e: e.tensor_scalar(LF, LF, TINY, None, ALU.max))
        yield
        act.wait(f1, f2)
        l2 = act.op(lambda e: e.activation(HD[:, 0, :], HD[:, 0, :], ACT.Ln))
        l1 = act.op(lambda e: e.activation(LF, LF, ACT.Ln))
        pool.wait(*last)
        sac = pool.op(lambda e: e.memset(SAC[:, :, :], 0.0))
        yield
        dve.wait(l1, l2)
        lf = dve.op(lambda e: e.tensor_tensor(LF, LF, HD[:, 0, :], ALU.add))
        dve.wait(lf)
        for c in range(CH):
            o = slice(c * P, (c + 1) * P)
            cb = dve.op(lambda e: e.tensor_tensor_scan(CB[:, o], ONES, LF[:, o], 0.0, ALU.mult, ALU.add))
        yield
        dve.wait(cb, q)
        pool.wait(k)
        nl = len(LEVELS)
        subs, exps, muls, prods = {}, {}, {}, {}
        for i in range(nl + 4):
            if i < nl:
                h = LEVELS[i]
                blk = lambda x: x.rearrange("p (n w) -> p n w", w=2 * h)
                nb = T // (2 * h)
                cbv, hd = blk(CB[:, :]), blk(HD[:, i % 2, :])
                if i >= 2:
                    dve.wait(*muls[i - 2])
                dd = dve.op(lambda e: e.tensor_tensor(hd, cbv, cbv[:, :, h - 1:h].to_broadcast([P, nb, 2 * h]), ALU.subtract))
                act.wait(dd)
                e1 = act.op(lambda e: e.activation(hd[:, :, h:2 * h], hd[:, :, h:2 * h], ACT.Exp))
                e2 = act.op(lambda e: e.activation(hd[:, :, 0:h], hd[:, :, 0:h], ACT.Exp, scale=-1.0))
                exps[i] = (e1, e2)
            n = i - 1
            if 0 <= n < nl:
                h = LEVELS[n]
                blk = lambda x: x.rearrange("p (n w) -> p n w", w=2 * h)
                hd = blk(HD[:, n % 2, :])
                qt, kt, qv, kv = blk(QT[:, n % 2, :]), blk(KT[:, n % 2, :]), blk(HQ), blk(HK)
                free = prods[n - 2][1:] if n >= 2 else ()
                dve.wait(exps[n][0], *free)
                pool.wait(exps[n][1], *free)
                a = dve.op(lambda e: e.tensor_tensor(qt[:, :, h:2 * h], qv[:, :, h:2 * h], hd[:, :, h:2 * h], ALU.mult))
                c_ = pool.op(lambda e: e.tensor_tensor(kt[:, :, 0:h], kv[:, :, 0:h], hd[:, :, 0:h], ALU.mult))
                muls[n] = (a, c_)
            n = i - 3
            if 0 <= n <= nl:
                b, t = prods[n]
                dve.wait(t, sac)
                sac = dve.op(lambda e: e.copy_predicated(
                    SAC[:, :, :], MSK[:, n, :].unsqueeze(1).to_broadcast([P, CH, P]),
                    PS[b][:, :].rearrange("p (c t) -> p c t", c=CH)))
                freed(b, sac)
            n = i - 2
            if 0 <= n <= nl:
                b = bank("side")
                if n < nl:
                    pe.wait(*muls[n])
                    lhs, rhs = KT[:, n % 2, :], QT[:, n % 2, :]
                else:
                    pe.wait(k, q)
                    lhs, rhs = HK, HQ
                for c in range(CH):
                    t = mm(PS[b][:, c * P:(c + 1) * P], lhs[:, c * P:(c + 1) * P], rhs[:, c * P:(c + 1) * P], True, True,
                           last=c == CH - 1)
                prods[n] = (b, t)
            yield
        act.wait(*muls[nl - 1], *muls[nl - 2], cb)
        E0 = HD[:, 0, :]
        eb = act.op(lambda e: e.activation(E0, CB[:, :], ACT.Exp))
        ends = [CB[:, c * P + P - 1:c * P + P] for c in range(CH)]
        whole = [E0[:, c * P + P - 1:c * P + P] for c in range(CH)]
        for c in range(3):
            o = slice(c * P, (c + 1) * P)
            ek = act.op(lambda e: e.activation(LF[:, o], CB[:, o], ACT.Exp, bias=ends[c], scale=-1.0))
        yield
        QX, KX = QT[:, 0, :], KT[:, 0, :]
        used = (prods[nl - 1][1], prods[nl][1])
        dve.wait(eb, ek, *used)
        pool.wait(ek, *used)
        a1 = dve.op(lambda e: e.tensor_tensor(QX[:, P:T], HQ[:, P:T], E0[:, P:T], ALU.mult))
        a2 = dve.op(lambda e: e.tensor_tensor(QX[:, 0:P], HQ[:, 3 * P:T], E0[:, 3 * P:T], ALU.mult))
        a4 = pool.op(lambda e: e.tensor_tensor(KX[:, 0:3 * P], HK[:, 0:3 * P], LF[:, 0:3 * P], ALU.mult))
        dve.wait(a1)
        a3 = dve.op(lambda e: e.tensor_scalar(QX[:, 3 * P:T], QX[:, 3 * P:T], whole[2], None, ALU.mult))
        yield
        dve.wait(a4)
        a5 = dve.op(lambda e: e.tensor_scalar(KX[:, 3 * P:T], KX[:, 0:P], whole[1], None, ALU.mult))
        yield
        pe.wait(a2, a3, a5)
        ba = bank("side")
        mm(PS[ba][:, 0:P], KX[:, 0:P], QX[:, P:2 * P], True, True)
        ta = mm(PS[ba][:, P:3 * P], KX[:, 3 * P:T], QX[:, 2 * P:T], True, True, last=True)
        bb = bank("side")
        mm(PS[bb][:, 0:2 * P], KX[:, P:2 * P], QX[:, 2 * P:T], True, True)
        tb = mm(PS[bb][:, 2 * P:3 * P], KX[:, 2 * P:3 * P], QX[:, 0:P], True, True, last=True)
        yield
        act.wait(ta, tb, *last)
        s1 = act.op(lambda e: e.copy(SOF[:, 0:384], PS[ba][:, 0:384]))
        s2 = act.op(lambda e: e.copy(SOF[:, 384:768], PS[bb][:, 0:384]))
        freed(ba, s1)
        freed(bb, s2)
        yield
        bo = bank("side")
        pe.wait(sac, s1, s2, *v_ready)
        v = [VH[:, c, j * P:(j + 1) * P] for c in range(CH)]
        o_ = PS[bo]
        kw = {"skip_group_check": True}
        mm(o_[:, P:T], v[0], SOF[:, 0:384], True, False, **kw)
        mm(o_[:, 0:P], v[0], SAC[:, 0, :], False, False, **kw)
        mm(o_[:, P:2 * P], v[1], SAC[:, 1, :], False, False, **kw)
        mm(o_[:, 2 * P:T], v[1], SOF[:, 384:640], False, False, **kw)
        mm(o_[:, 2 * P:3 * P], v[2], SAC[:, 2, :], False, False, **kw)
        mm(o_[:, 3 * P:T], v[2], SOF[:, 640:768], False, False, **kw)
        to = mm(o_[:, 3 * P:T], v[3], SAC[:, 3, :], False, True, last=True, **kw)
        yield
        act.wait(to)
        sq = act.op(lambda e: e.activation(SQ[:, 0, :], PS[bo][:, :], ACT.Square))
        yield
        bn = bank("side")
        pe.wait(sq)
        tn = mm(PS[bn][:, :], ONES, SQ[:, 0, :], True, True, last=True)
        yield
        r = inverse_root(RS[:, :], PS[bn][:, :], P, vec("eps"), tn)
        freed(bn, r)
        yield
        dve.wait(r, to, g)
        y = dve.op(lambda e: e.scalar_tensor_tensor(HF[:, 0, :], PS[bo][:, :], vec("hgn"), RS[:, :], ALU.mult, ALU.mult))
        freed(bo, y)
        dve.wait(y)
        y = dve.op(lambda e: e.tensor_tensor(HF[:, 0, :], HF[:, 0, :], HGS, ALU.mult))
        yield
        parts[j] = split(YHI[:, j, :], YLO[:, j, :], HF[:, 0, :], (y,))
        seen.append((a5, to, sac, *parts[j]))

    def conv_taps(j, ready, done):
        acc = CVA[:, j % 2, :]
        w = lambda k: vec("cvw", 8 * k + j)
        act.wait(ready, *([done[j - 2]] if j >= 2 else []))
        y = act.op(lambda e: e.activation(acc, CU[:, j, :], ACT.Identity, bias=vec("cvb", j), scale=w(TAPS - 1)))
        yield
        for s in range(1, TAPS):
            dve.wait(y)
            y = dve.op(lambda e: e.scalar_tensor_tensor(CVA[:, j % 2, s:T], CU[:, j, 0:T - s], w(TAPS - 1 - s),
                                                        CVA[:, j % 2, s:T], ALU.mult, ALU.add))
            if s % 3 == 0:
                yield
        act.wait(y)
        done[j] = act.op(lambda e: e.copy(CU[:, j, :], acc))
        yield

    sga_free = [(), ()]
    mg = {}

    def branch_gate(x, j, b, t):
        act.wait(t, *sga_free[j % 2])
        s = act.op(lambda e: e.activation(SGA[:, j % 2, :], PS[b][:, :], ACT.Sigmoid, bias=biased(64 + 8 * x + j)))
        freed(b, s)
        return s

    def merge(j, b, t, s, sg, first):
        dve.wait(s, t)
        if first:
            y = dve.op(lambda e: e.tensor_tensor(MG[:, j, :], sg, PS[b][:, :], ALU.mult))
            freed(b, y)
        else:
            y = dve.op(lambda e: e.tensor_tensor(sg, sg, PS[b][:, :], ALU.mult))
            freed(b, y)
            dve.wait(y, *mg[j])
            y = dve.op(lambda e: e.tensor_tensor(MG[:, j, :], MG[:, j, :], sg, ALU.add))
        mg[j] = (y,)

    def lru(j, x, gw, gw_used, gelu, out_, last):
        L = LX[:, j % 2, :]
        act.wait(x, *last)
        y = act.op(lambda e: e.activation(XB[:, :], L, ACT.Identity, bias=vec("lcb", j), scale=vec("lcw", 24 + j)))
        yield
        for s in range(1, 4):
            dve.wait(x, y)
            y = dve.op(lambda e: e.scalar_tensor_tensor(XB[:, s:T], L[:, 0:T - s], vec("lcw", 8 * (3 - s) + j),
                                                        XB[:, s:T], ALU.mult, ALU.add))
        yield
        pe.wait(y, gw)
        bt = []
        for i in range(2):
            b = bank("side")
            bt.append((b, mm(PS[b][:, :], GW[:, j % 2, i * P:(i + 1) * P], XB[:, :], True, True, last=True)))
        gw_used[j % 2] = (bt[1][1],)
        yield
        g = []
        for i, dst in ((0, GR), (1, GI)):
            b, t = bt[i]
            act.wait(t)
            g.append(act.op(lambda e: e.activation(dst[:, :], PS[b][:, :], ACT.Sigmoid, bias=vec("lgb", 8 * i + j))))
            freed(b, g[-1])
        act.wait(*g)
        th = act.op(lambda e: e.activation(GT[:, :], GR[:, :], ACT.Tanh, scale=C8[:, j:j + 1]))
        yield
        dve.wait(th, *g)
        th = dve.op(lambda e: e.tensor_scalar(GT[:, :], GT[:, :], -2.0 * TINY, None, ALU.min))
        u = dve.op(lambda e: e.tensor_tensor(GI[:, :], GI[:, :], XB[:, :], ALU.mult))
        a = act.op(lambda e: e.activation(GA[:, :], GR[:, :], ACT.Exp, scale=C8[:, j:j + 1]))
        act.wait(th)
        l1 = act.op(lambda e: e.activation(GM[:, :], GT[:, :], ACT.Ln, scale=-2.0))
        l2 = act.op(lambda e: e.activation(GT[:, :], GT[:, :], ACT.Ln, bias=vec("one"), scale=-1.0))
        yield
        dve.wait(l1, l2)
        d = dve.op(lambda e: e.tensor_tensor(GM[:, :], GM[:, :], GT[:, :], ALU.subtract))
        act.wait(d)
        mu = act.op(lambda e: e.activation(GM[:, :], GM[:, :], ACT.Exp, scale=0.5))
        yield
        dve.wait(mu, u)
        u = dve.op(lambda e: e.tensor_tensor(GI[:, :], GI[:, :], GM[:, :], ALU.mult))
        dve.wait(u, a)
        h = dve.op(lambda e: e.tensor_tensor_scan(GR[:, :], GA[:, :], GI[:, :], 0.0, ALU.mult, ALU.add))
        yield
        dve.wait(h, gelu[j])
        out_[j] = dve.op(lambda e: e.tensor_tensor(YL[:, j, :], GG[:, j % 2, :], GR[:, :], ALU.mult))

    def over_channels(src, ready):
        b = bank("side")
        for j in range(DT):
            pe.wait(*ready[j])
            t = mm(PS[b][:, :], ONES, src(j), j == 0, j == DT - 1, last=True)
        return b, t

    def block2():
        ffn(at["nf1"], "ffn1_w_in_2", "ffn1_w_in_2", "ffn1_w_out_2", 0, 2816, 0.5)
        for g in (dve, act, pool, pe, sp):
            g.wait(*everything())
        m = "w_in_mix_2"
        hb = load(HB[:, :], hbias, s_hb, 16)
        kept = spill()
        small_vectors()
        pool.op(lambda e: e.memset(KT[:, :, :], 0.0))
        lt = [pool.op(lambda e: e.memset(QT[:, :, :], 0.0))]
        for g in (dve, pe):
            g.wait(*lt)
        pool.wait(*lt)
        ready = norm_split(at["nmix2"])
        v_ready = []
        for g_ in range(2):
            for c, (b, t) in enumerate(product_tokens(m, 0, 2048 + 512 * g_, ready)):
                dve.wait(t, hb)
                v_ready.append(dve.op(lambda e: e.tensor_tensor(
                    VH[:, c, 512 * g_:512 * g_ + 512], PS[b][:, :], HB[:, 512 * g_:512 * g_ + 512], ALU.add)))
                freed(b, v_ready[-1])
        for g in (act, dve):
            g.wait(kept, *ready[-1], *v_ready)
        parts, seen, cu, done = [None] * 8, [()], [], {}

        def all_taps():
            for j in range(8):
                yield from conv_taps(j, cu[j], done)

        filler.append(all_taps())
        for j in range(8):
            p = j % 2
            ba, ta = product(m, 0, 6144 + j * P, HHI, HLO, ready)
            act.wait(ta)
            c = act.op(lambda e: e.activation(CU[:, j, :], PS[ba][:, :], ACT.Identity, bias=biased(48 + j)))
            freed(ba, c)
            bb, tb = product(m, 0, 7168 + j * P, HHI, HLO, ready)
            bf, tf = product(m, 0, 1024 + j * P, HHI, HLO, ready)
            bq, tq = product(m, 0, j * P, HHI, HLO, ready)
            bg, tg = product(m, 0, 3072 + j * P, HHI, HLO, ready)
            while len(side_work) > 1:
                pump()
            for e_ in (act, dve):
                e_.wait(*(seen[j - 1] if j >= 2 else ()))
            act.wait(tb, *([cu[j - 2]] if j >= 2 else []))
            s0 = act.op(lambda e: e.activation(SGA[:, p, :], PS[bb][:, :], ACT.Sigmoid, bias=biased(56 + j)))
            freed(bb, s0)
            act.wait(tf)
            f = act.op(lambda e: e.activation(FB[:, p, :], PS[bf][:, :], ACT.Sigmoid, bias=biased(8 + j)))
            k = act.op(lambda e: e.activation(KB[:, p, :], PS[bf][:, :], ACT.Sigmoid, bias=NEGB[:, j:j + 1], scale=-1.0))
            freed(bf, k)
            act.wait(tq)
            sq = act.op(lambda e: e.activation(QB[:, p, :], PS[bq][:, :], ACT.Sigmoid, bias=biased(j)))
            act.wait(tg)
            sg = act.op(lambda e: e.activation(GB[:, p, :], PS[bg][:, :], ACT.Sigmoid, bias=biased(24 + j)))
            dve.wait(s0, c)
            cu.append(dve.op(lambda e: e.tensor_tensor(CU[:, j, :], CU[:, j, :], SGA[:, p, :], ALU.mult)))
            dve.wait(sq, tq)
            q = dve.op(lambda e: e.scalar_tensor_tensor(QB[:, p, :], PS[bq][:, :], biased(j), QB[:, p, :], ALU.add, ALU.mult))
            freed(bq, q)
            dve.wait(sg, tg)
            g = dve.op(lambda e: e.scalar_tensor_tensor(GB[:, p, :], PS[bg][:, :], biased(24 + j), GB[:, p, :], ALU.add, ALU.mult))
            freed(bg, g)
            side_work.append(recurrence(j, (f, k, q, g), v_ready, parts, seen))
            if j:
                fill(2)
        finish()
        for g in (dve, act, pool):
            g.wait(*everything())
        gelu, yl, gw_used = {}, {}, [(), ()]
        sp.wait(*everything())
        for j in range(8):
            sp.wait(*gw_used[j % 2])
            gw = load(GW[:, j % 2, :], gates[j, :, :], s_gw[j % 2], 16 * (j // 2 + 1))
            b, t = product(m, 0, 4096 + j * P, HHI, HLO, ready)
            act.wait(t)
            if j >= 2:
                act.wait(yl[j - 2])
            x = act.op(lambda e: e.activation(LX[:, j % 2, :], PS[b][:, :], ACT.Identity, bias=biased(32 + j)))
            freed(b, x)
            finish()
            side_work.append(lru(j, x, gw, gw_used, gelu, yl, [yl[j - 1]] if j else []))
            fill(1)
            b, t = product(m, 0, 5120 + j * P, HHI, HLO, ready)
            act.wait(t)
            gelu[j] = act.op(lambda e: e.activation(GG[:, j % 2, :], PS[b][:, :], ACT.Gelu_apprx_tanh, bias=biased(40 + j)))
            freed(b, gelu[j])
            fill(1)
            b, t = product(m, 0, 8192 + j * P, HHI, HLO, ready)
            s = branch_gate(0, j, b, t)
            fill(2)
            b, t = product("w_branch_2", 0, j * P, YHI, YLO, parts)
            merge(j, b, t, s, SGA[:, j % 2, :], True)
            sga_free[j % 2] = mg[j]
            fill(1)
        finish()
        free = [pe.now()]
        parts = [split(YHI[:, j, :], YLO[:, j, :], YL[:, j, :], (yl[j],), free) for j in range(8)]
        restore(*(parts[-1]), dve.now(), act.now(), pe.now())
        for j in range(8):
            b, t = product(m, 0, 8192 + D + j * P, HHI, HLO, ready)
            s = branch_gate(1, j, b, t)
            fill(1)
            b, t = product("w_branch_2", 1, j * P, YHI, YLO, parts)
            merge(j, b, t, s, SGA[:, j % 2, :], False)
            sga_free[j % 2] = mg[j]
            fill(2)
        free = [pe.now()]
        while filler:
            fill()
        for g in (dve, act):
            g.wait(*everything())
        sgs = []

        def gate(j):
            b, t = product(m, 0, 8192 + 2 * D + j * P, HHI, HLO, ready)
            act.wait(t)
            sgs.append(act.op(lambda e: e.activation(GHT[:, j, :], PS[b][:, :], ACT.Sigmoid, bias=biased(80 + j))))
            freed(b, sgs[-1])

        b, t = over_channels(lambda j: CU[:, j, :], [(done[j],) for j in range(8)])
        act.wait(t)
        mu = act.op(lambda e: e.activation(LMU[:, :], PS[b][:, :], ACT.Copy, scale=1.0 / D))
        freed(b, mu)
        gate(0)
        gate(1)
        cen, used = [], []
        for j in range(8):
            dve.wait(mu, done[j])
            cen.append(dve.op(lambda e: e.tensor_tensor(CU[:, j, :], CU[:, j, :], LMU[:, :], ALU.subtract)))
        bv = bank("side")
        for j in range(8):
            act.wait(cen[j], *(used[j - 2:j - 1] if j >= 2 else []))
            sq = act.op(lambda e: e.activation(SQ[:, j % 2, :], CU[:, j, :], ACT.Square))
            pe.wait(sq)
            used.append(mm(PS[bv][:, :], ONES, SQ[:, j % 2, :], j == 0, j == 7, last=True))
        r = inverse_root(RS[:, :], PS[bv][:, :], D, vec("eps5"), used[-1])
        freed(bv, r)
        for j in range(2, 8):
            gate(j)
        parts = []
        act.wait(*free)
        for j in range(8):
            dve.wait(r, cen[j])
            y = dve.op(lambda e: e.tensor_tensor(CU[:, j, :], CU[:, j, :], RS[:, :], ALU.mult))
            act.wait(y)
            y = act.op(lambda e: e.activation(CU[:, j, :], CU[:, j, :], ACT.Silu, bias=vec("cvn", j), scale=vec("cvg", j)))
            parts.append(split(YHI[:, j, :], YLO[:, j, :], CU[:, j, :], (y,), free))
        for j in range(8):
            b, t = product("w_branch_2", 2, j * P, YHI, YLO, parts)
            merge(j, b, t, sgs[j], GHT[:, j, :], False)
        free = [pe.now()]
        parts = [split(YHI[:, j, :], YLO[:, j, :], MG[:, j, :], mg[j], free) for j in range(8)]
        for j in range(8):
            b, t = product("w_out_mix_2", 0, j * P, YHI, YLO, parts)
            add_to_x(j, b, t)
        for g in (dve, act, pool, pe):
            g.wait(*everything())
        ffn(at["nf2"], "ffn2_w_in_2", "ffn2_w_in_2", "ffn2_w_out_2", 0, 2816, 0.5)

    for l in range(2):
        block1(l)
    norm_x(at["fnorm"])
    block2()
    norm_x(at["nfin"])
    assert state["next"] == len(slots)
    for j in range(DT):
        sp.wait(*x_ready[j])
        load(out[:, j * T:(j + 1) * T], X[:, j, :], s_out, 0)
    sp.wait((s_out, 16 * DT))

    with nc.Block() as block:
        def run(g):
            def body(e):
                for make in g.queue:
                    make(e)
            return body

        block.sync(run(sp))
        block.tensor(run(pe))
        block.vector(run(dve))
        block.scalar(run(act))
        block.gpsimd(run(pool))


def shape_constants():
    i = np.arange(P)
    j, t = i[:, None], i[None, :]
    consts = np.stack([j == t, np.ones((P, P), bool), j // 64 == t // 64, j <= t, j >= t, j > t, j < t], 1)
    masks = [(j // (2 * h) == t // (2 * h)) & (j % (2 * h) < h) & (t % (2 * h) >= h) for h in LEVELS] + [j == t]
    masks = np.stack(masks, 1).astype(np.float32)
    half = 16
    inv = np.float32(10000.0) ** (-(np.float32(2.0) * np.arange(half, dtype=np.float32)) / np.float32(32))
    row = (np.arange(T) // 64).astype(np.float32)
    col = (np.arange(T) % 64).astype(np.float32)
    d = i % 64
    ang = np.where((d < 32)[:, None], row[None, :] * inv[d % 16][:, None], col[None, :] * inv[d % 16][:, None])
    ang = ang.astype(np.float32)
    turned = np.zeros((P, P), np.float32)
    for m in range(P):
        if m % 32 < 16:
            turned[m + 16, m] = -1.0
        else:
            turned[m - 16, m] = 1.0
    mats = [turned]
    for src in (np.eye(P, dtype=np.float32), turned):
        for g in range(2):
            mats.append(np.concatenate([src[:, 64 * g:64 * g + 64]] * 2, 1))
    rope = np.concatenate(mats + [np.cos(ang), np.sin(ang)], 1).astype(np.float32)
    return consts.astype(np.float32), masks, rope


def kernel(**inputs):
    import concourse.bacc as _bacc
    from concourse import mybir as _mybir
    from concourse.bass_utils import run_bass_kernel_spmd as _run

    a = {k: np.asarray(v) for k, v in inputs.items()}
    pieces = []
    for name, i, r0, nr, c0, ncol in plan():
        w = a[name]
        w = w[0, i] if name == "w_branch_2" else w[i]
        w = w[r0 * P:(r0 + nr) * P, c0:c0 + ncol]
        pieces.append(w.reshape(nr, P, ncol).transpose(1, 0, 2).reshape(-1))
    stream = np.concatenate(pieces)

    at, nvec = columns()
    vecs = np.zeros((P, nvec), np.float32)

    def put(key, v):
        v = v.reshape(-1, P).T
        vecs[:, at[key]:at[key] + v.shape[1]] = v

    def rows(key, v):
        v = v.reshape(1, -1)
        vecs[:, at[key]:at[key] + v.shape[1]] = np.broadcast_to(v, (P, v.shape[1]))

    for l in range(2):
        put(("nmix", l), a["norm_mix_w"][l])
        put(("qn", l), np.concatenate([a["q_norm_w"][l]] * 2))
        put(("kn", l), np.concatenate([a["k_norm_w"][l]] * 2))
        put(("cw", l), a["conv_w"][l])
        put(("cb", l), a["conv_b"][l])
        put(("sn", l), a["ssd_norm_w"][l])
        put(("nffn", l), a["norm_ffn_w"][l])
        rows(("dtb", l), a["dt_bias"][l])
        rows(("alog", l), a["a_log"][l])
        rows(("dsk", l), a["d_skip"][l])
    for key, name in (("fnorm", "final_norm_w"), ("nf1", "norm_ffn1_2"), ("nmix2", "norm_mix_2"), ("bin", "b_in_mix_2"),
                      ("lb", "hgrn_lb_logits_2"), ("hgn", "hg_norm_2"), ("lcw", "lru_conv_w_2"), ("lcb", "lru_conv_b_2"),
                      ("lgb", "lru_gate_b_2"), ("lam", "lru_lambda_2"), ("cvw", "cv_dw_w_2"), ("cvb", "cv_dw_b_2"),
                      ("cvg", "cv_ln_g_2"), ("cvn", "cv_ln_b_2"), ("nf2", "norm_ffn2_2"), ("nfin", "norm_final_2")):
        put(key, a[name])
    for key, value in (("eps", 1e-6), ("eps5", 1e-5), ("one", 1.0)):
        vecs[:, at[key]] = value
    xin = np.ascontiguousarray(a["x"][0].T.reshape(DT, P, T).transpose(1, 0, 2))
    hbias = np.ascontiguousarray(np.broadcast_to(a["b_in_mix_2"][0, 2048:3072][None, :], (P, D)))
    gates = np.ascontiguousarray(a["lru_gate_w_2"][0].transpose(1, 2, 0, 3).reshape(8, P, 256))
    consts, masks, rope = shape_constants()

    nc = _bacc.Bacc("TRN2", target_bir_lowering=False, num_devices=1)
    arrays, args = {}, []
    for name, v in (("stream", stream), ("xin", xin), ("vecs", vecs), ("consts", consts), ("masks", masks),
                    ("rope", rope), ("hbias", hbias), ("gates", gates)):
        arrays[f"in_{name}"] = v
        args.append(nc.dram_tensor(f"in_{name}", v.shape, _mybir.dt.from_np(v.dtype), kind="ExternalInput").ap())
    out = nc.dram_tensor("out_0", (P, DT * T), _mybir.dt.float32, kind="ExternalOutput").ap()
    xkeep = nc.dram_tensor("xkeep", (P, DT * T), _mybir.dt.float32, kind="Internal").ap()
    build(nc, xkeep, *args, out)
    r = _run(nc, [arrays], core_ids=[0])
    got = r.results[0]["out_0"].reshape(P, DT, T).transpose(1, 0, 2).reshape(D, T).T
    return np.ascontiguousarray(got).reshape(1, T, D)
```

```python
import numpy as np
import concourse.bass as bass
from concourse import mybir

F32 = mybir.dt.float32
F32R = mybir.dt.float32r
U8 = mybir.dt.uint8
ALU = mybir.AluOpType
ACT = mybir.ActivationFunctionType
AX = mybir.AxisListType.X

P = 128
T = 512
D = 1024
DT = 8
FT = 22
NH = 8
CH = 4
RAW = 4
SPL = 4
LOOK = 3
SLOT = 1024
LEVELS = (64, 32, 16, 8, 4, 2, 1)
TAPS = 31
TINY = 2.0 ** -63


def plan():
    s = []

    def fm(name, i, c0, rows=((0, DT),)):
        for r0, nr in rows:
            s.append((name, i, r0, nr, c0, P))

    def tm(name, i, c0):
        for r0 in range(0, DT, 2):
            s.append((name, i, r0, 2, c0, 512))

    down = ((0, 8), (8, 8), (16, 6))
    for l in range(2):
        tm("w_in", l, 768)
        for j in range(8):
            fm("w_in", l, 1280 + j * P)
        fm("w_in", l, 2192)
        fm("w_in", l, 640)
        for j in (4, 0, 1, 2, 3):
            fm("w_in", l, j * P)
        for j in range(DT):
            fm("w_out", l, j * P)
        for j in range(FT):
            fm("w_gate", l, j * P)
            fm("w_up", l, j * P)
        for j in range(DT):
            fm("w_down", l, j * P, down)

    def ffn(a, b):
        for j in range(FT):
            fm(a, 0, j * P)
            fm(a, 0, 2816 + j * P)
        for j in range(DT):
            fm(b, 0, j * P, down)

    ffn("ffn1_w_in_2", "ffn1_w_out_2")
    m = "w_in_mix_2"
    tm(m, 0, 2048)
    tm(m, 0, 2560)
    for j in range(8):
        for c in (1024, 0, 3072, 6144, 7168):
            fm(m, 0, c + j * P)
    for j in range(8):
        fm(m, 0, 4096 + j * P)
        fm(m, 0, 5120 + j * P)
        fm(m, 0, 8192 + j * P)
        fm("w_branch_2", 0, j * P)

    def branch(x):
        for j in range(8):
            fm(m, 0, 8192 + x * D + j * P)
            fm("w_branch_2", x, j * P)

    branch(1)
    for j in range(8):
        fm(m, 0, 8192 + 2 * D + j * P)
    for j in range(8):
        fm("w_branch_2", 2, j * P)
    for j in range(8):
        fm("w_out_mix_2", 0, j * P)
    ffn("ffn2_w_in_2", "ffn2_w_out_2")
    return s


def columns():
    at, n = {}, 0
    for l in range(2):
        for name, k in (("nmix", 8), ("qn", 1), ("kn", 1), ("cw", 40), ("cb", 8), ("sn", 4), ("nffn", 8),
                        ("dtb", 16), ("alog", 16), ("dsk", 8)):
            at[name, l] = n
            n += k
    for name, k in (("fnorm", 8), ("nf1", 8), ("nmix2", 8), ("bin", 88), ("lb", 8), ("hgn", 1), ("lcw", 32),
                    ("lcb", 8), ("lgb", 16), ("lam", 8), ("cvw", 8 * TAPS), ("cvb", 8), ("cvg", 8), ("cvn", 8),
                    ("nf2", 8), ("nfin", 8), ("eps", 1), ("eps5", 1), ("one", 1)):
        at[name] = n
        n += k
    return at, n


class Record:

    def copy(self, *a, **k):
        return lambda e: e.copy(*a, **k)

    def activation(self, *a, **k):
        return lambda e: e.activation(*a, **k)

    def tensor_tensor(self, *a, **k):
        return lambda e: e.tensor_tensor(*a, **k)

    def tensor_scalar(self, *a, **k):
        return lambda e: e.tensor_scalar(*a, **k)

    def scalar_tensor_tensor(self, *a, **k):
        return lambda e: e.scalar_tensor_tensor(*a, **k)

    def tensor_tensor_scan(self, *a, **k):
        return lambda e: e.tensor_tensor_scan(*a, **k)

    def tensor_reduce(self, *a, **k):
        return lambda e: e.tensor_reduce(*a, **k)

    def tensor_copy(self, *a, **k):
        return lambda e: e.tensor_copy(*a, **k)

    def reciprocal(self, *a, **k):
        return lambda e: e.reciprocal(*a, **k)

    def copy_predicated(self, *a, **k):
        return lambda e: e.copy_predicated(*a, **k)

    def memset(self, *a, **k):
        return lambda e: e.memset(*a, **k)

    def matmul(self, *a, **k):
        return lambda e: e.matmul(*a, **k)

    def transpose(self, *a, **k):
        return lambda e: e.transpose(*a, **k)


class Engine:

    def __init__(self, sem):
        self.sem, self.n, self.queue, self.seen = sem, 0, [], {}

    def wait(self, *tokens):
        for sem, value in tokens:
            if self.seen.get(id(sem), 0) < value:
                self.seen[id(sem)] = value
                self.queue.append(lambda e, s=sem, v=value: e.wait_ge(s, v))

    def op(self, make):
        self.n += 1
        instruction = make(Record())
        self.queue.append(lambda e: instruction(e).then_inc(self.sem, 1))
        return (self.sem, self.n)

    def quiet(self, make):
        self.queue.append(make(Record()))

    def now(self):
        return (self.sem, self.n)


def build(nc, xkeep, stream, xin, vecs, consts, masks, rope, hbias, gates, out):
    slots = plan()
    at, nvec = columns()
    base = nc.sbuf_base + (-nc.sbuf_base) % 64
    K = 1024

    def sb(name, kib, shape, dt=F32):
        return nc.alloc_sbuf_tensor_at(name, [P] + shape, dt, offset=base + int(kib * K))

    X = sb("X", 0, [DT, T])
    WR = sb("WR", 16, [RAW, SLOT])
    WHI = sb("WHI", 32, [SPL, SLOT], F32R)
    WLO = sb("WLO", 48, [SPL, SLOT], F32R)
    CON = sb("CON", 64, [7, P])
    VEC = sb("VEC", 67.5, [nvec])
    MSK = sb("MSK", 71, [8, P], U8)
    MSF = sb("MSF", 164, [8, P])
    NEGB = sb("NEGB", 72, [8])
    OML = sb("OML", 72.0625, [8])
    LBV = sb("LBV", 72.125, [8])
    C8 = sb("C8", 72.1875, [8])
    SMT = sb("SMT", 72.25, [4, 8])
    QNS = sb("QNS", 72.5, [2])
    SQ = sb("SQ", 74, [2, T])
    HF = sb("HF", 78, [2, T])
    RS = sb("RS", 82, [T])
    HHI = sb("HHI", 84, [DT, T], F32R)
    HLO = sb("HLO", 100, [DT, T], F32R)
    YHI = sb("YHI", 116, [DT, T], F32R)
    YLO = sb("YLO", 132, [DT, T], F32R)
    FHI = sb("FHI", 116, [FT, T], F32R)
    FLO = sb("FLO", 160, [FT, T], F32R)
    RQ = sb("RQ", 0, [4, T])
    RT = sb("RT", 148, [5, P])
    COS = sb("COS", 150.5, [T])
    SIN = sb("SIN", 152.5, [T])
    Z = sb("Z", 156, [CH, T])
    XBC = sb("XBC", 164, [DT, T])
    Q = sb("Q", 180, [4, T])
    KD = sb("KD", 188, [2, T])
    V = sb("V", 192, [CH, P])
    PR = sb("PR", 194, [2, T])
    PT = sb("PT", 198, [2, CH, 256])
    NM = sb("NM", 206, [4])
    RSM = sb("RSM", 206.0625, [4])
    RIN = sb("RIN", 206.125, [4])
    DTR = sb("DTR", 206.25, [CH, 16])
    SGB = sb("SGB", 74, [4, T])
    RRS = sb("RRS", 82, [T])
    XST = XBC
    BT = sb("BT", 8, [CH, 256])
    XCD = sb("XCD", 12, [T])
    XCE = sb("XCE", 14, [T])
    MF = sb("MF", 12, [2, P])
    MB = sb("MB", 13, [2, P])
    STF = sb("STF", 124, [3, T])
    SD = sb("SD", 130, [7, CH, 16])
    STB = sb("STB", 140, [3, T])
    EX = sb("EX", 146, [5, CH, 16])
    DTE = sb("DTE", 147.25, [CH, 16])
    SS = sb("SS", 147.5, [2, 8])
    RAF = sb("RAF", 84, [8, P])
    DEF = sb("DEF", 88, [8, P])
    RAB = sb("RAB", 92, [8, P])
    DEB = sb("DEB", 96, [8, P])
    WF = sb("WF", 100, [8, P])
    WB = sb("WB", 104, [8, P])
    XCF = sb("XCF", 108, [T])
    XCB = sb("XCB", 110, [T])
    YA = sb("YA", 112, [T])
    YB = sb("YB", 114, [T])
    FB = sb("FB", 0, [2, T])
    KB = sb("KB", 4, [2, T])
    QB = sb("QB", 8, [2, T])
    GB = sb("GB", 12, [2, T])
    YL = sb("YL", 0, [DT, T])
    GHT = sb("GHT", 148, [8, T])
    CVA = sb("CVA", 148, [2, T])
    SGA = sb("SGA", 152, [2, T])
    CB = sb("CB", 156, [T])
    SAC = sb("SAC", 158, [CH, P])
    HD = sb("HD", 160, [2, T])
    HB = sb("HB", 132, [D])
    CU = sb("CU", 164, [DT, T])
    VH = sb("VH", 180, [CH, D])
    MG = sb("MG", 180, [DT, T])
    QT = sb("QT", 196, [2, T])
    KT = sb("KT", 200, [2, T])
    SOF = sb("SOF", 204, [768])
    QTX = sb("QTX", 128, [2, T])
    KTX = sb("KTX", 144, [2, T])
    LX = sb("LX", 156, [2, T])
    GG = sb("GG", 160, [2, T])
    XB = sb("XB", 74, [T])
    GR = sb("GR", 76, [T])
    GI = sb("GI", 78, [T])
    GA = sb("GA", 80, [T])
    GT = sb("GT", 82, [T])
    GM = sb("GM", 196, [T])
    GW = sb("GW", 198, [2, 256])
    LMU = sb("LMU", 196, [T])
    PS = [nc.alloc_psum_tensor(f"PS{i}", [P, 512], F32) for i in range(8)]

    IDN, ONES, BONES, TRIF, TRIB, UP, LOW = (CON[:, i, :] for i in range(7))

    def vec(name, i=0, n=1):
        return VEC[:, at[name] + i:at[name] + i + n]

    sems = {}

    def sem(name):
        sems[name] = nc.alloc_semaphore(name)
        return sems[name]

    pe, dve, act, pool = (Engine(sem(n)) for n in ("s_pe", "s_dve", "s_act", "s_pool"))
    sp = Engine(None)
    engines = (pe, dve, act, pool)
    s_con, s_rope, s_hb, s_out = sem("s_con"), sem("s_rope"), sem("s_hb"), sem("s_out")
    s_spill = sem("s_spill")
    s_back = [sem(f"s_back{i}") for i in range(DT)]
    s_x = [sem(f"s_x{i}") for i in range(DT)]
    s_gw = [sem(f"s_gw{i}") for i in range(2)]
    s_w = [sem(f"s_w{i}") for i in range(RAW)]

    def load(dst, src, s, value, g=None):
        (g or sp).queue.append(lambda e: e.dma_start(dst, src).then_inc(s, 16))
        return (s, value)

    def everything():
        return [g.now() for g in engines]

    load(VEC[:, :], vecs, s_con, 0)
    load(CON[:, :, :], consts, s_con, 0)
    x_ready = [[load(X[:, j, :], xin[:, j, :], s_x[j], 16, act)] for j in range(DT)]
    for g in engines:
        g.wait((s_con, 32))

    offset, o = [], 0
    for _, _, _, nr, _, ncol in slots:
        offset.append(o)
        o += P * nr * ncol
    state = {"load": 0, "split": 0, "next": 0, "pool": False}
    raw_free, split_free, split_done = {}, {}, {}

    def load_slot():
        i = state["load"]
        if i >= len(slots):
            return
        state["load"] += 1
        n = slots[i][3] * slots[i][5]
        if i >= RAW:
            sp.wait(*raw_free[i - RAW])
        src = stream[offset[i]:offset[i] + P * n].rearrange("(p n) -> p n", p=P)
        load(WR[:, i % RAW, 0:n], src, s_w[i % RAW], 0)

    def split_slot():
        i = state["split"]
        if i >= len(slots):
            return
        state["split"] += 1
        n = slots[i][3] * slots[i][5]
        raw, hi, lo = WR[:, i % RAW, 0:n], WHI[:, i % SPL, 0:n], WLO[:, i % SPL, 0:n]
        landed = (s_w[i % RAW], 16 * (i // RAW + 1))
        act.wait(landed)
        g = pool if state["pool"] else dve
        if i >= SPL:
            act.wait(split_free[i - SPL])
            g.wait(split_free[i - SPL])
        a = act.op(lambda e: e.copy(hi, raw))
        g.wait(a, landed)
        b = g.op(lambda e: e.tensor_tensor(lo, raw, hi.bitcast(F32), ALU.subtract))
        raw_free[i] = (a, b)
        split_done[i] = (a, b)
        load_slot()

    def advance(look=LOOK):
        while state["split"] < state["next"] + look and (state["split"] < SPL or state["split"] - SPL in split_free):
            if state["split"] >= len(slots):
                return
            split_slot()

    for _ in range(RAW):
        load_slot()
    advance()

    def take(name, i, r0, c0):
        k = state["next"]
        state["next"] += 1
        s = slots[k]
        assert s[:3] + (s[4],) == (name, i, r0, c0), (s, name, i, r0, c0)
        advance()
        pe.wait(*split_done[k])
        nr, ncol = s[3], s[5]
        n = nr * ncol
        hi = WHI[:, k % SPL, 0:n].rearrange("p (r c) -> p r c", r=nr)
        lo = WLO[:, k % SPL, 0:n].rearrange("p (r c) -> p r c", r=nr)
        return k, hi, lo

    def release(k, t):
        split_free[k] = t
        advance()

    bank_free = {i: [] for i in range(8)}
    turn = {"main": 0, "side": 0}

    held = set()

    def bank(kind="main"):
        first = 0 if kind == "main" else 4
        b = next(b for b in (first + (turn[kind] + i) % 4 for i in range(4)) if b not in held)
        turn[kind] = b - first + 1
        held.add(b)
        pe.wait(*bank_free[b])
        return b

    def freed(b, *tokens):
        held.discard(b)
        bank_free[b] = list(tokens)

    def mm(out_, lhsT, rhs, start, stop, last=False, **k):
        make = lambda e: e.matmul(out_, lhsT, rhs, start=start, stop=stop, **k)
        return pe.op(make) if last else pe.quiet(make)

    def transpose(out_, in_):
        return pe.op(lambda e: e.transpose(out_, in_, IDN))

    side_work, other_work, third_work, filler = [], [], [], []
    flip, order = [0], [side_work, other_work, third_work]

    def pump(n=1):
        for _ in range(n):
            flip[0] += 1
            chains = [w for w in order if w]
            if not chains:
                return
            w = chains[flip[0] % len(chains)]
            if next(w[0], "end") == "end":
                w.pop(0)

    def fill(n=1):
        for _ in range(n):
            if filler and next(filler[0], "end") == "end":
                filler.pop(0)

    rate = {"pump": 4, "fill": 0}

    def beat(r):
        for _ in range((r + 1) * rate["pump"] // 8 - r * rate["pump"] // 8):
            pump()
        fill((r + 1) * rate["fill"] // 8 - r * rate["fill"] // 8)

    def finish():
        while side_work or other_work or third_work:
            pump()

    def product(name, i, c0, rhi, rlo, ready, rows=((0, DT),)):
        b = bank()
        for r0, nr in rows:
            k, hi, lo = take(name, i, r0, c0)
            for r in range(nr):
                pe.wait(*ready[r0 + r])
                first, final = r0 + r == 0, r0 + r == rows[-1][0] + rows[-1][1] - 1
                mm(PS[b][:, :], hi[:, r, :], rhi[:, r0 + r, :], first, False)
                mm(PS[b][:, :], hi[:, r, :], rlo[:, r0 + r, :], False, False)
                t = mm(PS[b][:, :], lo[:, r, :], rhi[:, r0 + r, :], False, final, last=r == nr - 1)
                if r == nr - 1:
                    release(k, t)
                beat(r)
        return b, t

    def product_group(columns_, ready):
        bs, ks = [], []
        for name, i, c0 in columns_:
            bs.append(bank())
            ks.append(take(name, i, 0, c0))
        ts = [None] * len(bs)
        for r in range(DT):
            pe.wait(*ready[r])
            for n, (b, (k, hi, lo)) in enumerate(zip(bs, ks)):
                mm(PS[b][:, :], hi[:, r, :], HHI[:, r, :], r == 0, False)
                mm(PS[b][:, :], hi[:, r, :], HLO[:, r, :], False, False)
                ts[n] = mm(PS[b][:, :], lo[:, r, :], HHI[:, r, :], False, r == DT - 1, last=r == DT - 1)
        for (k, _, _), t in zip(ks, ts):
            release(k, t)
        return list(zip(bs, ts))

    def product_tokens(name, i, c0, ready):
        bs = [bank() for _ in range(CH)]
        ts = [None] * CH
        for r0 in range(0, DT, 2):
            k, hi, lo = take(name, i, r0, c0)
            for c in range(CH):
                for r in range(2):
                    pe.wait(*ready[r0 + r])
                    a, l = HHI[:, r0 + r, c * P:(c + 1) * P], HLO[:, r0 + r, c * P:(c + 1) * P]
                    first, final = r0 + r == 0, r0 + r == DT - 1
                    mm(PS[bs[c]][:, :], a, hi[:, r, :], first, False)
                    mm(PS[bs[c]][:, :], a, lo[:, r, :], False, False)
                    ts[c] = mm(PS[bs[c]][:, :], l, hi[:, r, :], False, final, last=r == 1)
                pump()
            release(k, ts[CH - 1])
        return list(zip(bs, ts))

    rs_free = [[]]

    def inverse_root(dst, src, n, eps, *ready):
        act.wait(*ready)
        t = act.op(lambda e: e.activation(dst, src, ACT.Ln, bias=eps, scale=1.0 / n))
        act.wait(t)
        return act.op(lambda e: e.activation(dst, dst, ACT.Exp, scale=-0.5))

    squares = {"bank": None, "used": []}

    def begin_squares(*after):
        act.wait(*after)
        squares["bank"], squares["used"] = bank("side"), []

    def square(j):
        used, b = squares["used"], squares["bank"]
        act.wait(*x_ready[j], *used[j - 2:j - 1] if j >= 2 else ())
        t = act.op(lambda e: e.activation(SQ[:, j % 2, :], X[:, j, :], ACT.Square))
        yield
        pe.wait(t)
        used.append(mm(PS[b][:, :], ONES, SQ[:, j % 2, :], j == 0, j == DT - 1, last=True))

    def mean_square():
        if squares["bank"] is None:
            begin_squares()
            for j in range(DT):
                for _ in square(j):
                    pass
        finish()
        b = squares["bank"]
        squares["bank"] = None
        act.wait(*rs_free[0])
        t = inverse_root(RS[:, :], PS[b][:, :], D, vec("eps"), squares["used"][-1])
        freed(b, t)
        return t

    def split(hi, lo, src, ready, free=()):
        act.wait(*ready, *free)
        a = act.op(lambda e: e.copy(hi, src))
        dve.wait(a, *ready, *free)
        return a, dve.op(lambda e: e.tensor_tensor(lo, src, hi.bitcast(F32), ALU.subtract))

    def norm_split(w):
        for g in (act, dve):
            g.wait(*everything())
        advance(SPL)
        rs = mean_square()
        ready, free = [], [(), ()]
        for j in range(DT):
            dve.wait(rs, *x_ready[j], *free[j % 2])
            t = dve.op(lambda e, j=j: e.scalar_tensor_tensor(HF[:, j % 2, :], X[:, j, :], VEC[:, w + j:w + j + 1],
                                                            RS[:, :], ALU.mult, ALU.mult))
            ready.append(split(HHI[:, j, :], HLO[:, j, :], HF[:, j % 2, :], (t,)))
            free[j % 2] = ready[-1]
        rs_free[0] = [t]
        return ready

    def norm_x(w):
        rs = mean_square()
        for j in range(DT):
            dve.wait(rs, *x_ready[j])
            x_ready[j] = [dve.op(lambda e, j=j: e.scalar_tensor_tensor(
                X[:, j, :], X[:, j, :], VEC[:, w + j:w + j + 1], RS[:, :], ALU.mult, ALU.mult))]
        rs_free[0] = [x_ready[-1][0]]

    spills = [0]

    def spill():
        spills[0] += 1
        for r in x_ready:
            pool.wait(*r)
        return load(xkeep, X[:, :, :].rearrange("p a b -> p (a b)"), s_spill, 16 * spills[0], pool)

    def restore(*users):
        pool.wait(*users)
        for j in range(DT):
            x_ready[j] = [load(X[:, j, :], xkeep[:, j * T:(j + 1) * T], s_back[j], 16 * spills[0], pool)]

    def add_to_x(j, b, t, scale=1.0):
        dve.wait(t, *x_ready[j])
        x_ready[j] = [dve.op(lambda e: e.scalar_tensor_tensor(X[:, j, :], PS[b][:, :], scale, X[:, j, :],
                                                              ALU.mult, ALU.add))]
        freed(b, x_ready[j][0])
        side_work.append(square(j))

    def ffn(w, gate, up, down, i, up0, scale):
        ready = norm_split(w)
        parts, sg_free, af_free = [], [(), ()], [(), ()]
        early = product_group([(n, i, c + j * P) for j in range(2) for n, c in ((gate, 0), (up, up0))], ready)
        for j in range(FT):
            bg, tg = early[2 * j] if j < 2 else product(gate, i, j * P, HHI, HLO, ready)
            act.wait(tg, *sg_free[j % 2])
            s = act.op(lambda e: e.activation(SQ[:, j % 2, :], PS[bg][:, :], ACT.Silu))
            freed(bg, s)
            bu, tu = early[2 * j + 1] if j < 2 else product(up, i, up0 + j * P, HHI, HLO, ready)
            dve.wait(s, tu, *af_free[j % 2])
            m = dve.op(lambda e: e.tensor_tensor(HF[:, j % 2, :], SQ[:, j % 2, :], PS[bu][:, :], ALU.mult))
            sg_free[j % 2] = (m,)
            freed(bu, m)
            parts.append(split(FHI[:, j, :], FLO[:, j, :], HF[:, j % 2, :], (m,)))
            af_free[j % 2] = parts[-1]
        begin_squares(*sg_free[0], *sg_free[1])
        for j in range(DT):
            b, t = product(down, i, j * P, FHI, FLO, parts, ((0, 8), (8, 8), (16, 6)))
            add_to_x(j, b, t, scale)

    def rotated(j, raw, copied, w, done):
        dve_last = done[-1:]
        act.wait(copied, *dve_last)
        s = act.op(lambda e: e.activation(SGB[:, 0, :], raw, ACT.Square))
        yield
        n = bank("side")
        pe.wait(s)
        t = mm(PS[n][:, :], BONES, SGB[:, 0, :], True, True, last=True)
        yield
        r = inverse_root(RRS[:, :], PS[n][:, :], 64, vec("eps"), t)
        freed(n, r)
        dve.wait(r)
        qn = dve.op(lambda e: e.scalar_tensor_tensor(raw, raw, w, RRS[:, :], ALU.mult, ALU.mult))
        yield
        for dst, plain, turned in ([(Q[:, j, :], None, 0)] if j < 4 else [(KD[:, 0, :], 1, 3), (KD[:, 1, :], 2, 4)]):
            pe.wait(qn)
            src, b1 = raw, None
            if plain is not None:
                b1 = bank("side")
                t1 = mm(PS[b1][:, :], RT[:, plain, :], raw, True, True, last=True)
                src = PS[b1][:, :]
            b2 = bank("side")
            t2 = mm(PS[b2][:, :], RT[:, turned, :], raw, True, True, last=True)
            yield
            dve.wait(qn, t2, *done[-1:])
            u = dve.op(lambda e: e.tensor_tensor(SGB[:, 2, :], src, COS[:, :], ALU.mult))
            if b1 is not None:
                freed(b1, u)
            v = dve.op(lambda e: e.tensor_tensor(SGB[:, 3, :], PS[b2][:, :], SIN[:, :], ALU.mult))
            freed(b2, v)
            dve.wait(u, v)
            done.append(dve.op(lambda e: e.tensor_tensor(dst, SGB[:, 2, :], SGB[:, 3, :], ALU.add)))
            yield

    def attention(turned, v_ready, parts):
        probs, pr_free, pt_free, pt_done = {}, [(), (), ()], [(), ()], {}
        PRS = (PR[:, 0, :], PR[:, 1, :], SGB[:, 1, :])
        steps = [(h, c) for h in range(NH) for c in range(CH)]

        def scores(i):
            h, c = steps[i]
            lo = 64 * (h % 2)
            b = bank("side")
            pe.wait(turned[0], turned[1], turned[2 + h // 2])
            t = mm(PS[b][:, :], Q[lo:lo + 64, h // 2, c * P:(c + 1) * P], KD[lo:lo + 64, h // 4, :], True, True, last=True)
            k = i % 4
            dve.wait(t, *(probs[i - 4] if i >= 4 else ()))
            m = dve.op(lambda e: e.tensor_reduce(NM[:, k:k + 1], PS[b][:, :], AX, ALU.max, negate=True))
            act.wait(m, *pr_free[i % 3])
            x = act.op(lambda e: e.activation(PRS[i % 3], PS[b][:, :], ACT.Exp, bias=NM[:, k:k + 1],
                                              accum_out=RSM[:, k:k + 1]))
            freed(b, x)
            dve.wait(x)
            r = dve.op(lambda e: e.reciprocal(RIN[:, k:k + 1], RSM[:, k:k + 1]))
            dve.wait(r)
            n = dve.op(lambda e: e.tensor_scalar(PRS[i % 3], PRS[i % 3], RIN[:, k:k + 1], None, ALU.mult))
            probs[i] = (n, x)

        def turn_probs(i):
            h, c = steps[i]
            half = i // 2
            b = bank("side")
            pe.wait(probs[i][0])
            for k in range(CH):
                t = transpose(PS[b][:, k * P:(k + 1) * P], PRS[i % 3][:, k * P:(k + 1) * P])
            pr_free[i % 3] = (t,)
            g = act if i % 2 else dve
            g.wait(t, *pt_free[half % 2])
            dst = PT[:, half % 2, :, (c % 2) * P:(c % 2 + 1) * P]
            src = PS[b][:, :].rearrange("p (k q) -> p k q", k=CH)
            e_ = g.op((lambda e: e.copy(dst, src)) if g is act else (lambda e: e.tensor_copy(dst, src)))
            freed(b, e_)
            pt_done[i] = e_

        def values(half):
            h, q0 = half // 2, 256 * (half % 2)
            lo = 64 * (h % 2)
            b = bank("side")
            pe.wait(pt_done[2 * half], pt_done[2 * half + 1], *v_ready)
            for k in range(CH):
                t = mm(PS[b][lo:lo + 64, 0:256], V[:, k, 64 * (h // 4):64 * (h // 4) + 64], PT[:, half % 2, k, :],
                       k == 0, k == CH - 1, last=k == CH - 1)
            pt_free[half % 2] = (t,)
            a, l = split(YHI[lo:lo + 64, h // 2, q0:q0 + 256], YLO[lo:lo + 64, h // 2, q0:q0 + 256],
                         PS[b][lo:lo + 64, 0:256], (t,))
            freed(b, a, l)
            parts[h // 2] += [a, l]

        n = len(steps)
        for i in range(n + 4):
            while i < n and (len(turned) < 3 + steps[i][0] // 2 or not v_ready):
                yield
            if i < n:
                scores(i)
            if 2 <= i <= n + 1:
                turn_probs(i - 2)
            if i >= 5 and i % 2 == 1:
                values((i - 5) // 2)
            yield

    def heads_by(x, n=8, w=64):
        return x.unsqueeze(2).to_broadcast([P, n, w])

    def block1(l):
        cols = lambda name, i=0, n=1: VEC[:, at[name, l] + i:at[name, l] + i + n]
        for g in (dve, act, pool, pe, sp):
            g.wait(*everything())
        load(RT[:, :, :], rope[:, 0:640].rearrange("p (a b) -> p a b", a=5), s_rope, 0)
        load(COS[:, :], rope[:, 640:1152], s_rope, 0)
        tables = [load(SIN[:, :], rope[:, 1152:1664], s_rope, 48 * (l + 1))]
        for g in (pe, dve):
            g.wait(*tables)
        kept = spill()
        ready = norm_split(at["nmix", l])
        dve.op(lambda e: e.tensor_scalar(QNS[:, 0:1], cols("qn"), 0.125, None, ALU.mult))
        dve.wait(dve.now())
        for g in (act, dve):
            g.wait(kept, *ready[-1], dve.now())
        z_done, x_done = [], []
        for c, (b, t) in enumerate(product_tokens("w_in", l, 768, ready)):
            act.wait(t)
            z_done.append(act.op(lambda e: e.activation(Z[:, c, :], PS[b][:, :], ACT.Silu)))
            freed(b, z_done[-1])
        for j in range(8):
            b, t = product("w_in", l, 1280 + j * P, HHI, HLO, ready)
            act.wait(t)
            w = lambda k: cols("cw", 8 * k + j)
            y = act.op(lambda e: e.activation(XBC[:, j, :], PS[b][:, :], ACT.Copy, scale=w(2)))
            for k, s in ((0, -2), (1, -1), (3, 1), (4, 2)):
                o0, o1 = max(0, -s), T - max(0, s)
                dve.wait(y)
                y = dve.op(lambda e: e.scalar_tensor_tensor(
                    XBC[:, j, o0:o1], PS[b][:, o0 + s:o1 + s], w(k), XBC[:, j, o0:o1], ALU.mult, ALU.add))
            freed(b, y)
            act.wait(y)
            x_done.append(act.op(lambda e: e.activation(XBC[:, j, :], XBC[:, j, :], ACT.Silu, bias=cols("cb", j))))
        v_ready, dt_ready, done, raw_used = [], [], [], {}

        def raw_tile(n, c0):
            b, t = product("w_in", l, c0, HHI, HLO, ready)
            while n >= 4 and n - 4 not in raw_used:
                pump()
            act.wait(t, *(raw_used[n - 4] if n >= 4 else ()))
            a = act.op(lambda e: e.copy(RQ[:, n % 4, :], PS[b][:, :]))
            freed(b, a)
            return a

        def tokens(n, copied, after):
            b = bank("side")
            pe.wait(copied)
            for c in range(CH):
                t = transpose(PS[b][:, c * P:(c + 1) * P], RQ[:, n % 4, c * P:(c + 1) * P])
            raw_used[n] = (t,)
            yield
            after(b, t)
            yield

        def v_out(b, t):
            act.wait(t)
            v_ready.append(act.op(lambda e: e.copy(V[:, :, :].rearrange("p a b -> p (a b)"), PS[b][:, :])))
            freed(b, v_ready[-1])

        def dt_out(b, t):
            dve.wait(t)
            dt_ready.append(dve.op(lambda e: e.tensor_tensor(
                DTR[:, :, :], PS[b][:, :].rearrange("p (c h) -> p c h", c=CH)[:, :, 112:128],
                cols("dtb", 0, 16).unsqueeze(1).to_broadcast([P, CH, 16]), ALU.add)))
            freed(b, dt_ready[-1])

        def rotate(n, j, copied):
            yield from rotated(j, RQ[:, n % 4, :], copied, QNS[:, 0:1] if j < 4 else cols("kn"), done)
            raw_used[n] = (done[-1],)

        parts = [[] for _ in range(DT)]
        states = {}

        def ssd_first():
            for g in (act, dve):
                g.wait(*x_done, *z_done, *dt_ready)
            yield from ssd_states(cols, turned, states)

        rate.update(pump=12)
        a = raw_tile(0, 2192)
        v = raw_tile(1, 640)
        turned = tokens_first(x_done)
        other_work.append(tokens(0, a, dt_out))
        other_work.append(tokens(1, v, v_out))
        other_work.append(ssd_first())
        third_work.append(attention(done, v_ready, parts))
        for n, j in enumerate((4, 0, 1, 2, 3)):
            a = raw_tile(2 + n, j * P)
            side_work.append(rotate(2 + n, j, a))
        while other_work:
            pump()
        rate.update(pump=4)
        for g in (act, dve):
            g.wait(pe.now())
        other_work.append(ssd(cols, x_done, parts, states))
        finish()
        restore(*everything())
        begin_squares(*everything())
        for j in range(DT):
            b, t = product("w_out", l, j * P, YHI, YLO, parts)
            add_to_x(j, b, t)
        for g in (dve, act, pool):
            g.wait(*everything())
        ffn(at["nffn", l], "w_gate", "w_up", "w_down", l, 0, 1.0)

    def tokens_first(inputs):
        pe.wait(*inputs)
        bs = []
        for c in range(CH):
            b = bank("side")
            for i in range(4):
                t = transpose(PS[b][:, i * P:(i + 1) * P], XBC[:, i, c * P:(c + 1) * P])
            bs.append(b)
        act.wait(t)
        dve.wait(t)
        done = []
        for c, b in enumerate(bs):
            if c % 2:
                done.append(act.op(lambda e: e.copy(XST[:, c, :], PS[b][:, :])))
            else:
                done.append(dve.op(lambda e: e.tensor_copy(XST[:, c, :], PS[b][:, :])))
            freed(b, done[-1])
        for c in range(2):
            b = bank("side")
            for n in range(2):
                for i in range(2):
                    t = transpose(PS[b][:, (2 * n + i) * P:(2 * n + i + 1) * P], XBC[:, 4 + i, (2 * c + n) * P:(2 * c + n + 1) * P])
            act.wait(t)
            done.append(act.op(lambda e: e.copy(BT[:, 2 * c:2 * c + 2, :].rearrange("p a b -> p (a b)"), PS[b][:, :])))
            freed(b, done[-1])
        return done

    def ssd_states(cols, turned, out_):
        sd = lambda i: SD[:, i, :, :]

        def chain(g, make, *also):
            g.wait(*also)
            t = g.op(make)
            for o_ in (dve, act):
                o_.wait(t)
            return t

        x0 = DTR[:, :, :]
        chain(dve, lambda e: e.tensor_scalar(sd(0), x0, -1.0, None, ALU.mult))
        chain(dve, lambda e: e.tensor_tensor(sd(0), sd(0), x0, ALU.max))
        chain(act, lambda e: e.activation(sd(1), sd(0), ACT.Exp, scale=-1.0))
        chain(dve, lambda e: e.tensor_scalar(sd(2), sd(1), 1.0, None, ALU.add))
        chain(act, lambda e: e.activation(sd(3), sd(2), ACT.Ln))
        yield
        chain(dve, lambda e: e.tensor_scalar(sd(2), sd(2), -1.0, None, ALU.add))
        chain(dve, lambda e: e.tensor_tensor(sd(2), sd(1), sd(2), ALU.subtract))
        chain(dve, lambda e: e.tensor_tensor(sd(3), sd(3), sd(2), ALU.add))
        chain(dve, lambda e: e.tensor_scalar(sd(0), x0, 0.0, None, ALU.max))
        chain(dve, lambda e: e.tensor_tensor(sd(4), sd(0), sd(3), ALU.add))
        step_ = sd(4)
        chain(act, lambda e: e.activation(SD[:, 5, 0, :], cols("alog", 0, 16), ACT.Exp))
        chain(dve, lambda e: e.tensor_scalar(SD[:, 5, 0, :], SD[:, 5, 0, :], -1.0, None, ALU.mult))
        da = chain(dve, lambda e: e.tensor_tensor(
            sd(6), step_, SD[:, 5, 0, :].unsqueeze(1).to_broadcast([P, CH, 16]), ALU.mult))
        yield
        b = bank()
        pe.wait(da)
        dA = sd(6).rearrange("p a b -> p (a b)")
        for i, m in enumerate((UP, LOW, TRIF, TRIB, ONES)):
            t = mm(PS[b][:, i * 64:(i + 1) * 64], m, dA, True, True, last=True)
        yield
        ex = chain(act, lambda e: e.activation(EX[:, :, :, :].rearrange("p a b c -> p (a b c)"), PS[b][:, 0:320], ACT.Exp), t)
        freed(b, ex)
        for d in range(2):
            dte = chain(dve, lambda e: e.tensor_tensor(
                DTE[:, :, 8 * d:8 * d + 8], step_[:, :, 8 * d:8 * d + 8], EX[:, d, :, 8 * d:8 * d + 8], ALU.mult))
        by_head = lambda x: x.rearrange("p (h d) -> p h d", h=8)
        st, prev, xcd = {}, [None, None], [(), ()]
        XD = (XCD, XCE)
        for n in range(3):
            banks = []
            for d, c in ((0, n), (1, 3 - n)):
                dve.wait(*turned, dte, *xcd[d])
                x = dve.op(lambda e: e.tensor_tensor(
                    by_head(XD[d][:, :]), by_head(XST[:, c, :]), heads_by(DTE[:, c, 8 * d:8 * d + 8]), ALU.mult))
                banks.append((d, c, x))
            yield
            got = []
            for d, c, x in banks:
                b = bank()
                pe.wait(x, *turned)
                for g in range(2):
                    t = mm(PS[b][:, 256 * g:256 * g + 256], BT[:, c, g * P:(g + 1) * P], XD[d][:, 256 * g:256 * g + 256],
                           True, True, last=True)
                xcd[d] = (t,)
                got.append((d, c, b, t))
            yield
            for d, c, b, t in got:
                S = (STF, STB)[d]
                dve.wait(t)
                if n == 0:
                    s = dve.op(lambda e: e.tensor_copy(S[:, 0, :], PS[b][:, :]))
                else:
                    dve.wait(prev[d])
                    s = dve.op(lambda e: e.tensor_tensor(
                        by_head(S[:, n, :]), by_head(S[:, n - 1, :]), heads_by(EX[:, 4, c, 8 * d:8 * d + 8]), ALU.mult))
                    dve.wait(s)
                    s = dve.op(lambda e: e.tensor_tensor(S[:, n, :], S[:, n, :], PS[b][:, :], ALU.add))
                freed(b, s)
                prev[d] = s
                st[d, c + 1 if d == 0 else c - 1] = (S, n, s)
        out_.update(st=st, tok=turned, step=step_, sd=sd, by_head=by_head, last=[xcd[0][0], xcd[1][0], prev[0], prev[1]])

    def ssd(cols, inputs, parts, o):
        st, tok, step_, sd, by_head = o["st"], o["tok"], o["step"], o["sd"], o["by_head"]
        ways = ((0, TRIF, UP, MF, RAF, DEF, WF, XCF), (1, TRIB, LOW, MB, RAB, DEB, WB, XCB))
        ra_read, w_read, ws, sq, y_out = [(), ()], o["last"], [], [], []
        tail = iter(())

        def exponents(c):
            tokens_ = []
            for d, tri, side_, M, RA, DEC, W, XC in ways:
                dve.wait(*ra_read[d])
                tokens_.append(dve.op(lambda e: e.tensor_tensor(
                    RA[:, :, :], heads_by(sd(6)[:, c, 8 * d:8 * d + 8], 8, P),
                    tri.unsqueeze(1).to_broadcast([P, 8, P]), ALU.mult)))
            return tokens_

        ras = exponents(0)

        def gate(c, offs, y, yb, td):
            for d, b, t in offs:
                dve.wait(t, y, *sq)
                u = dve.op(lambda e: e.tensor_tensor(
                    by_head(YB[:, :]), by_head(PS[b][:, :]), heads_by(EX[:, 2 + d, c, 8 * d:8 * d + 8]), ALU.mult))
                freed(b, u)
                dve.wait(u)
                y = dve.op(lambda e: e.tensor_tensor(YA[:, :], YA[:, :], YB[:, :], ALU.add))
            dve.wait(y, td)
            y = dve.op(lambda e: e.tensor_tensor(YA[:, :], YA[:, :], PS[yb][:, :], ALU.add))
            freed(yb, y)
            dve.wait(y)
            y = dve.op(lambda e: e.tensor_tensor(YA[:, :], YA[:, :], Z[:, c, :], ALU.mult))
            act.wait(y)
            yield
            for g in range(2):
                q = act.op(lambda e: e.activation(YB[:, 256 * g:256 * g + 256], YA[:, 256 * g:256 * g + 256], ACT.Square,
                                                  accum_out=SS[:, 0, 2 * c + g:2 * c + g + 1]))
            sq[:] = [q]
            r = inverse_root(SS[:, 1, 2 * c:2 * c + 2], SS[:, 0, 2 * c:2 * c + 2], 256, vec("eps"), q)
            yield
            dve.wait(r, y)
            y_out[:] = [dve.op(lambda e: e.tensor_scalar(
                Z[:, c, 256 * g:256 * g + 256], YA[:, 256 * g:256 * g + 256], SS[:, 1, 2 * c + g:2 * c + g + 1], None, ALU.mult))
                for g in range(2)]
            z_out.extend(y_out)

        z_out = []
        for c in range(CH):
            bs = bank()
            for g in range(2):
                ts = mm(PS[bs][:, g * P:(g + 1) * P], XBC[:, 4 + g, c * P:(c + 1) * P], XBC[:, 6 + g, c * P:(c + 1) * P],
                        True, True, last=True)
            yield
            next(tail, None)
            sc = PS[bs][:, 0:256].rearrange("p (g t) -> p g t", g=2)
            both = []
            dve.wait(ts, *ws, *w_read)
            for d, tri, side_, M, RA, DEC, W, XC in ways:
                both.append(dve.op(lambda e: e.tensor_tensor(M[:, :, :], sc, tri.unsqueeze(1).to_broadcast([P, 2, P]), ALU.mult)))
            freed(bs, *both)
            xs_ = []
            for d, tri, side_, M, RA, DEC, W, XC in ways:
                xs_.append(dve.op(lambda e: e.tensor_tensor(
                    by_head(XC[:, :]), by_head(XST[:, c, :]), heads_by(step_[:, c, 8 * d:8 * d + 8]), ALU.mult)))
            decays = []
            for d, tri, side_, M, RA, DEC, W, XC in ways:
                pe.wait(ras[d])
                bd = []
                for g in range(2):
                    b = bank()
                    t = mm(PS[b][:, :], side_, RA[:, 4 * g:4 * g + 4, :].rearrange("p h t -> p (h t)"), True, True, last=True)
                    bd.append((b, t))
                ra_read[d] = (t,)
                yield
                next(tail, None)
                for g, (b, t) in enumerate(bd):
                    act.wait(t, *ws)
                    a = act.op(lambda e: e.activation(
                        DEC[:, 4 * g:4 * g + 4, :].rearrange("p h t -> p (h t)"), PS[b][:, :], ACT.Exp))
                    freed(b, a)
                decays.append(a)
            yield
            ws = []
            for d, tri, side_, M, RA, DEC, W, XC in ways:
                dve.wait(decays[d], *both)
                for g in range(2):
                    ws.append(dve.op(lambda e: e.tensor_tensor(
                        W[:, 4 * g:4 * g + 4, :], DEC[:, 4 * g:4 * g + 4, :],
                        M[:, g, :].unsqueeze(1).to_broadcast([P, 4, P]), ALU.mult)))
            dve.wait(*tok, *y_out)
            y = dve.op(lambda e: e.tensor_tensor(by_head(YA[:, :]), by_head(XST[:, c, :]), heads_by(cols("dsk", 0, 8)), ALU.mult))
            yield
            if c < CH - 1:
                ras = exponents(c + 1)
            offs = []
            for d in range(2):
                if (d, c) not in st:
                    continue
                S, n, s = st[d, c]
                b = bank()
                pe.wait(s)
                for g in range(2):
                    t = mm(PS[b][:, 256 * g:256 * g + 256], XBC[:, 6 + g, c * P:(c + 1) * P], S[:, n, 256 * g:256 * g + 256],
                           True, True, last=True)
                offs.append((d, b, t))
            yb = bank()
            pe.wait(*ws, *xs_)
            for h in range(8):
                o_ = PS[yb][:, 64 * h:64 * h + 64]
                mm(o_, WF[:, h, :], XCF[:, 64 * h:64 * h + 64], True, False)
                td = mm(o_, WB[:, h, :], XCB[:, 64 * h:64 * h + 64], False, True, last=True)
            w_read = [td]
            tail = gate(c, offs, y, yb, td)
            yield
        for _ in tail:
            yield
        pe.wait(*z_out)
        for i in range(4):
            b = bank()
            for c in range(CH):
                t = transpose(PS[b][:, c * P:(c + 1) * P], Z[:, c, i * P:(i + 1) * P])
            act.wait(t)
            a = act.op(lambda e: e.activation(YHI[:, 4 + i, :], PS[b][:, :], ACT.Copy, scale=cols("sn", i)))
            dve.wait(a)
            d_ = dve.op(lambda e: e.scalar_tensor_tensor(YLO[:, 4 + i, :], PS[b][:, :], cols("sn", i),
                                                         YHI[:, 4 + i, :].bitcast(F32), ALU.mult, ALU.subtract))
            freed(b, d_)
            parts[4 + i] += [a, d_]
            yield

    def biased(i):
        return vec("bin", i)

    def gated(dst, b, t, bias, tmp, free=()):
        act.wait(t, *free)
        s = act.op(lambda e: e.activation(tmp, PS[b][:, :], ACT.Sigmoid, bias=bias))
        dve.wait(s, *free)
        y = dve.op(lambda e: e.scalar_tensor_tensor(dst, PS[b][:, :], bias, tmp, ALU.add, ALU.mult))
        freed(b, y)
        return y

    def small_vectors():
        s = lambda i: SMT[:, i, :]

        def go(g, make):
            t = g.op(make)
            for o_ in (dve, act):
                o_.wait(t)

        lg, lam = vec("lb", 0, 8), vec("lam", 0, 8)
        go(dve, lambda e: e.tensor_tensor(s(0), lg, lg, ALU.subtract))
        go(act, lambda e: e.activation(s(1), s(0), ACT.Exp))
        go(dve, lambda e: e.reciprocal(s(2), s(1)))
        go(dve, lambda e: e.tensor_tensor(s(3), s(1), s(2), ALU.mult))
        go(dve, lambda e: e.tensor_tensor(LBV[:, :], s(3), s(3), ALU.subtract))
        go(dve, lambda e: e.tensor_scalar(OML[:, :], LBV[:, :], -1.0, 1.0, ALU.mult, ALU.add))
        go(dve, lambda e: e.tensor_scalar(NEGB[:, :], vec("bin", 8, 8), -1.0, None, ALU.mult))
        go(dve, lambda e: e.tensor_scalar(s(0), lam, -1.0, None, ALU.mult))
        go(dve, lambda e: e.tensor_tensor(s(1), s(0), lam, ALU.max))
        go(act, lambda e: e.activation(s(1), s(1), ACT.Exp, scale=-1.0))
        go(dve, lambda e: e.tensor_scalar(s(2), s(1), 1.0, None, ALU.add))
        go(act, lambda e: e.activation(s(3), s(2), ACT.Ln))
        go(dve, lambda e: e.tensor_scalar(s(2), s(2), -1.0, None, ALU.add))
        go(dve, lambda e: e.tensor_tensor(s(2), s(1), s(2), ALU.subtract))
        go(dve, lambda e: e.tensor_tensor(s(3), s(3), s(2), ALU.add))
        go(dve, lambda e: e.tensor_scalar(s(0), s(0), 0.0, None, ALU.max))
        go(dve, lambda e: e.tensor_tensor(s(3), s(3), s(0), ALU.add))
        go(dve, lambda e: e.tensor_scalar(C8[:, :], s(3), -8.0, None, ALU.mult))

    def recurrence(j, inputs, v_ready, parts, seen):
        f, k = inputs["f"], inputs["k"]
        LF, HK, HQ, HGS = (B[:, j % 2, :] for B in (FB, KB, QB, GB))
        last = seen[-1]
        dve.wait(f, k, *last)
        f = dve.op(lambda e: e.tensor_scalar(LF, LF, OML[:, j:j + 1], LBV[:, j:j + 1], ALU.mult, ALU.add))
        k = dve.op(lambda e: e.tensor_scalar(HK, HK, OML[:, j:j + 1], None, ALU.mult))
        dve.wait(f)
        f2 = dve.op(lambda e: e.tensor_scalar(HD[:, 0, :], LF, 1.0 / TINY, 1.0, ALU.mult, ALU.min))
        dve.wait(f2)
        f1 = dve.op(lambda e: e.tensor_scalar(LF, LF, TINY, None, ALU.max))
        yield
        act.wait(f1, f2)
        l2 = act.op(lambda e: e.activation(HD[:, 0, :], HD[:, 0, :], ACT.Ln))
        l1 = act.op(lambda e: e.activation(LF, LF, ACT.Ln))
        pool.wait(*last)
        sac = pool.op(lambda e: e.memset(SAC[:, :, :], 0.0))
        yield
        dve.wait(l1, l2)
        lf = dve.op(lambda e: e.tensor_tensor(LF, LF, HD[:, 0, :], ALU.add))
        dve.wait(lf)
        for c in range(CH):
            o = slice(c * P, (c + 1) * P)
            cb = dve.op(lambda e: e.tensor_tensor_scan(CB[:, o], ONES, LF[:, o], 0.0, ALU.mult, ALU.add))
        yield
        while "q" not in inputs:
            yield
        q = inputs["q"]
        dve.wait(cb, q)
        pool.wait(k)
        nl = len(LEVELS)
        exps, muls, prods = {}, {}, {}
        QTS = (QT[:, 0, :], QT[:, 1, :], SQ[:, 1, :]) + tuple(QTX[:, i, :] for i in (1, 0) if j < 6 + i)
        KTS = (KT[:, 0, :], KT[:, 1, :], HF[:, 1, :]) + tuple(KTX[:, i, :] for i in (1, 0) if j < 6 + i)
        lag = len(QTS)
        for i in range(nl + 2 + lag):
            if i < nl:
                h = LEVELS[i]
                blk = lambda x: x.rearrange("p (n w) -> p n w", w=2 * h)
                nb = T // (2 * h)
                cbv, hd = blk(CB[:, :]), blk(HD[:, i % 2, :])
                if i >= 2:
                    dve.wait(*muls[i - 2])
                dd = dve.op(lambda e: e.tensor_tensor(hd, cbv, cbv[:, :, h - 1:h].to_broadcast([P, nb, 2 * h]), ALU.subtract))
                act.wait(dd)
                e1 = act.op(lambda e: e.activation(hd[:, :, h:2 * h], hd[:, :, h:2 * h], ACT.Exp))
                e2 = act.op(lambda e: e.activation(hd[:, :, 0:h], hd[:, :, 0:h], ACT.Exp, scale=-1.0))
                exps[i] = (e1, e2)
            n = i - 1
            if 0 <= n < nl:
                h = LEVELS[n]
                blk = lambda x: x.rearrange("p (n w) -> p n w", w=2 * h)
                hd = blk(HD[:, n % 2, :])
                qt, kt, qv, kv = blk(QTS[n % lag]), blk(KTS[n % lag]), blk(HQ), blk(HK)
                free = prods[n - lag][1:] if n >= lag else last
                dve.wait(exps[n][0], *free)
                pool.wait(exps[n][1], *free)
                a = dve.op(lambda e: e.tensor_tensor(qt[:, :, h:2 * h], qv[:, :, h:2 * h], hd[:, :, h:2 * h], ALU.mult))
                c_ = pool.op(lambda e: e.tensor_tensor(kt[:, :, 0:h], kv[:, :, 0:h], hd[:, :, 0:h], ALU.mult))
                muls[n] = (a, c_)
            n = i - lag - 1
            if 0 <= n <= nl:
                b, t = prods[n]
                dve.wait(t, sac)
                sac = dve.op(lambda e: e.copy_predicated(
                    SAC[:, :, :], MSK[:, n, :].unsqueeze(1).to_broadcast([P, CH, P]),
                    PS[b][:, :].rearrange("p (c t) -> p c t", c=CH)))
                freed(b, sac)
            n = i - lag
            if 0 <= n <= nl:
                b = bank("side")
                if n < nl:
                    pe.wait(*muls[n])
                    lhs, rhs = KTS[n % lag], QTS[n % lag]
                else:
                    pe.wait(k, q)
                    lhs, rhs = HK, HQ
                for c in range(CH):
                    t = mm(PS[b][:, c * P:(c + 1) * P], lhs[:, c * P:(c + 1) * P], rhs[:, c * P:(c + 1) * P], True, True,
                           last=c == CH - 1)
                prods[n] = (b, t)
            yield
        act.wait(*muls[nl - 1], *muls[nl - 2], cb)
        E0 = HD[:, 0, :]
        eb = act.op(lambda e: e.activation(E0, CB[:, :], ACT.Exp))
        ends = [CB[:, c * P + P - 1:c * P + P] for c in range(CH)]
        whole = [E0[:, c * P + P - 1:c * P + P] for c in range(CH)]
        for c in range(3):
            o = slice(c * P, (c + 1) * P)
            ek = act.op(lambda e: e.activation(LF[:, o], CB[:, o], ACT.Exp, bias=ends[c], scale=-1.0))
        yield
        QX, KX = QT[:, 0, :], KT[:, 0, :]
        used = (prods[nl - 1][1], prods[nl][1])
        dve.wait(eb, ek, *used)
        pool.wait(ek, *used)
        a1 = dve.op(lambda e: e.tensor_tensor(QX[:, P:T], HQ[:, P:T], E0[:, P:T], ALU.mult))
        a2 = dve.op(lambda e: e.tensor_tensor(QX[:, 0:P], HQ[:, 3 * P:T], E0[:, 3 * P:T], ALU.mult))
        a4 = pool.op(lambda e: e.tensor_tensor(KX[:, 0:3 * P], HK[:, 0:3 * P], LF[:, 0:3 * P], ALU.mult))
        dve.wait(a1)
        a3 = dve.op(lambda e: e.tensor_scalar(QX[:, 3 * P:T], QX[:, 3 * P:T], whole[2], None, ALU.mult))
        yield
        dve.wait(a4)
        a5 = dve.op(lambda e: e.tensor_scalar(KX[:, 3 * P:T], KX[:, 0:P], whole[1], None, ALU.mult))
        yield
        yield
        pe.wait(a2, a3, a5)
        ba = bank("side")
        mm(PS[ba][:, 0:P], KX[:, 0:P], QX[:, P:2 * P], True, True)
        ta = mm(PS[ba][:, P:3 * P], KX[:, 3 * P:T], QX[:, 2 * P:T], True, True, last=True)
        bb = bank("side")
        mm(PS[bb][:, 0:2 * P], KX[:, P:2 * P], QX[:, 2 * P:T], True, True)
        tb = mm(PS[bb][:, 2 * P:3 * P], KX[:, 2 * P:3 * P], QX[:, 0:P], True, True, last=True)
        yield
        act.wait(ta, tb, *last)
        s1 = act.op(lambda e: e.copy(SOF[:, 0:384], PS[ba][:, 0:384]))
        s2 = act.op(lambda e: e.copy(SOF[:, 384:768], PS[bb][:, 0:384]))
        freed(ba, s1)
        freed(bb, s2)
        yield
        bo = bank("side")
        pe.wait(sac, s1, s2, *v_ready)
        v = [VH[:, c, j * P:(j + 1) * P] for c in range(CH)]
        o_ = PS[bo]
        kw = {"skip_group_check": True}
        mm(o_[:, P:T], v[0], SOF[:, 0:384], True, False, **kw)
        mm(o_[:, 0:P], v[0], SAC[:, 0, :], False, False, **kw)
        mm(o_[:, P:2 * P], v[1], SAC[:, 1, :], False, False, **kw)
        mm(o_[:, 2 * P:T], v[1], SOF[:, 384:640], False, False, **kw)
        mm(o_[:, 2 * P:3 * P], v[2], SAC[:, 2, :], False, False, **kw)
        mm(o_[:, 3 * P:T], v[2], SOF[:, 640:768], False, False, **kw)
        to = mm(o_[:, 3 * P:T], v[3], SAC[:, 3, :], False, True, last=True, **kw)
        yield
        act.wait(to)
        sq = act.op(lambda e: e.activation(SQ[:, 0, :], PS[bo][:, :], ACT.Square))
        yield
        bn = bank("side")
        pe.wait(sq)
        tn = mm(PS[bn][:, :], ONES, SQ[:, 0, :], True, True, last=True)
        yield
        r = inverse_root(RS[:, :], PS[bn][:, :], P, vec("eps"), tn)
        freed(bn, r)
        yield
        while "g" not in inputs:
            yield
        dve.wait(r, to, inputs["g"])
        y = dve.op(lambda e: e.scalar_tensor_tensor(HF[:, 0, :], PS[bo][:, :], vec("hgn"), RS[:, :], ALU.mult, ALU.mult))
        freed(bo, y)
        dve.wait(y)
        y = dve.op(lambda e: e.tensor_tensor(HF[:, 0, :], HF[:, 0, :], HGS, ALU.mult))
        yield
        parts[j] = split(YHI[:, j, :], YLO[:, j, :], HF[:, 0, :], (y,))
        seen.append((a5, to, sac, *parts[j]))

    def conv_taps(j, ready, done):
        acc = CVA[:, j % 2, :]
        w = lambda k: vec("cvw", 8 * k + j)
        act.wait(ready, *([done[j - 2]] if j >= 2 else []))
        y = act.op(lambda e: e.activation(acc, CU[:, j, :], ACT.Identity, bias=vec("cvb", j), scale=w(TAPS - 1)))
        yield
        for s in range(1, TAPS):
            dve.wait(y)
            y = dve.op(lambda e: e.scalar_tensor_tensor(CVA[:, j % 2, s:T], CU[:, j, 0:T - s], w(TAPS - 1 - s),
                                                        CVA[:, j % 2, s:T], ALU.mult, ALU.add))
            if s % 2 == 0:
                yield
        act.wait(y)
        done[j] = act.op(lambda e: e.copy(CU[:, j, :], acc))
        yield

    sga_free = [(), ()]
    mg = {}

    def branch_gate(x, j, b, t):
        act.wait(t, *sga_free[j % 2])
        s = act.op(lambda e: e.activation(SGA[:, j % 2, :], PS[b][:, :], ACT.Sigmoid, bias=biased(64 + 8 * x + j)))
        freed(b, s)
        return s

    def merge(j, b, t, s, sg, first):
        dve.wait(s, t)
        if first:
            y = dve.op(lambda e: e.tensor_tensor(MG[:, j, :], sg, PS[b][:, :], ALU.mult))
            freed(b, y)
        else:
            y = dve.op(lambda e: e.tensor_tensor(sg, sg, PS[b][:, :], ALU.mult))
            freed(b, y)
            dve.wait(y, *mg[j])
            y = dve.op(lambda e: e.tensor_tensor(MG[:, j, :], MG[:, j, :], sg, ALU.add))
        mg[j] = (y,)

    def lru(j, x, gw, gw_used, gelu, out_, last):
        L = LX[:, j % 2, :]
        act.wait(x, *last)
        y = act.op(lambda e: e.activation(XB[:, :], L, ACT.Identity, bias=vec("lcb", j), scale=vec("lcw", 24 + j)))
        yield
        for s in range(1, 4):
            dve.wait(x, y)
            y = dve.op(lambda e: e.scalar_tensor_tensor(XB[:, s:T], L[:, 0:T - s], vec("lcw", 8 * (3 - s) + j),
                                                        XB[:, s:T], ALU.mult, ALU.add))
        yield
        yield
        yield
        yield
        pe.wait(y, gw)
        bt = []
        for i in range(2):
            b = bank("side")
            bt.append((b, mm(PS[b][:, :], GW[:, j % 2, i * P:(i + 1) * P], XB[:, :], True, True, last=True)))
        gw_used[j % 2] = (bt[1][1],)
        yield
        g = []
        for i, dst in ((0, GR), (1, GI)):
            b, t = bt[i]
            act.wait(t)
            g.append(act.op(lambda e: e.activation(dst[:, :], PS[b][:, :], ACT.Sigmoid, bias=vec("lgb", 8 * i + j))))
            freed(b, g[-1])
        act.wait(*g)
        th = act.op(lambda e: e.activation(GT[:, :], GR[:, :], ACT.Tanh, scale=C8[:, j:j + 1]))
        yield
        dve.wait(th, *g)
        th = dve.op(lambda e: e.tensor_scalar(GT[:, :], GT[:, :], -2.0 * TINY, None, ALU.min))
        u = dve.op(lambda e: e.tensor_tensor(GI[:, :], GI[:, :], XB[:, :], ALU.mult))
        a = act.op(lambda e: e.activation(GA[:, :], GR[:, :], ACT.Exp, scale=C8[:, j:j + 1]))
        act.wait(th)
        l1 = act.op(lambda e: e.activation(GM[:, :], GT[:, :], ACT.Ln, scale=-2.0))
        l2 = act.op(lambda e: e.activation(GT[:, :], GT[:, :], ACT.Ln, bias=vec("one"), scale=-1.0))
        yield
        dve.wait(l1, l2)
        d = dve.op(lambda e: e.tensor_tensor(GM[:, :], GM[:, :], GT[:, :], ALU.subtract))
        act.wait(d)
        mu = act.op(lambda e: e.activation(GM[:, :], GM[:, :], ACT.Exp, scale=0.5))
        yield
        dve.wait(mu, u)
        u = dve.op(lambda e: e.tensor_tensor(GI[:, :], GI[:, :], GM[:, :], ALU.mult))
        dve.wait(u, a)
        h = dve.op(lambda e: e.tensor_tensor_scan(GR[:, :], GA[:, :], GI[:, :], 0.0, ALU.mult, ALU.add))
        yield
        dve.wait(h, gelu[j])
        out_[j] = dve.op(lambda e: e.tensor_tensor(YL[:, j, :], GG[:, j % 2, :], GR[:, :], ALU.mult))

    def over_channels(src, ready):
        b = bank("side")
        for j in range(DT):
            pe.wait(*ready[j])
            t = mm(PS[b][:, :], ONES, src(j), j == 0, j == DT - 1, last=True)
        return b, t

    def block2():
        ffn(at["nf1"], "ffn1_w_in_2", "ffn1_w_in_2", "ffn1_w_out_2", 0, 2816, 0.5)
        for g in (dve, act, pool, pe, sp):
            g.wait(*everything())
        m = "w_in_mix_2"
        hb = load(HB[:, :], hbias, s_hb, 32)
        kept = spill()
        small_vectors()
        dve.wait(load(MSF[:, :, :], masks, s_hb, 32))
        mask_bytes = dve.op(lambda e: e.tensor_copy(MSK[:, :, :], MSF[:, :, :]))
        act.wait(mask_bytes)
        pool.op(lambda e: e.memset(KT[:, :, :], 0.0))
        lt = [pool.op(lambda e: e.memset(QT[:, :, :], 0.0))]
        for g in (dve, pe):
            g.wait(*lt)
        pool.wait(*lt)
        ready = norm_split(at["nmix2"])
        v_ready = []
        for g_ in range(2):
            for c, (b, t) in enumerate(product_tokens(m, 0, 2048 + 512 * g_, ready)):
                dve.wait(t, hb)
                v_ready.append(dve.op(lambda e: e.tensor_tensor(
                    VH[:, c, 512 * g_:512 * g_ + 512], PS[b][:, :], HB[:, 512 * g_:512 * g_ + 512], ALU.add)))
                freed(b, v_ready[-1])
        for g in (act, dve):
            g.wait(kept, *ready[-1], *v_ready)
        act.op(lambda e: e.copy(SQ[:, 1, :], QT[:, 0, :]))
        act.op(lambda e: e.copy(QTX[:, :, :], QT[:, :, :]))
        act.op(lambda e: e.copy(KTX[:, :, :], QT[:, :, :]))
        lt = [act.op(lambda e: e.copy(HF[:, 1, :], QT[:, 0, :]))]
        for g in (dve, pool, pe):
            g.wait(*lt)
        parts, seen, cu, done = [None] * 8, [()], [], {}

        def all_taps():
            for j in range(8):
                yield from conv_taps(j, cu[j], done)

        filler.append(all_taps())
        state["pool"] = True
        for j in range(8):
            p = j % 2
            rate.update(pump=7, fill=2 if j else 0)
            while len(side_work) > 1:
                pump()
            for e_ in (act, dve):
                e_.wait(*(seen[j - 1] if j >= 2 else ()))
            bf, tf = product(m, 0, 1024 + j * P, HHI, HLO, ready)
            act.wait(tf)
            f = act.op(lambda e: e.activation(FB[:, p, :], PS[bf][:, :], ACT.Sigmoid, bias=biased(8 + j)))
            k = act.op(lambda e: e.activation(KB[:, p, :], PS[bf][:, :], ACT.Sigmoid, bias=NEGB[:, j:j + 1], scale=-1.0))
            freed(bf, k)
            got = {"f": f, "k": k}
            side_work.append(recurrence(j, got, v_ready, parts, seen))
            bq, tq = product(m, 0, j * P, HHI, HLO, ready)
            act.wait(tq)
            sq = act.op(lambda e: e.activation(QB[:, p, :], PS[bq][:, :], ACT.Sigmoid, bias=biased(j)))
            dve.wait(sq, tq)
            got["q"] = dve.op(lambda e: e.scalar_tensor_tensor(
                QB[:, p, :], PS[bq][:, :], biased(j), QB[:, p, :], ALU.add, ALU.mult))
            freed(bq, got["q"])
            bg, tg = product(m, 0, 3072 + j * P, HHI, HLO, ready)
            ba, ta = product(m, 0, 6144 + j * P, HHI, HLO, ready)
            act.wait(ta)
            c = act.op(lambda e: e.activation(CU[:, j, :], PS[ba][:, :], ACT.Identity, bias=biased(48 + j)))
            freed(ba, c)
            bb, tb = product(m, 0, 7168 + j * P, HHI, HLO, ready)
            act.wait(tg)
            sg = act.op(lambda e: e.activation(GB[:, p, :], PS[bg][:, :], ACT.Sigmoid, bias=biased(24 + j)))
            act.wait(tb, *([cu[j - 2]] if j >= 2 else []))
            s0 = act.op(lambda e: e.activation(SGA[:, p, :], PS[bb][:, :], ACT.Sigmoid, bias=biased(56 + j)))
            freed(bb, s0)
            dve.wait(sg, tg)
            got["g"] = dve.op(lambda e: e.scalar_tensor_tensor(
                GB[:, p, :], PS[bg][:, :], biased(24 + j), GB[:, p, :], ALU.add, ALU.mult))
            freed(bg, got["g"])
            dve.wait(s0, c)
            cu.append(dve.op(lambda e: e.tensor_tensor(CU[:, j, :], CU[:, j, :], SGA[:, p, :], ALU.mult)))
        finish()
        for g in (dve, act, pool):
            g.wait(*everything())
        gelu, yl, gw_used = {}, {}, [(), ()]
        rate.update(pump=4, fill=2)
        sp.wait(*everything())
        for j in range(8):
            sp.wait(*gw_used[j % 2])
            gw = load(GW[:, j % 2, :], gates[j, :, :], s_gw[j % 2], 16 * (j // 2 + 1))
            b, t = product(m, 0, 4096 + j * P, HHI, HLO, ready)
            act.wait(t)
            if j >= 2:
                act.wait(yl[j - 2])
            x = act.op(lambda e: e.activation(LX[:, j % 2, :], PS[b][:, :], ACT.Identity, bias=biased(32 + j)))
            freed(b, x)
            finish()
            side_work.append(lru(j, x, gw, gw_used, gelu, yl, [yl[j - 1]] if j else []))
            b, t = product(m, 0, 5120 + j * P, HHI, HLO, ready)
            act.wait(t)
            gelu[j] = act.op(lambda e: e.activation(GG[:, j % 2, :], PS[b][:, :], ACT.Gelu_apprx_tanh, bias=biased(40 + j)))
            freed(b, gelu[j])
            b, t = product(m, 0, 8192 + j * P, HHI, HLO, ready)
            s = branch_gate(0, j, b, t)
            b, t = product("w_branch_2", 0, j * P, YHI, YLO, parts)
            merge(j, b, t, s, SGA[:, j % 2, :], True)
            sga_free[j % 2] = mg[j]
        rate.update(fill=0)
        finish()
        while filler:
            fill()
        state["pool"] = False
        free = [pe.now()]
        parts = [split(YHI[:, j, :], YLO[:, j, :], YL[:, j, :], (yl[j],), free) for j in range(8)]
        restore(*(parts[-1]), dve.now(), act.now(), pe.now())
        cen, scaled = [], []

        def center():
            b, t = over_channels(lambda j: CU[:, j, :], [(done[j],) for j in range(8)])
            yield
            act.wait(t, dve.now(), pe.now())
            mu = act.op(lambda e: e.activation(LMU[:, :], PS[b][:, :], ACT.Copy, scale=1.0 / D))
            freed(b, mu)
            for j in range(8):
                dve.wait(mu, done[j])
                cen.append(dve.op(lambda e: e.tensor_tensor(CU[:, j, :], CU[:, j, :], LMU[:, :], ALU.subtract)))
                if j % 2:
                    yield
            bv = bank("side")
            used = []
            for j in range(8):
                act.wait(cen[j], *(used[j - 2:j - 1] if j >= 2 else []))
                sq = act.op(lambda e: e.activation(SQ[:, j % 2, :], CU[:, j, :], ACT.Square))
                yield
                pe.wait(sq)
                used.append(mm(PS[bv][:, :], ONES, SQ[:, j % 2, :], j == 0, j == 7, last=True))
            yield
            r = inverse_root(RS[:, :], PS[bv][:, :], D, vec("eps5"), used[-1])
            freed(bv, r)
            yield
            for j in range(8):
                dve.wait(r, cen[j])
                scaled.append(dve.op(lambda e: e.tensor_tensor(CU[:, j, :], CU[:, j, :], RS[:, :], ALU.mult)))
                if j % 2:
                    yield

        side_work.append(center())
        for j in range(8):
            b, t = product(m, 0, 8192 + D + j * P, HHI, HLO, ready)
            s = branch_gate(1, j, b, t)
            b, t = product("w_branch_2", 1, j * P, YHI, YLO, parts)
            merge(j, b, t, s, SGA[:, j % 2, :], False)
            sga_free[j % 2] = mg[j]
        finish()
        free = [pe.now()]
        sgs, parts = [], []
        act.wait(*mg[7], *done.values())
        for j in range(8):
            dve.wait(scaled[j])
            act.wait(scaled[j])
            y = act.op(lambda e: e.activation(CU[:, j, :], CU[:, j, :], ACT.Silu, bias=vec("cvn", j), scale=vec("cvg", j)))
            parts.append(split(YHI[:, j, :], YLO[:, j, :], CU[:, j, :], (y,), free))
        for j in range(8):
            b, t = product(m, 0, 8192 + 2 * D + j * P, HHI, HLO, ready)
            act.wait(t)
            sgs.append(act.op(lambda e: e.activation(GHT[:, j, :], PS[b][:, :], ACT.Sigmoid, bias=biased(80 + j))))
            freed(b, sgs[-1])
        for j in range(8):
            b, t = product("w_branch_2", 2, j * P, YHI, YLO, parts)
            merge(j, b, t, sgs[j], GHT[:, j, :], False)
        free = [pe.now()]
        parts = [split(YHI[:, j, :], YLO[:, j, :], MG[:, j, :], mg[j], free) for j in range(8)]
        begin_squares(*everything())
        for j in range(8):
            b, t = product("w_out_mix_2", 0, j * P, YHI, YLO, parts)
            add_to_x(j, b, t)
        for g in (dve, act, pool):
            g.wait(*everything())
        ffn(at["nf2"], "ffn2_w_in_2", "ffn2_w_in_2", "ffn2_w_out_2", 0, 2816, 0.5)

    for l in range(2):
        block1(l)
    norm_x(at["fnorm"])
    block2()
    norm_x(at["nfin"])
    assert state["next"] == len(slots)
    for j in range(DT):
        sp.wait(*x_ready[j])
        load(out[:, j * T:(j + 1) * T], X[:, j, :], s_out, 0)
    sp.wait((s_out, 16 * DT))

    with nc.Block() as block:
        def run(g):
            def body(e):
                for make in g.queue:
                    make(e)
            return body

        block.sync(run(sp))
        block.tensor(run(pe))
        block.vector(run(dve))
        block.scalar(run(act))
        block.gpsimd(run(pool))


def shape_constants():
    i = np.arange(P)
    j, t = i[:, None], i[None, :]
    consts = np.stack([j == t, np.ones((P, P), bool), j // 64 == t // 64, j <= t, j >= t, j > t, j < t], 1)
    masks = [(j // (2 * h) == t // (2 * h)) & (j % (2 * h) < h) & (t % (2 * h) >= h) for h in LEVELS] + [j == t]
    masks = np.stack(masks, 1).astype(np.float32)
    half = 16
    inv = np.float32(10000.0) ** (-(np.float32(2.0) * np.arange(half, dtype=np.float32)) / np.float32(32))
    row = (np.arange(T) // 64).astype(np.float32)
    col = (np.arange(T) % 64).astype(np.float32)
    d = i % 64
    ang = np.where((d < 32)[:, None], row[None, :] * inv[d % 16][:, None], col[None, :] * inv[d % 16][:, None])
    ang = ang.astype(np.float32)
    turned = np.zeros((P, P), np.float32)
    for m in range(P):
        if m % 32 < 16:
            turned[m + 16, m] = -1.0
        else:
            turned[m - 16, m] = 1.0
    mats = [turned]
    for src in (np.eye(P, dtype=np.float32), turned):
        for g in range(2):
            mats.append(np.concatenate([src[:, 64 * g:64 * g + 64]] * 2, 1))
    rope = np.concatenate(mats + [np.cos(ang), np.sin(ang)], 1).astype(np.float32)
    return consts.astype(np.float32), masks, rope


def kernel(**inputs):
    import concourse.bacc as _bacc
    from concourse import mybir as _mybir
    from concourse.bass_utils import run_bass_kernel_spmd as _run

    a = {k: np.asarray(v) for k, v in inputs.items()}
    pieces = []
    for name, i, r0, nr, c0, ncol in plan():
        w = a[name]
        w = w[0, i] if name == "w_branch_2" else w[i]
        w = w[r0 * P:(r0 + nr) * P, c0:c0 + ncol]
        pieces.append(w.reshape(nr, P, ncol).transpose(1, 0, 2).reshape(-1))
    stream = np.concatenate(pieces)

    at, nvec = columns()
    vecs = np.zeros((P, nvec), np.float32)

    def put(key, v):
        v = v.reshape(-1, P).T
        vecs[:, at[key]:at[key] + v.shape[1]] = v

    def rows(key, v):
        v = v.reshape(1, -1)
        vecs[:, at[key]:at[key] + v.shape[1]] = np.broadcast_to(v, (P, v.shape[1]))

    for l in range(2):
        put(("nmix", l), a["norm_mix_w"][l])
        put(("qn", l), np.concatenate([a["q_norm_w"][l]] * 2))
        put(("kn", l), np.concatenate([a["k_norm_w"][l]] * 2))
        put(("cw", l), a["conv_w"][l])
        put(("cb", l), a["conv_b"][l])
        put(("sn", l), a["ssd_norm_w"][l])
        put(("nffn", l), a["norm_ffn_w"][l])
        rows(("dtb", l), a["dt_bias"][l])
        rows(("alog", l), a["a_log"][l])
        rows(("dsk", l), a["d_skip"][l])
    for key, name in (("fnorm", "final_norm_w"), ("nf1", "norm_ffn1_2"), ("nmix2", "norm_mix_2"), ("bin", "b_in_mix_2"),
                      ("lb", "hgrn_lb_logits_2"), ("hgn", "hg_norm_2"), ("lcw", "lru_conv_w_2"), ("lcb", "lru_conv_b_2"),
                      ("lgb", "lru_gate_b_2"), ("lam", "lru_lambda_2"), ("cvw", "cv_dw_w_2"), ("cvb", "cv_dw_b_2"),
                      ("cvg", "cv_ln_g_2"), ("cvn", "cv_ln_b_2"), ("nf2", "norm_ffn2_2"), ("nfin", "norm_final_2")):
        put(key, a[name])
    for key, value in (("eps", 1e-6), ("eps5", 1e-5), ("one", 1.0)):
        vecs[:, at[key]] = value
    xin = np.ascontiguousarray(a["x"][0].T.reshape(DT, P, T).transpose(1, 0, 2))
    hbias = np.ascontiguousarray(np.broadcast_to(a["b_in_mix_2"][0, 2048:3072][None, :], (P, D)))
    gates = np.ascontiguousarray(a["lru_gate_w_2"][0].transpose(1, 2, 0, 3).reshape(8, P, 256))
    consts, masks, rope = shape_constants()

    nc = _bacc.Bacc("TRN2", target_bir_lowering=False, num_devices=1)
    arrays, args = {}, []
    for name, v in (("stream", stream), ("xin", xin), ("vecs", vecs), ("consts", consts), ("masks", masks),
                    ("rope", rope), ("hbias", hbias), ("gates", gates)):
        arrays[f"in_{name}"] = v
        args.append(nc.dram_tensor(f"in_{name}", v.shape, _mybir.dt.from_np(v.dtype), kind="ExternalInput").ap())
    out = nc.dram_tensor("out_0", (P, DT * T), _mybir.dt.float32, kind="ExternalOutput").ap()
    xkeep = nc.dram_tensor("xkeep", (P, DT * T), _mybir.dt.float32, kind="Internal").ap()
    build(nc, xkeep, *args, out)
    r = _run(nc, [arrays], core_ids=[0])
    got = r.results[0]["out_0"].reshape(P, DT, T).transpose(1, 0, 2).reshape(D, T).T
    return np.ascontiguousarray(got).reshape(1, T, D)
```
